# Optimizing a Trainium2 kernel written in Bass

```python
import jax, jax.numpy as jnp
from jax import lax
import numpy as np

D_MODEL = 1024
BATCH = 1
SEQ = 1024
DEPTH = 1
DEC_BATCH = 8
DEC_SEQ = 16
PAST_LEN = 512

CHUNK = 64
LEFT_CHUNKS = 8
ATT_WINDOW = LEFT_CHUNKS * CHUNK
BAND = (LEFT_CHUNKS + 1) * CHUNK
N_HEADS = 8
HEAD_DIM = 64
D_ATT = N_HEADS * HEAD_DIM
MAX_REL = 128
D_CONV = D_MODEL // 2
CONV_W = 3
N_GROUPS = 4
EXPERTS_PER_GROUP = 8
N_EXPERTS = N_GROUPS * EXPERTS_PER_GROUP
TOP_K = 2
D_EXPERT = 512
MOE_BLOCK = 128
EPS = 1e-6
IN_SIZES = [D_ATT, D_ATT, D_ATT, D_CONV, D_CONV, D_CONV, D_MODEL, D_MODEL]
IN_COLS = sum(IN_SIZES)
IN_SPLITS = [int(i) for i in np.cumsum(IN_SIZES)[:-1]]

kernel_name = 'chunk_stream_hybrid_step'

def rmsnorm(x, g):
    x32 = x.astype(jnp.float32)
    y = x32 * lax.rsqrt(jnp.mean(x32 * x32, axis=-1, keepdims=True) + EPS)
    return (y * g.astype(jnp.float32)).astype(x.dtype)

def ada_mod(c, w_ada, b_ada):
    m = jax.nn.silu(c) @ w_ada + b_ada
    return jnp.split(m[:, None, :], 6, axis=-1)

def band_attention(q, k, v, q_pos, k_pos, k_valid, rel_bias):
    s = jnp.einsum('nqhd,nkhd->nhqk', q, k).astype(jnp.float32) * (HEAD_DIM ** -0.5)
    rel = jnp.clip(q_pos[:, None] - k_pos[None, :], -MAX_REL, MAX_REL) + MAX_REL
    s = s + rel_bias[:, rel].astype(jnp.float32)[None]
    s = jnp.where(k_valid[None, None, None, :], s, -1e30)
    p = jax.nn.softmax(s, axis=-1)
    return jnp.einsum('nhqk,nkhd->nqhd', p.astype(v.dtype), v)

def prompt_attention(q, k, v, rel_bias):
    n, L = q.shape[:2]
    nc = L // CHUNK
    pad = ((0, 0), (ATT_WINDOW, 0), (0, 0), (0, 0))
    k_pad = jnp.pad(k, pad)
    v_pad = jnp.pad(v, pad)
    q_ch = q.reshape(n, nc, CHUNK, N_HEADS, HEAD_DIM).swapaxes(0, 1)

    def one_chunk(args):
        q_c, i = args
        start = i * CHUNK
        k_b = lax.dynamic_slice_in_dim(k_pad, start, BAND, axis=1)
        v_b = lax.dynamic_slice_in_dim(v_pad, start, BAND, axis=1)
        q_pos = start + jnp.arange(CHUNK, dtype=jnp.int32)
        k_pos = start - ATT_WINDOW + jnp.arange(BAND, dtype=jnp.int32)
        return band_attention(q_c, k_b, v_b, q_pos, k_pos, k_pos >= 0, rel_bias)

    o = lax.map(one_chunk, (q_ch, jnp.arange(nc, dtype=jnp.int32)))
    return o.swapaxes(0, 1).reshape(n, L, D_ATT)

def sample_attention(q, k_new, v_new, k_cache, v_cache, rel_bias):
    n, L = q.shape[:2]
    n_old = k_cache.shape[1]
    k = jnp.concatenate([k_cache.astype(k_new.dtype), k_new], axis=1)
    v = jnp.concatenate([v_cache.astype(v_new.dtype), v_new], axis=1)
    q_pos = PAST_LEN + jnp.arange(L, dtype=jnp.int32)
    k_pos = jnp.concatenate([PAST_LEN - n_old + jnp.arange(n_old, dtype=jnp.int32), q_pos])
    o = band_attention(q, k, v, q_pos, k_pos, k_pos >= 0, rel_bias)
    return o.reshape(n, L, D_ATT)

def short_conv(cb, cc, cv, prev, conv_w, conv_b):
    u = cc * cv
    u_pad = jnp.concatenate([prev.astype(u.dtype), u], axis=1)
    L = u.shape[1]
    y = sum(conv_w[j] * u_pad[:, j:j + L] for j in range(CONV_W)) + conv_b
    return cb * y, u_pad[:, -(CONV_W - 1):]

def route(h, w_group, b_group, w_expert, b_expert):
    lg = (h @ w_group + b_group).astype(jnp.float32)
    pg = jax.nn.softmax(lg, axis=-1)
    g = jnp.argmax(lg, axis=-1).astype(jnp.int32)
    le = (h @ w_expert + b_expert).astype(jnp.float32).reshape(-1, N_GROUPS, EXPERTS_PER_GROUP)
    le_g = jnp.take_along_axis(le, g[:, None, None], axis=1)[:, 0]
    top_p, top_i = lax.top_k(jax.nn.softmax(le_g, axis=-1), TOP_K)
    top_p = top_p / jnp.sum(top_p, axis=-1, keepdims=True)
    weights = jnp.take_along_axis(pg, g[:, None], axis=1) * top_p
    experts = g[:, None] * EXPERTS_PER_GROUP + top_i.astype(jnp.int32)
    return experts, weights

def moe_ffn(h, experts, weights, w_gate, w_up, w_down):
    T, D = h.shape
    A = T * TOP_K
    flat_e = experts.reshape(-1)
    flat_t = jnp.repeat(jnp.arange(T, dtype=jnp.int32), TOP_K)
    order = jnp.argsort(flat_e)
    se = flat_e[order]
    st = flat_t[order]
    counts = jnp.bincount(flat_e, length=N_EXPERTS).astype(jnp.int32)
    pcounts = (counts + MOE_BLOCK - 1) // MOE_BLOCK * MOE_BLOCK
    starts = jnp.cumsum(counts) - counts
    pends = jnp.cumsum(pcounts)
    pstarts = pends - pcounts
    dest = pstarts[se] + jnp.arange(A, dtype=jnp.int32) - starts[se]
    n_blocks = -(-A // MOE_BLOCK) + N_EXPERTS
    P = n_blocks * MOE_BLOCK
    slot_tok = jnp.full((P,), T, jnp.int32).at[dest].set(st)
    h_pad = jnp.concatenate([h, jnp.zeros((1, D), h.dtype)], axis=0)
    xb = h_pad[slot_tok].reshape(n_blocks, MOE_BLOCK, D)
    blk_e = jnp.minimum(jnp.searchsorted(pends, jnp.arange(n_blocks, dtype=jnp.int32) * MOE_BLOCK, side='right'), N_EXPERTS - 1)

    def expert_block(args):
        xblk, e = args
        return (jax.nn.silu(xblk @ w_gate[e]) * (xblk @ w_up[e])) @ w_down[e]

    yb = lax.map(expert_block, (xb, blk_e)).reshape(P, D)
    y_assign = yb[dest][jnp.argsort(order)].reshape(T, TOP_K, D)
    return jnp.einsum('tkd,tk->td', y_assign, weights.astype(h.dtype))

def trunk_layer(x, c, kv_cache, conv_prev, w_ada, b_ada, norm1_g, norm2_g, w_in, rel_bias, conv_w, conv_b,
                w_pa, w_pb, w_o, w_group, b_group, w_expert, b_expert, w_e_gate, w_e_up, w_e_down):
    n, L = x.shape[:2]
    sh1, sc1, gt1, sh2, sc2, gt2 = ada_mod(c, w_ada, b_ada)
    h = rmsnorm(x, norm1_g) * (1 + sc1) + sh1
    q, k, v, cb, cc, cv, ga, gb = jnp.split(h @ w_in, IN_SPLITS, axis=-1)
    q = q.reshape(n, L, N_HEADS, HEAD_DIM)
    k = k.reshape(n, L, N_HEADS, HEAD_DIM)
    v = v.reshape(n, L, N_HEADS, HEAD_DIM)
    if kv_cache is None:
        att = prompt_attention(q, k, v, rel_bias)
        keep = min(ATT_WINDOW, L)
        new_k, new_v = k[:, L - keep:], v[:, L - keep:]
        conv_prev = jnp.zeros((n, CONV_W - 1, D_CONV), x.dtype)
    else:
        att = sample_attention(q, k, v, kv_cache[0], kv_cache[1], rel_bias)
        new_k, new_v = k, v
    conv_out, new_conv = short_conv(cb, cc, cv, conv_prev, conv_w, conv_b)
    mix = (jax.nn.sigmoid(ga) * (att @ w_pa) + jax.nn.sigmoid(gb) * (conv_out @ w_pb)) @ w_o
    x = x + gt1 * mix
    h2 = (rmsnorm(x, norm2_g) * (1 + sc2) + sh2).reshape(n * L, D_MODEL)
    experts, weights = route(h2, w_group, b_group, w_expert, b_expert)
    ffn = moe_ffn(h2, experts, weights, w_e_gate, w_e_up, w_e_down).reshape(n, L, D_MODEL)
    x = x + gt2 * ffn
    return x, new_k, new_v, new_conv

def setup_inputs(seed: int = 0) -> dict:
    key = jax.random.key(seed)
    ks = jax.random.split(key, 27)
    nrm = lambda k, shape, s: jax.random.normal(k, shape, jnp.float32) * s
    kv_rows = min(ATT_WINDOW, PAST_LEN)
    return {
        'x_prompt': nrm(ks[0], (BATCH, SEQ, D_MODEL), 1.0),
        'x_sample': nrm(ks[1], (DEC_BATCH, DEC_SEQ, D_MODEL), 1.0),
        'cache_attn_k': nrm(ks[2], (DEPTH, DEC_BATCH, kv_rows, N_HEADS, HEAD_DIM), 1.0),
        'cache_attn_v': nrm(ks[3], (DEPTH, DEC_BATCH, kv_rows, N_HEADS, HEAD_DIM), 1.0),
        'state_conv': nrm(ks[4], (DEPTH, DEC_BATCH, CONV_W - 1, D_CONV), 1.0),
        'c_prompt': nrm(ks[5], (BATCH, D_MODEL), 1.0),
        'c_sample': nrm(ks[6], (DEC_BATCH, D_MODEL), 1.0),
        'w_ada': nrm(ks[7], (DEPTH, D_MODEL, 6 * D_MODEL), 0.5 * D_MODEL ** -0.5),
        'b_ada': nrm(ks[8], (DEPTH, 6 * D_MODEL), 0.02),
        'norm1_g': 1.0 + nrm(ks[9], (DEPTH, D_MODEL), 0.02),
        'norm2_g': 1.0 + nrm(ks[10], (DEPTH, D_MODEL), 0.02),
        'w_in': nrm(ks[11], (DEPTH, D_MODEL, IN_COLS), D_MODEL ** -0.5),
        'rel_bias': nrm(ks[12], (DEPTH, N_HEADS, 2 * MAX_REL + 1), 0.5),
        'conv_w': nrm(ks[13], (DEPTH, CONV_W, D_CONV), CONV_W ** -0.5),
        'conv_b': nrm(ks[14], (DEPTH, D_CONV), 0.02),
        'w_pa': nrm(ks[15], (DEPTH, D_ATT, D_MODEL), D_ATT ** -0.5),
        'w_pb': nrm(ks[16], (DEPTH, D_CONV, D_MODEL), D_CONV ** -0.5),
        'w_o': nrm(ks[17], (DEPTH, D_MODEL, D_MODEL), D_MODEL ** -0.5),
        'w_group': nrm(ks[18], (DEPTH, D_MODEL, N_GROUPS), D_MODEL ** -0.5),
        'b_group': nrm(ks[19], (DEPTH, N_GROUPS), 0.01),
        'w_expert': nrm(ks[20], (DEPTH, D_MODEL, N_EXPERTS), D_MODEL ** -0.5),
        'b_expert': nrm(ks[21], (DEPTH, N_EXPERTS), 0.01),
        'w_e_gate': nrm(ks[22], (DEPTH, N_EXPERTS, D_MODEL, D_EXPERT), D_MODEL ** -0.5),
        'w_e_up': nrm(ks[23], (DEPTH, N_EXPERTS, D_MODEL, D_EXPERT), D_MODEL ** -0.5),
        'w_e_down': nrm(ks[24], (DEPTH, N_EXPERTS, D_EXPERT, D_MODEL), D_EXPERT ** -0.5),
        'final_g': 1.0 + nrm(ks[25], (D_MODEL,), 0.02),
    }

def reference(x_prompt, x_sample, cache_attn_k, cache_attn_v, state_conv, c_prompt, c_sample,
              w_ada, b_ada, norm1_g, norm2_g, w_in, rel_bias, conv_w, conv_b, w_pa, w_pb, w_o,
              w_group, b_group, w_expert, b_expert, w_e_gate, w_e_up, w_e_down, final_g):
    xp, xs = x_prompt, x_sample
    kp_l, vp_l, cp_l, ks_l, vs_l, cs_l = [], [], [], [], [], []
    for l in range(DEPTH):
        lw = (w_ada[l], b_ada[l], norm1_g[l], norm2_g[l], w_in[l], rel_bias[l], conv_w[l], conv_b[l],
              w_pa[l], w_pb[l], w_o[l], w_group[l], b_group[l], w_expert[l], b_expert[l],
              w_e_gate[l], w_e_up[l], w_e_down[l])
        xp, kp, vp, cp = trunk_layer(xp, c_prompt, None, None, *lw)
        xs, ks_, vs_, cs_ = trunk_layer(xs, c_sample, (cache_attn_k[l], cache_attn_v[l]), state_conv[l], *lw)
        kp_l.append(kp); vp_l.append(vp); cp_l.append(cp)
        ks_l.append(ks_); vs_l.append(vs_); cs_l.append(cs_)
    y_prompt = rmsnorm(xp, final_g)
    y_sample = rmsnorm(xs, final_g)
    return (y_prompt, y_sample, jnp.stack(kp_l), jnp.stack(vp_l), jnp.stack(cp_l),
            jnp.stack(ks_l), jnp.stack(vs_l), jnp.stack(cs_l))


_drawn_inputs = setup_inputs


def setup_inputs(seed=0):
    import zlib

    import numpy as np

    out = dict(_drawn_inputs(seed))
    spreads = {}
    factors = {'cache_attn_k': 4.921,
     'cache_attn_v': 3.829,
     'norm2_g': 5.11,
     'rel_bias': 5.226,
     'conv_b': 8.0,
     'b_group': 8.0,
     'b_expert': 8.0,
     'final_g': 2.786}
    for name, (base, spread) in spreads.items():
        noise = np.random.default_rng([zlib.crc32(name.encode()), seed]).standard_normal(out[name].shape)
        drawn = base * np.exp(spread * noise) if base else spread * noise
        out[name] = __import__('jax').numpy.asarray(drawn.astype(out[name].dtype))
    for name, factor in factors.items():
        out[name] = (out[name] * factor).astype(out[name].dtype)
    return out
```

```python
from contextlib import ExitStack

import concourse.bass as bass
from concourse import mybir

ALU = mybir.AluOpType
ACT = mybir.ActivationFunctionType
AX = mybir.AxisListType
F32 = mybir.dt.float32
I32 = mybir.dt.int32

P = 128
D = 1024
KT = D // P
NP_TOK, SEQS, DEC = 1024, 8, 16
NS_TOK = SEQS * DEC
T = NP_TOK + NS_TOK
NPT = NP_TOK // P
NT = T // P
H, HD = 8, 64
HP = H // 2
DA = H * HD
CW = 3
PAST = 512
MAXREL = 128
NREL = 2 * MAXREL + 1
BAND = 5 * P
NEG = -1e30
EPS = 1e-6
G, EPG = 4, 8
E = G * EPG
DE = 512
NLOG = G + E
CAP = P
OVF = (2 * T) // CAP - 1
NBLK = E + OVF
SEQROW = SEQS
TOKCH = [(0, 512), (512, 512), (1024, 128)]


class Link:

    def __init__(self, eng, sem):
        self.eng, self.sem, self.n = eng, sem, 0

    def __call__(self, ins):
        self.n += 1
        ins.then_inc(self.sem, 1)
        self.eng.wait_ge(self.sem, self.n)


def wait(eng, sem, value):
    if isinstance(value, int) and value <= 0:
        return
    eng.wait_ge(sem, value)


def build(nc, x_prompt, x_sample, cache_attn_k, cache_attn_v, state_conv, c_prompt, c_sample,
          w_ada, b_ada, norm1_g, norm2_g, w_in, rel_bias, conv_w, conv_b, w_pa, w_pb, w_o,
          w_group, b_group, w_expert, b_expert, w_e_gate, w_e_up, w_e_down, final_g,
          y_prompt, y_sample, new_k_prompt, new_v_prompt, new_conv_prompt,
          new_k_sample, new_v_sample, new_conv_sample):
    with ExitStack() as ctx:
        base = (nc.sbuf_base + 63) // 64 * 64
        KB = 1024
        CONST, RING, ARENA = 0, 8 * KB + 512, 72 * KB + 512

        def at(name, shape, offset, dt=F32):
            return nc.alloc_sbuf_tensor_at(name, shape, dt, offset=base + int(offset))

        def sem(name):
            return ctx.enter_context(nc.semaphore(name))

        def psum(name, shape):
            return ctx.enter_context(nc.psum_tensor(name, shape, F32))

        def dram(name, shape, dt=F32):
            return nc.dram_tensor(name, shape, dt).ap()

        mod_d = dram("mod_d", (SEQS + 1, 6 * D))
        relrow_d = dram("relrow_d", (H, P, P - 1 + BAND))
        h2_d = dram("h2_d", (T, D))
        table_d = dram("table_d", (P * NBLK, 1), I32)
        y_d = dram("y_d", (P * NBLK, D))

        cur = [CONST]

        def small(name, shape, dt=F32):
            n = 1
            for s in shape[1:]:
                n *= s
            n = (n * 4 + 31) // 32 * 32
            t = at(name, shape, cur[0], dt)
            cur[0] += n
            assert cur[0] <= RING, cur[0]
            return t

        ident = small("ident", [P, P])
        before = small("before", [P, P])
        ones = small("ones", [P, P])
        eps = small("eps", [P, 1])
        tokid = small("tokid", [P, NT], I32)
        sumsq = small("sumsq", [P, 4, NT])
        rowmax = small("rowmax", [P, 72])
        negmax = small("negmax", [P, 72])
        rowsum = small("rowsum", [P, 72])
        rinv = small("rinv", [P, 72])
        convw = small("convw", [P, CW + 1, HP])
        wr = small("wr", [P, KT, NLOG])
        br = small("br", [P, NLOG])
        logits = small("logits", [P, NT, NLOG])
        table = small("table", [P, NBLK], I32)
        dest = small("dest", [P, 2, NT], I32)
        wts = small("wts", [P, 2, NT])
        eids = small("eids", [P, OVF + 1], I32)
        idx = small("idx", [P, 2], I32)
        lastu = small("lastu", [P, HP, 18])

        SLOT = 16 * KB
        ring = [at(f"ring{s}", [P, KT, 512], RING + s * SLOT) for s in range(4)]
        mring = [at(f"mring{s}", [P, KT * 512], RING + s * SLOT) for s in range(6)]

        def A(kb):
            return ARENA + kb * KB

        hT = at("hT", [P, KT, T], A(0))
        qT = at("qT", [P, HP, T], A(36))
        kT = at("kT", [P, HP, NP_TOK], A(54))
        v = at("v", [P, NT, DA], A(72))
        kTs = at("kTs", [P, HP, NS_TOK], A(126))
        qTs = at("qTs", [P, HP, NS_TOK], A(128))
        kk = at("kk", [P, 2, DA], A(130))
        zrow = at("zrow", [P, 256], A(134))
        c_sb = at("c_sb", [SEQS + 1, D], A(36))
        sc_sb = at("sc_sb", [SEQS + 1, D], A(40))
        cT = at("cT", [P, KT, SEQS + 1], A(44))
        modc = at("modc", [SEQS + 1, 2, 512], A(46))
        bada = at("bada", [SEQS + 1, 6 * D], A(50))
        xt = at("xt", [P, 2, D], A(90))
        ht = at("ht", [P, 2, D], A(98))
        scale1 = at("scale1", [P, 2, D], A(106))
        shift1 = at("shift1", [P, 2, D], A(114))
        g1 = at("g1", [P, D], A(122))
        relin = at("relin", [H, NREL], A(76))
        relrow = at("relrow", [H, P - 1 + BAND], A(78))
        bias = at("bias", [P, H, BAND], A(90))
        S = at("S", [P, 2, BAND], A(110))
        Pr = at("Pr", [P, 2, BAND], A(115))
        PT = at("PT", [P, 2, 5, P], A(120))
        attt = at("attt", [P, 2, P], A(125))
        kc = at("kc", [P, 2, 4, DA], A(54))
        vc = at("vc", [P, 2, 4, DA], A(70))
        kcT = at("kcT", [P, HP, PAST], A(90))
        NK = PAST + DEC
        Ss = at("Ss", [P, NK], A(98))
        Ps = at("Ps", [P, NK], A(100.5))
        Pn = at("Pn", [P, NK], A(103))
        PTs = at("PTs", [P, 5, P], A(105.5))
        sbias = at("sbias", [P, NK], A(108))
        qblk = at("qblk", [P, 2, 640], A(110.5))
        v16 = at("v16", [DEC, 2, DA], A(115.5))
        U = at("U", [P, HP, NP_TOK + 2], A(72))
        Us = at("Us", [P, HP, SEQS, DEC + 2], A(88.5))
        Y = at("Y", [P, HP, T], A(54))
        st_in = at("st_in", [SEQS * 2, DA], A(91))
        newc = at("newc", [18, DA], A(93))
        mixT = at("mixT", [P, KT, T], A(91))
        sgA = at("sgA", [P, 2, 512], A(128))
        tA = at("tA", [P, 512], A(132))
        tB = at("tB", [P, 512], A(88.5))
        sgB = at("sgB", [P, 2, 512], A(84))
        x1 = at("x1", [P, NT, D], A(36))
        gate1 = at("gate1", [P, 2, D], A(0))
        scale2 = at("scale2", [P, 2, D], A(8))
        shift2 = at("shift2", [P, 2, D], A(16))
        xr = at("xr", [P, 2, D], A(24))
        g2 = at("g2", [P, D], A(32))
        h2 = at("h2", [P, 2, D], A(72))
        h2T = at("h2T", [P, D], A(80))
        sq = at("sq", [P, D], A(84))
        R = 104

        def rt(i, shape, dt=F32):
            return at(f"route{i}", shape, A(R) + i * 1184, dt)

        lg = rt(0, [P, NT, G])
        gmask = rt(1, [P, NT, G])
        le = rt(2, [P, NT, E])
        o1 = rt(3, [P, NT, E])
        o2 = rt(4, [P, NT, E])
        picked = rt(5, [P, NT, E])
        rank = rt(6, [P, NT, E])
        tot = rt(7, [P, NT, E])
        tmp = rt(8, [P, NT, E])
        chunk = rt(9, [P, NT, E])
        slot = rt(10, [P, NT, E])
        tieb = rt(11, [P, 64])
        eidx = rt(12, [P, E])
        cnt = rt(13, [P, E])
        ovc = rt(14, [P, E])
        ovi = rt(15, [P, E])
        ove = rt(16, [P, E])
        sm = rt(17, [P, 8, NT])
        ocmp = rt(18, [P, OVF, E])
        ocmp2 = rt(21, [P, OVF + 1])
        oidx = rt(22, [P, OVF])
        zero_i = rt(23, [P, NBLK], I32)
        xg = at("xg", [P, 2, D], A(72))
        xT = at("xT", [P, 2, D], A(80))
        sg = at("sg", [P, DE], A(88))
        hh = at("hh", [P, DE], A(90))
        hhT = at("hhT", [P, DE], A(92))
        yy = at("yy", [P, 2, D], A(94))
        gate2 = at("gate2", [P, 2, D], RING)
        fg = at("fg", [P, D], RING + 8 * KB)
        ya = at("ya", [P, 2, D], RING + 12 * KB)
        yb = at("yb", [P, 2, D], RING + 20 * KB)
        yo = at("yo", [P, 2, D], RING + 28 * KB)
        yq = at("yq", [P, D], RING + 36 * KB)

        ps = psum("ps", [P, 8, 512])

        def bank(b, n=1):
            return ps[:, b:b + n, :].rearrange("p b c -> p (b c)")

        names = """consts conv_in c_in badain c_silu cT_ps cT_sb unit_used mod_sb mod_out rel_in rel_sb rel_out
            mods1 modA x_in0 x_in1 n1_sq n1_rt n1_h n1_tr n1_evac
            gemm gev_qk gev_kout gev_v gev_prev gev_conv kk_out v_out bias_in bias_ok
            s_scores s_sb s_p s_pt s_ptc s_pv s_at s_att s_attc
            kv_in0 kv_in1 sb_in k_tr k_trc qb ks_sc ks_sb ks_p ks_pn ks_pt ks_ptc ks_pv ks_at v16_in0 v16_in1
            prev_in conv_last conv_tr conv_out newc_sb cu_done
            g_ready g_sig g_done wr_in
            mods2 modB xr_in0 xr_in1 o_done x1_done n2_sq n2_rt n2_h n2_tr n2_evac n2_log n2_lev h2_out0 h2_out1
            picks ranks route_done zeroed zero_out scat table_in routed gathers zrow_ok y_zeroed
            xg_in0 xg_in1 idxc xg_tr xT_ok gate_mm up_mm silu_ok h_ok h_tr hT_ok down_mm y_ok y_out0 y_out1
            o_w o_idx o_xg o_tr o_xT o_g o_u o_s o_h o_ht o_hT o_dn o_y o_out
            mods3 ya_in0 ya_in1 f_sq f_rt f_out0 f_out1 f_done
            link_dve link_act link_pool""".split()
        s = {n: sem(n) for n in names}
        landed = [sem(f"landed{i}") for i in range(4)]
        mlanded = [sem(f"mlanded{i}") for i in range(6)]

        w_in2 = w_in[0].rearrange("(k p) n -> p k n", p=P)
        w_ada2 = w_ada[0].rearrange("(k p) n -> p k n", p=P)
        w_pa2 = w_pa[0].rearrange("(k p) n -> p k n", p=P)
        w_pb2 = w_pb[0].rearrange("(k p) n -> p k n", p=P)
        w_o2 = w_o[0].rearrange("(k p) n -> p k n", p=P)

        def cols(w, c):
            return [w[:, 0:4, c * 512:(c + 1) * 512], w[:, 4:8, c * 512:(c + 1) * 512]]

        NADA = 6 * D // 512
        units = [cols(w_ada2, c) for c in range(NADA)]
        UQ, UK, UV, UCC, UCV, UCB = [NADA + i for i in range(6)]
        for c in (0, 1, 2, 4, 5, 3):
            units.append(cols(w_in2, c))
        UGATE = len(units)
        for h in range(2):
            units.append(cols(w_in2, 6 + h))
            units.append(cols(w_in2, 8 + h))
            units.append([w_pa2[:, :, h * 512:(h + 1) * 512], w_pb2[:, :, h * 512:(h + 1) * 512]])
        UO = len(units)
        for h in range(2):
            units.append(cols(w_o2, h))
        NU = len(units)

        def unit_landed(eng, u):
            eng.wait_ge(landed[u % 4], 32 * (u // 4 + 1))

        block = ctx.enter_context(nc.Block())

        @block.sync
        def _(sp):
            for u, halves in enumerate(units):
                wait(sp, s["unit_used"], u - 3)
                for i, src in enumerate(halves):
                    sp.dma_start(ring[u % 4][:, 4 * i:4 * i + 4, :], src).then_inc(landed[u % 4], 16)

            gate_d = w_e_gate[0].rearrange("e (k p) n -> p e k n", p=P)
            up_d = w_e_up[0].rearrange("e (k p) n -> p e k n", p=P)
            down_d = w_e_down[0].rearrange("e (k p) n -> p e k n", p=P)

            def gu_slot(slot_no):
                return mring[slot_no][:].rearrange("p (k n) -> p k n", k=KT)

            def load_expert(e, first):
                r = e % 2 if isinstance(e, int) else first
                ex = e
                for j, (w, used, c) in enumerate(((gate_d, "gate_mm", -1), (up_d, "up_mm", -1),
                                                  (down_d, "down_mm", -1))):
                    wait(sp, s[used], ex + c)
                    q = 3 * r + j
                    k = KT if j < 2 else 4
                    dst = mring[q][:].rearrange("p (k n) -> p k n", k=k)
                    src = w[:, ex] if isinstance(ex, int) else w[:, bass.ds(ex, 1)].rearrange(
                        "p e k n -> p (e k) n")
                    sp.dma_start(dst, src).then_inc(mlanded[q], 16)

            sp.wait_ge(s["unit_used"], NU)
            for q in range(4):
                sp.wait_ge(landed[q], 32 * ((NU - 1 - q) // 4 + 1))
            sp.wait_ge(s["n2_h"], NT)
            load_expert(0, 0)
            load_expert(1, 1)
            with sp.Fori(1, E // 2) as i:
                load_expert(i * 2, 0)
                load_expert(i * 2 + 1, 1)

            sp.wait_ge(s["routed"], 1)
            sp.wait_ge(s["down_mm"], E)
            n_ov = sp.value_load(eids[0:1, OVF:OVF + 1], min_val=0, max_val=OVF)
            with sp.Fori(0, OVF) as o:
                with sp.If(o < n_ov):
                    ex = sp.value_load(eids[0:1, bass.ds(o, 1)], min_val=0, max_val=E - 1)
                    sp.wait_ge(s["o_dn"], o + 1)
                    for j, w in enumerate((gate_d, up_d, down_d)):
                        k = KT if j < 2 else 4
                        sp.dma_start(mring[j][:].rearrange("p (k n) -> p k n", k=k),
                                     w[:, bass.ds(ex, 1)].rearrange("p e k n -> p (e k) n")
                                     ).then_inc(s["o_w"], 16)

            for t in range(NT):
                sp.wait_ge(s["f_done"], t + 1)
                dst = y_prompt[0, t * P:(t + 1) * P, :] if t < NPT else y_sample.rearrange("s t d -> (s t) d")
                sp.dma_start(dst, yo[:, t % 2, :]).then_inc(s[f"f_out{t % 2}"], 16)
            sp.wait_ge(s["f_out0"], 16 * 5)
            sp.wait_ge(s["f_out1"], 16 * 4)
            sp.wait_ge(s["conv_out"], 32)
            sp.wait_ge(s["kk_out"], 16 * 5)
            sp.wait_ge(s["v_out"], 16 * 2)

        @block.gpsimd
        def _(pool):
            link = Link(pool, s["link_pool"])

            def row_all(src):
                return src.partition_broadcast(P)

            def load_mod(dst, part, signal):
                pool.dma_start(dst[:, 0, :], bass.AP(mod_d.tensor, SEQROW * 6 * D + part * D, [[0, P], [1, D]])
                               ).then_inc(signal, 16)
                for q in range(SEQS):
                    pool.dma_start(dst[q * DEC:(q + 1) * DEC, 1, :],
                                   bass.AP(mod_d.tensor, q * 6 * D + part * D, [[0, DEC], [1, D]])
                                   ).then_inc(signal, 16)

            def vec_all(dst, vec, n, signal):
                pool.dma_start(dst, bass.AP(vec.tensor, vec.offset, [[0, P], [1, n]])).then_inc(signal, 16)

            pool.dma_start(c_sb[0:SEQS, :], c_sample).then_inc(s["c_in"], 16)
            pool.dma_start(c_sb[SEQS:SEQS + 1, :], c_prompt).then_inc(s["c_in"], 16)
            pool.dma_start(bada[:, :], bass.AP(b_ada.tensor, b_ada.offset, [[0, SEQS + 1], [1, 6 * D]])
                           ).then_inc(s["badain"], 16)
            link(nc.gpsimd.memset(ident[:], 0.0))
            link(nc.gpsimd.affine_select(out=ident[:], in_=ident[:], compare_op=ALU.not_equal, fill=1.0,
                                         base=0, pattern=[[-1, P]], channel_multiplier=1))
            link(nc.gpsimd.memset(before[:], 1.0))
            link(nc.gpsimd.affine_select(out=before[:], in_=before[:], compare_op=ALU.is_gt, fill=0.0,
                                         base=0, pattern=[[1, P]], channel_multiplier=-1))
            link(nc.gpsimd.memset(ones[:], 1.0))
            link(nc.gpsimd.memset(eps[:], EPS))
            nc.gpsimd.iota(tokid[:], [[P, NT]], base=0, channel_multiplier=1).then_inc(s["consts"], 1)

            pool.dma_start(relin[:], rel_bias[0]).then_inc(s["rel_in"], 16)
            with nc.allow_non_contiguous_dma("conv taps, channel-major"):
                for j in range(CW):
                    pool.dma_start(convw[:, j, :], conv_w[0, j].rearrange("(m p) -> p m", p=P)
                                   ).then_inc(s["conv_in"], 16)
                pool.dma_start(convw[:, CW, :], conv_b[0].rearrange("(m p) -> p m", p=P)
                               ).then_inc(s["conv_in"], 16)
                pool.dma_start(wr[:, :, 0:G], w_group[0].rearrange("(k p) g -> p k g", p=P)
                               ).then_inc(s["wr_in"], 16)
                pool.dma_start(wr[:, :, G:NLOG], w_expert[0].rearrange("(k p) g -> p k g", p=P)
                               ).then_inc(s["wr_in"], 16)
            vec_all(br[:, 0:G], b_group, G, s["wr_in"])
            vec_all(br[:, G:NLOG], b_expert, E, s["wr_in"])

            vec_all(g1[:], norm1_g, D, s["mods1"])
            for t in range(2):
                pool.dma_start(xt[:, t, :], x_prompt[0, t * P:(t + 1) * P, :]).then_inc(s[f"x_in{t}"], 16)
            pool.wait_ge(s["mod_out"], 16 * 4)
            load_mod(shift1, 0, s["mods1"])
            load_mod(scale1, 1, s["mods1"])
            for t in range(2, NT):
                pool.wait_ge(s["n1_h"], t - 1)
                src = x_prompt[0, t * P:(t + 1) * P, :] if t < NPT else x_sample.rearrange("s t d -> (s t) d")
                pool.dma_start(xt[:, t % 2, :], src).then_inc(s[f"x_in{t % 2}"], 16)

            pool.wait_ge(s["rel_sb"], 2)
            pool.dma_start(relrow_d, relrow[:].unsqueeze(1).to_broadcast([H, P, P - 1 + BAND])
                           ).then_inc(s["rel_out"], 16)
            pool.wait_ge(s["rel_out"], 16)
            pool.wait_ge(s["n1_h"], NT)
            pool.wait_ge(s["n1_tr"], NT)
            RW = P - 1 + BAND
            for h in range(H):
                pool.dma_start(bias[:, h, :], bass.AP(relrow_d.tensor, h * P * RW + P - 1, [[RW - 1, P], [1, BAND]])
                               ).then_inc(s["bias_in"], 16)

            nc.gpsimd.memset(zrow[:], 0.0).then_inc(s["zrow_ok"], 1)
            pool.wait_ge(s["zrow_ok"], 1)
            y_rows = y_d.rearrange("(p b) (j c) -> p b j c", b=NBLK, c=256)
            with pool.Fori(E, NBLK) as b:
                for j in range(D // 256):
                    pool.dma_start(y_rows[:, bass.ds(b, 1), j, :].rearrange("p b c -> p (b c)"), zrow[:]
                                   ).then_inc(s["y_zeroed"], 16)

            for i in range(5):
                pool.wait_ge(s["gev_kout"], i + 1)
                dst = (new_k_prompt[0, 0, i * P:(i + 1) * P].rearrange("t h d -> t (h d)") if i < 4
                       else new_k_sample[0].rearrange("s t h d -> (s t) (h d)"))
                pool.dma_start(dst, kk[:, i % 2, :]).then_inc(s["kk_out"], 16)
                pool.wait_ge(s["kk_out"], 16 * (i + 1))
            pool.wait_ge(s["gev_v"], NT)
            pool.dma_start(new_v_prompt[0, 0].rearrange("(i p) h d -> p i (h d)", p=P), v[:, NPT - 4:NPT, :]
                           ).then_inc(s["v_out"], 16)
            pool.dma_start(new_v_sample[0].rearrange("s t h d -> (s t) (h d)"), v[:, NPT, :]
                           ).then_inc(s["v_out"], 16)

            pool.wait_ge(s["v_out"], 32)
            pool.wait_ge(s["s_attc"], HP * NPT)
            pool.wait_ge(s["s_ptc"], H * NPT)
            for h in range(H):
                pool.dma_start(sbias[h * DEC:(h + 1) * DEC, :],
                               bass.AP(relrow_d.tensor, h * P * RW + P - 1, [[RW - 1, DEC], [1, NK]])
                               ).then_inc(s["sb_in"], 16)
            for q in range(SEQS):
                r = q % 2
                wait(pool, s["ks_pv"], q - 1)
                pool.dma_start(kc[:, r], cache_attn_k[0, q].rearrange("(c p) h d -> p c (h d)", p=P)
                               ).then_inc(s[f"kv_in{r}"], 16)
                pool.dma_start(vc[:, r], cache_attn_v[0, q].rearrange("(c p) h d -> p c (h d)", p=P)
                               ).then_inc(s[f"kv_in{r}"], 16)
                pool.dma_start(v16[:, r, :], v[q * DEC:(q + 1) * DEC, NPT, :]).then_inc(s[f"v16_in{r}"], 16)

            pool.wait_ge(s["ks_at"], SEQS)
            pool.dma_start(st_in[:], state_conv[0].rearrange("s j c -> (s j) c")).then_inc(s["prev_in"], 16)
            pool.wait_ge(s["newc_sb"], 1)
            pool.dma_start(new_conv_sample[0].rearrange("s j c -> (s j) c"), newc[0:16, :]
                           ).then_inc(s["conv_out"], 16)
            pool.dma_start(new_conv_prompt[0, 0], newc[16:18, :]).then_inc(s["conv_out"], 16)

            pool.wait_ge(s["g_ready"], 4 * 24)
            vec_all(g2[:], norm2_g, D, s["mods2"])
            pool.wait_ge(s["mod_out"], 16 * NADA)
            load_mod(gate1, 2, s["mods2"])
            load_mod(shift2, 3, s["mods2"])
            load_mod(scale2, 4, s["mods2"])
            for t in range(NT):
                wait(pool, s["x1_done"], t - 1)
                src = x_prompt[0, t * P:(t + 1) * P, :] if t < NPT else x_sample.rearrange("s t d -> (s t) d")
                pool.dma_start(xr[:, t % 2, :], src).then_inc(s[f"xr_in{t % 2}"], 16)
                if t >= 1:
                    pool.wait_ge(s["n2_h"], t)
                    pool.dma_start(h2_d[(t - 1) * P:t * P, :], h2[:, (t - 1) % 2, :]
                                   ).then_inc(s[f"h2_out{(t - 1) % 2}"], 16)
            pool.wait_ge(s["n2_h"], NT)
            pool.dma_start(h2_d[(NT - 1) * P:, :], h2[:, (NT - 1) % 2, :]).then_inc(s["h2_out0"], 16)

            pool.wait_ge(s["o_done"], NT)
            link(nc.gpsimd.iota(tieb[:], [[-1, 64]], base=64, channel_multiplier=0,
                                allow_small_or_imprecise_dtypes=True))
            link(nc.gpsimd.iota(eidx[:], [[1, E]], base=0, channel_multiplier=0,
                                allow_small_or_imprecise_dtypes=True))
            link(nc.gpsimd.iota(oidx[:], [[1, OVF]], base=0, channel_multiplier=0,
                                allow_small_or_imprecise_dtypes=True))
            nc.gpsimd.memset(zero_i[:], 0).then_inc(s["zeroed"], 1)
            pool.wait_ge(s["zeroed"], 1)
            pool.dma_start(table_d.rearrange("(p b) o -> p (b o)", b=NBLK), zero_i[:]).then_inc(s["zero_out"], 16)
            pool.wait_ge(s["zero_out"], 16)

            pool.wait_ge(s["route_done"], 1)
            for k in range(2):
                for t in range(NT):
                    pool.indirect_dma_start(
                        out=table_d, out_offset=bass.IndirectOffsetOnAxis(ap=dest[:, k, t:t + 1], axis=0),
                        in_=tokid[:, t:t + 1], in_offset=None).then_inc(s["scat"], 16)
            pool.wait_ge(s["scat"], 16 * 2 * NT)
            pool.dma_start(table[:], table_d.rearrange("(p b) o -> p (b o)", b=NBLK)).then_inc(s["table_in"], 16)
            pool.wait_ge(s["table_in"], 16)
            pool.wait_ge(s["h2_out0"], 16 * 5)
            pool.wait_ge(s["h2_out1"], 16 * 4)

            def gather(e, r):
                wait(pool, s["xg_tr"], e - 1)
                col = table[:, e:e + 1] if isinstance(e, int) else table[:, bass.ds(e, 1)]
                nc.gpsimd.tensor_copy(idx[:, r:r + 1], col).then_inc(s["idxc"], 1)
                pool.wait_ge(s["idxc"], e + 1)
                pool.sem_inc(s["gathers"], 1)
                pool.indirect_dma_start(out=xg[:, r, :], out_offset=None, in_=h2_d,
                                        in_offset=bass.IndirectOffsetOnAxis(ap=idx[:, r:r + 1], axis=0)
                                        ).then_inc(s[f"xg_in{r}"], 16)

            gather(0, 0)
            gather(1, 1)
            with pool.Fori(1, E // 2) as i:
                gather(i * 2, 0)
                gather(i * 2 + 1, 1)
            pool.wait_ge(s["routed"], 1)
            pool.wait_ge(s["y_zeroed"], 16 * OVF * (D // 256))
            n_ov = pool.value_load(eids[0:1, OVF:OVF + 1], min_val=0, max_val=OVF)
            pool.wait_ge(s["xg_tr"], E)
            with pool.Fori(0, OVF) as o:
                with pool.If(o < n_ov):
                    nc.gpsimd.tensor_copy(idx[:, 0:1], table[:, bass.ds(o + E, 1)]).then_inc(s["o_idx"], 1)
                    pool.wait_ge(s["o_idx"], o + 1)
                    pool.sem_inc(s["gathers"], 1)
                    pool.indirect_dma_start(out=xg[:, 0, :], out_offset=None, in_=h2_d,
                                            in_offset=bass.IndirectOffsetOnAxis(ap=idx[:, 0:1], axis=0)
                                            ).then_inc(s["o_xg"], 16)
                    pool.wait_ge(s["o_out"], (o + 1) * 16)

            pool.wait_ge(s["down_mm"], E)
            for r in range(2):
                pool.wait_ge(s[f"y_out{r}"], 16 * (E // 2))
            vec_all(fg[:], final_g, D, s["mods3"])
            load_mod(gate2, 5, s["mods3"])
            for t in range(NT):
                r = t % 2
                wait(pool, s["f_done"], t - 1)
                for k, buf in enumerate((ya, yb)):
                    pool.indirect_dma_start(out=buf[:, r, :], out_offset=None, in_=y_d,
                                            in_offset=bass.IndirectOffsetOnAxis(ap=dest[:, k, t:t + 1], axis=0)
                                            ).then_inc(s[f"ya_in{r}"], 16)

        @block.scalar
        def _(act):
            act.wait_ge(s["c_in"], 32)
            nc.scalar.activation(sc_sb[:], c_sb[:], ACT.Silu).then_inc(s["c_silu"], 1)
            for u in range(NADA):
                act.wait_ge(s["mod_sb"], u + 1)
                act.dma_start(mod_d[:, u * 512:(u + 1) * 512], modc[:, u % 2, :]).then_inc(s["mod_out"], 16)
                act.wait_ge(s["mod_out"], 16 * (u + 1))
            act.wait_ge(s["consts"], 1)

            def square_root(t):
                r = t % 2
                act.wait_ge(s[f"x_in{r}"], 16 * (t // 2 + 1))
                wait(act, s["n1_tr"], t - 1)
                nc.scalar.activation(ht[:, r, :], xt[:, r, :], ACT.Square, accum_out=sumsq[:, 0, t:t + 1]
                                     ).then_inc(s["n1_sq"], 1)
                act.wait_ge(s["n1_sq"], t + 1)
                nc.scalar.activation(sumsq[:, 1, t:t + 1], sumsq[:, 0, t:t + 1], ACT.Sqrt, scale=1.0 / D,
                                     bias=eps[:, 0:1]).then_inc(s["n1_rt"], 1)

            square_root(0)
            for t in range(NT):
                if t + 1 < NT:
                    square_root(t + 1)
                act.wait_ge(s["n1_tr"], t + 1)
                b = 2 * (t % 2)
                nc.scalar.copy(hT[:, :, t * P:(t + 1) * P], bank(b, 2).rearrange("p (k c) -> p k c", k=KT)
                               ).then_inc(s["n1_evac"], 1)

            g = 0
            for what in range(2):
                for m in range(HP):
                    for c0, cn in TOKCH:
                        act.wait_ge(s["gemm"], g + 1)
                        src = ps[:, 4 + g % 4, 0:cn]
                        if what == 0:
                            dst = qT[:, m, c0:c0 + cn] if c0 < NP_TOK else qTs[:, m, :]
                            nc.scalar.mul(dst, src, HD ** -0.5).then_inc(s["gev_qk"], 1)
                        else:
                            dst = kT[:, m, c0:c0 + cn] if c0 < NP_TOK else kTs[:, m, :]
                            nc.scalar.copy(dst, src).then_inc(s["gev_qk"], 1)
                        g += 1
            for i in range(5):
                act.wait_ge(s["gemm"], g + 1)
                if i >= 2:
                    act.wait_ge(s["kk_out"], 16 * (i - 1))
                nc.scalar.copy(kk[:, i % 2, :], ps[:, 4 + g % 4, :]).then_inc(s["gev_kout"], 1)
                g += 1
            act.wait_ge(s["rel_out"], 16)
            for t in range(NT):
                act.wait_ge(s["gemm"], g + 1)
                nc.scalar.copy(v[:, t, :], ps[:, 4 + g % 4, :]).then_inc(s["gev_v"], 1)
                g += 1

            NA = H * NPT

            def exp_rows(a):
                act.wait_ge(s["s_sb"], a + 1)
                wait(act, s["s_pt"], a - 1)
                c0 = P * (4 - min(a // 2 % NPT, 4))
                nc.scalar.activation(Pr[:, a % 2, c0:BAND], S[:, a % 2, c0:BAND], ACT.Exp,
                                     bias=negmax[:, a:a + 1], accum_out=rowsum[:, a:a + 1]
                                     ).then_inc(s["s_p"], 1)

            def prob_cols(a):
                act.wait_ge(s["s_pt"], a + 1)
                wait(act, s["s_pv"], a - 1)
                j0 = 4 - min(a // 2 % NPT, 4)
                nc.scalar.copy(PT[:, a % 2, j0:5, :],
                               bank(4, 2)[:, j0 * P:BAND].rearrange("p (j c) -> p j c", c=P)
                               ).then_inc(s["s_ptc"], 1)

            exp_rows(0)
            for a in range(NA):
                if a + 1 < NA:
                    exp_rows(a + 1)
                prob_cols(a)

            for q in range(SEQS):
                act.wait_ge(s["k_tr"], q + 1)
                wait(act, s["ks_sc"], q)
                nc.scalar.copy(kcT[:], bank(0, 4).rearrange("p (m c) -> p m c", m=HP)).then_inc(s["k_trc"], 1)
                act.wait_ge(s["ks_sb"], q + 1)
                wait(act, s["ks_pn"], q)
                nc.scalar.activation(Ps[:], Ss[:], ACT.Exp, bias=negmax[:, 64 + q:65 + q],
                                     accum_out=rowsum[:, 64 + q:65 + q]).then_inc(s["ks_p"], 1)
                act.wait_ge(s["ks_pt"], q + 1)
                wait(act, s["ks_pv"], q)
                nc.scalar.copy(PTs[:, 0:4, :], ps[:, 6, :].rearrange("p (j c) -> p j c", c=P)
                               ).then_inc(s["ks_ptc"], 1)
                nc.scalar.copy(PTs[0:DEC, 4, :], ps[0:DEC, 7, 0:P]).then_inc(s["ks_ptc"], 1)

            g0 = g
            for m in range(HP):
                for c0, cn in TOKCH:
                    act.wait_ge(s["gemm"], g + 1)
                    src = ps[:, 4 + g % 4, 0:cn]
                    dst = (U[:, m, 2 + c0:2 + c0 + cn] if c0 < NP_TOK else Us[:, m, :, 2:])
                    if c0 >= NP_TOK:
                        src = src.rearrange("p (q t) -> p q t", t=DEC)
                    nc.scalar.copy(dst, src).then_inc(s["gev_conv"], 1)
                    g += 1

            for i in range(24):
                cn = TOKCH[i % 3][1]
                for k, sb_ in ((0, sgA), (2, sgB)):
                    act.wait_ge(s["g_ready"], 4 * i + k + 1)
                    wait(act, s["g_done"], i - 1)
                    nc.scalar.activation(sb_[:, i % 2, 0:cn], ps[:, 4 * (i % 2) + k, 0:cn], ACT.Sigmoid
                                         ).then_inc(s["g_sig"], 1)

            for t in range(NT):
                act.wait_ge(s["x1_done"], t + 1)
                nc.scalar.activation(sq[:], x1[:, t, :], ACT.Square, accum_out=sumsq[:, 0, t:t + 1]
                                     ).then_inc(s["n2_sq"], 1)
                act.wait_ge(s["n2_sq"], t + 1)
                nc.scalar.activation(sumsq[:, 1, t:t + 1], sumsq[:, 0, t:t + 1], ACT.Sqrt, scale=1.0 / D,
                                     bias=eps[:, 0:1]).then_inc(s["n2_rt"], 1)
                act.wait_ge(s["n2_tr"], t + 1)
                wait(act, s["n2_log"], t)
                nc.scalar.copy(h2T[:], bank(4, 2)).then_inc(s["n2_evac"], 1)

            act.wait_ge(s["picks"], 1)
            nc.scalar.activation(gmask[:], lg[:], ACT.Exp).then_inc(s["picks"], 1)
            act.wait_ge(s["picks"], 3)
            nc.scalar.activation(sm[:, 3, :], sm[:, 2, :], ACT.Exp).then_inc(s["picks"], 1)

            def rows_cols(e, r):
                act.wait_ge(s["xg_tr"], e + 1)
                wait(act, s["up_mm"], e - 1)
                nc.scalar.copy(xT[:, r, :], bank(0, 2)).then_inc(s["xT_ok"], 1)

            def silu(e):
                act.wait_ge(s["gate_mm"], e + 1)
                wait(act, s["h_ok"], e)
                nc.scalar.activation(sg[:], bank(2), ACT.Silu).then_inc(s["silu_ok"], 1)

            def store(e, r):
                act.wait_ge(s["y_ok"], e + 1)
                dst = y_d.rearrange("(p b) d -> p b d", b=NBLK)
                dst = dst[:, e, :] if isinstance(e, int) else dst[:, bass.ds(e, 1), :].rearrange("p b d -> p (b d)")
                act.dma_start(dst, yy[:, r, :]).then_inc(s[f"y_out{r}"], 16)

            rows_cols(0, 0)
            silu(0)
            rows_cols(1, 1)
            silu(1)
            rows_cols(2, 0)
            store(0, 0)
            with act.Fori(1, E // 2 - 1) as i:
                silu(i * 2)
                rows_cols(i * 2 + 1, 1)
                store(i * 2 - 1, 1)
                silu(i * 2 + 1)
                rows_cols(i * 2 + 2, 0)
                store(i * 2, 0)
            silu(E - 2)
            rows_cols(E - 1, 1)
            store(E - 3, 1)
            silu(E - 1)
            store(E - 2, 0)
            store(E - 1, 1)
            act.wait_ge(s["routed"], 1)
            act.wait_ge(s["y_zeroed"], 16 * OVF * (D // 256))
            n_ov = act.value_load(eids[0:1, OVF:OVF + 1], min_val=0, max_val=OVF)
            with act.Fori(0, OVF) as o:
                with act.If(o < n_ov):
                    act.wait_ge(s["o_tr"], o + 1)
                    nc.scalar.copy(xT[:, 0, :], bank(0, 2)).then_inc(s["o_xT"], 1)
                    act.wait_ge(s["o_g"], o + 1)
                    nc.scalar.activation(sg[:], bank(2), ACT.Silu).then_inc(s["o_s"], 1)
                    act.wait_ge(s["o_y"], o + 1)
                    dst = y_d.rearrange("(p b) d -> p b d", b=NBLK)[:, bass.ds(o + E, 1), :]
                    act.dma_start(dst.rearrange("p b d -> p (b d)"), yy[:, 0, :]).then_inc(s["o_out"], 16)

            for t in range(NT):
                act.wait_ge(s["f_sq"], 2 * t + 1)
                nc.scalar.activation(yq[:], x1[:, t, :], ACT.Square, accum_out=sumsq[:, 2, t:t + 1]
                                     ).then_inc(s["f_sq"], 1)
                act.wait_ge(s["f_sq"], 2 * t + 2)
                nc.scalar.activation(sumsq[:, 3, t:t + 1], sumsq[:, 2, t:t + 1], ACT.Sqrt, scale=1.0 / D,
                                     bias=eps[:, 0:1]).then_inc(s["f_rt"], 1)

        @block.vector
        def _(dve):
            link = Link(dve, s["link_dve"])
            V = nc.vector

            dve.wait_ge(s["cT_ps"], 1)
            V.tensor_copy(cT[:], ps[:, 6, 0:KT * (SEQS + 1)].rearrange("p (k s) -> p k s", k=KT)
                          ).then_inc(s["cT_sb"], 1)

            dve.wait_ge(s["badain"], 16)
            for u in range(NADA):
                dve.wait_ge(s["unit_used"], u + 1)
                if u >= 2:
                    dve.wait_ge(s["mod_out"], 16 * (u - 1))
                V.tensor_tensor(modc[:, u % 2, :], ps[0:SEQS + 1, 4 + u % 2, :], bada[:, u * 512:(u + 1) * 512],
                                ALU.add).then_inc(s["mod_sb"], 1)
                if u == 3:
                    dve.wait_ge(s["rel_in"], 16)
                    link(V.memset(relrow[:, 0:4 * P], 0.0))
                    V.tensor_scalar(relrow[:, 0:4 * P], relrow[:, 0:4 * P], relin[:, NREL - 1:NREL], None,
                                    ALU.add).then_inc(s["rel_sb"], 1)
                    n = P - 1 + BAND - 4 * P
                    V.tensor_copy(relrow[:, 4 * P:], bass.AP(relin, n, [[NREL, H], [-1, n]])).then_inc(s["rel_sb"], 1)

            dve.wait_ge(s["mods1"], 16 * (1 + 2 * 9))
            for r in range(2):
                link(V.scalar_tensor_tensor(out=scale1[:, r, :], in0=scale1[:, r, :], scalar=1.0, in1=g1[:],
                                            op0=ALU.add, op1=ALU.mult))
            for t in range(NT):
                r, side = t % 2, int(t == NPT)
                dve.wait_ge(s["n1_rt"], t + 1)
                link(V.reciprocal(sumsq[:, 1, t:t + 1], sumsq[:, 1, t:t + 1]))
                link(V.scalar_tensor_tensor(out=ht[:, r, :], in0=xt[:, r, :], scalar=sumsq[:, 1, t:t + 1],
                                            in1=scale1[:, side, :], op0=ALU.mult, op1=ALU.mult))
                V.tensor_tensor(ht[:, r, :], ht[:, r, :], shift1[:, side, :], ALU.add).then_inc(s["n1_h"], 1)

            dve.wait_ge(s["bias_in"], 16 * H)
            V.memset(bias[0:HD, :, BAND - 64:BAND], NEG).then_inc(s["bias_ok"], 1)
            V.memset(bias[HD:P, :, 0:64], NEG).then_inc(s["bias_ok"], 1)
            dve.wait_ge(s["bias_ok"], 2)
            NA = H * NPT

            def masked(a):
                i, h = a // 2 % NPT, 2 * (a // 2 // NPT) + a % 2
                c0 = P * (4 - min(i, 4))
                dve.wait_ge(s["s_scores"], a + 1)
                wait(dve, s["s_p"], a - 1)
                link(V.tensor_tensor_reduce(out=S[:, a % 2, c0:BAND], in0=bank(2 * (a % 2), 2)[:, c0:BAND],
                                            in1=bias[:, h, c0:BAND], scale=1.0, scalar=-3e38,
                                            op0=ALU.add, op1=ALU.max, accum_out=rowmax[:, a:a + 1]))
                V.tensor_scalar(negmax[:, a:a + 1], rowmax[:, a:a + 1], -1.0, None, ALU.mult
                                ).then_inc(s["s_sb"], 1)

            def normed(pair):
                a = 2 * pair
                dve.wait_ge(s["s_pv"], a + 2)
                wait(dve, s["s_att"], pair - 1)
                link(V.reciprocal(rinv[:, a:a + 2], rowsum[:, a:a + 2]))
                V.tensor_tensor(attt[:, pair % 2, :].rearrange("p (h d) -> p h d", h=2),
                                ps[:, 6, 0:P].rearrange("p (h d) -> p h d", h=2),
                                rinv[:, a:a + 2].unsqueeze(2).to_broadcast([P, 2, HD]), ALU.mult
                                ).then_inc(s["s_at"], 1)

            def att_cols(pair):
                i, hp = pair % NPT, pair // NPT
                dve.wait_ge(s["s_att"], pair + 1)
                V.tensor_copy(qT[:, hp, i * P:(i + 1) * P], ps[:, 7, 0:P]).then_inc(s["s_attc"], 1)

            masked(0)
            masked(1)
            for a in range(NA):
                if a + 2 < NA:
                    masked(a + 2)
                if a % 2 == 0 and a >= 2:
                    normed(a // 2 - 1)
                if a % 2 == 1 and a >= 3:
                    att_cols(a // 2 - 1)
            normed(NA // 2 - 1)
            att_cols(NA // 2 - 1)

            link(V.memset(qblk[:, :, :], 0.0))
            dve.wait_ge(s["sb_in"], 16 * H)
            for q in range(SEQS):
                r = q % 2
                wait(dve, s["ks_sc"], q - 1)
                qv = qblk[:, r, :].rearrange("p (a b) -> p a b", b=160)
                V.tensor_copy(qv[0:HD, 0:HP, 0:DEC], qTs[0:HD, :, q * DEC:(q + 1) * DEC]).then_inc(s["qb"], 1)
                V.tensor_copy(qv[HD:P, 0:HP, DEC:2 * DEC], qTs[HD:P, :, q * DEC:(q + 1) * DEC]
                              ).then_inc(s["qb"], 1)
                dve.wait_ge(s["ks_sc"], q + 1)
                wait(dve, s["ks_p"], q)
                link(V.tensor_tensor_reduce(out=Ss[:], in0=bank(4, 2)[:, 0:NK], in1=sbias[:], scale=1.0,
                                            scalar=-3e38, op0=ALU.add, op1=ALU.max,
                                            accum_out=rowmax[:, 64 + q:65 + q]))
                V.tensor_scalar(negmax[:, 64 + q:65 + q], rowmax[:, 64 + q:65 + q], -1.0, None, ALU.mult
                                ).then_inc(s["ks_sb"], 1)
                dve.wait_ge(s["ks_p"], q + 1)
                wait(dve, s["ks_pt"], q)
                link(V.reciprocal(rinv[:, 64 + q:65 + q], rowsum[:, 64 + q:65 + q]))
                V.tensor_scalar(Pn[:], Ps[:], rinv[:, 64 + q:65 + q], None, ALU.mult).then_inc(s["ks_pn"], 1)
                dve.wait_ge(s["ks_pv"], q + 1)
                pv = ps[:, 5, P:2 * P].rearrange("p (m c) -> p m c", m=HP)
                cols_ = slice(NP_TOK + q * DEC, NP_TOK + (q + 1) * DEC)
                link(V.tensor_copy(qT[0:HD, :, cols_], pv[0:HD, :, 0:DEC]))
                V.tensor_copy(qT[HD:P, :, cols_], pv[HD:P, :, DEC:2 * DEC]).then_inc(s["ks_at"], 1)

            g = 12 + 12 + 5 + NT
            link(V.memset(U[:, :, 0:2], 0.0))
            g += 12
            for m in range(HP):
                for n, (c0, cn) in enumerate(TOKCH):
                    dve.wait_ge(s["gemm"], g + 1)
                    dve.wait_ge(s["gev_conv"], g - 12 - 38 + 1)
                    src = ps[:, 4 + g % 4, 0:cn]
                    dst = (U[:, m, 2 + c0:2 + c0 + cn] if c0 < NP_TOK else Us[:, m, :, 2:])
                    if c0 >= NP_TOK:
                        src = src.rearrange("p (q t) -> p q t", t=DEC)
                    V.tensor_tensor(dst, dst, src, ALU.mult).then_inc(s["cu_done"], 1)
                    g += 1
            dve.wait_ge(s["cu_done"], 12)
            dve.wait_ge(s["gemm"], g + 1)
            V.tensor_copy(Us[:, :, :, 0:2],
                          ps[:, 4 + g % 4, 0:HP * 16].rearrange("p (m q j) -> p m q j", m=HP, j=2)
                          ).then_inc(s["gev_prev"], 1)
            g += 1
            link(V.tensor_copy(lastu[:, :, 0:16].rearrange("p m (q j) -> p m q j", j=2), Us[:, :, :, DEC:]))
            V.tensor_copy(lastu[:, :, 16:18], U[:, :, NP_TOK:]).then_inc(s["conv_last"], 1)
            dve.wait_ge(s["gev_prev"], 1)
            dve.wait_ge(s["conv_in"], 16 * (CW + 1))
            for m in range(HP):
                yp, us = Y[:, m, 0:NP_TOK], Y[:, m, NP_TOK:].rearrange("p (q t) -> p q t", t=DEC)
                w = [convw[:, j, m:m + 1] for j in range(CW + 1)]
                link(V.tensor_scalar(yp, U[:, m, 0:NP_TOK], w[0], w[CW], ALU.mult, ALU.add))
                link(V.tensor_scalar(us, Us[:, m, :, 0:DEC], w[0], w[CW], ALU.mult, ALU.add))
                for j in (1, 2):
                    link(V.scalar_tensor_tensor(out=yp, in0=U[:, m, j:j + NP_TOK], scalar=w[j], in1=yp,
                                                op0=ALU.mult, op1=ALU.add))
                    link(V.scalar_tensor_tensor(out=us, in0=Us[:, m, :, j:j + DEC], scalar=w[j], in1=us,
                                                op0=ALU.mult, op1=ALU.add))
            dve.wait_ge(s["gemm"], g + 1)
            V.tensor_copy(newc[:], ps[0:18, 4 + g % 4, :]).then_inc(s["newc_sb"], 1)
            g += 1
            for m in range(HP):
                for c0, cn in TOKCH:
                    dve.wait_ge(s["gemm"], g + 1)
                    V.tensor_tensor(Y[:, m, c0:c0 + cn], Y[:, m, c0:c0 + cn], ps[:, 4 + g % 4, 0:cn], ALU.mult
                                    ).then_inc(s["cu_done"], 1)
                    g += 1

            dve.wait_ge(s["conv_out"], 32)
            for i in range(24):
                f, (c0, cn) = i // 3, TOKCH[i % 3]
                b = 4 * (i % 2)
                wait(dve, s["g_done"], i)
                dve.wait_ge(s["g_ready"], 4 * i + 2)
                dve.wait_ge(s["g_sig"], 2 * i + 1)
                link(V.tensor_tensor(tA[:, 0:cn], sgA[:, i % 2, 0:cn], ps[:, b + 1, 0:cn], ALU.mult))
                dve.wait_ge(s["g_ready"], 4 * i + 4)
                dve.wait_ge(s["g_sig"], 2 * i + 2)
                link(V.tensor_tensor(tB[:, 0:cn], sgB[:, i % 2, 0:cn], ps[:, b + 3, 0:cn], ALU.mult))
                V.tensor_tensor(mixT[:, f, c0:c0 + cn], tA[:, 0:cn], tB[:, 0:cn], ALU.add
                                ).then_inc(s["g_done"], 1)

            dve.wait_ge(s["mods2"], 16 * (1 + 3 * 9))
            for r in range(2):
                link(V.scalar_tensor_tensor(out=scale2[:, r, :], in0=scale2[:, r, :], scalar=1.0, in1=g2[:],
                                            op0=ALU.add, op1=ALU.mult))

            def residual(t):
                r, side = t % 2, int(t == NPT)
                dve.wait_ge(s["o_done"], t + 1)
                link(V.tensor_tensor(x1[:, t, :], bank(2 * r, 2), gate1[:, side, :], ALU.mult))
                dve.wait_ge(s[f"xr_in{r}"], 16 * (t // 2 + 1))
                V.tensor_tensor(x1[:, t, :], x1[:, t, :], xr[:, r, :], ALU.add).then_inc(s["x1_done"], 1)

            def log_bias(t):
                dve.wait_ge(s["n2_log"], t + 1)
                V.tensor_tensor(logits[:, t, :], ps[:, 6, 0:NLOG], br[:], ALU.add).then_inc(s["n2_lev"], 1)

            dve.wait_ge(s["wr_in"], 64)
            residual(0)
            for t in range(NT):
                r, side = t % 2, int(t == NPT)
                dve.wait_ge(s["n2_rt"], t + 1)
                dve.wait_ge(s["x1_done"], t + 1)
                link(V.reciprocal(sumsq[:, 1, t:t + 1], sumsq[:, 1, t:t + 1]))
                if t >= 2:
                    dve.wait_ge(s[f"h2_out{r}"], 16 * (t // 2))
                    dve.wait_ge(s["n2_tr"], t - 1)
                link(V.scalar_tensor_tensor(out=h2[:, r, :], in0=x1[:, t, :], scalar=sumsq[:, 1, t:t + 1],
                                            in1=scale2[:, side, :], op0=ALU.mult, op1=ALU.mult))
                V.tensor_tensor(h2[:, r, :], h2[:, r, :], shift2[:, side, :], ALU.add).then_inc(s["n2_h"], 1)
                if t + 1 < NT:
                    residual(t + 1)
                log_bias(t)
            dve.wait_ge(s["n2_lev"], NT)

            dve.wait_ge(s["zeroed"], 1)

            def b3(x2, n):
                return x2.unsqueeze(2).to_broadcast([P, NT, n])

            def c3(row, n):
                return row.unsqueeze(1).to_broadcast([P, NT, n])

            def first_max(out, src, mx, n, buf, m2):
                link(V.tensor_reduce(mx, src, AX.X, ALU.max))
                link(V.tensor_tensor(buf, src, b3(mx, n), ALU.is_equal))
                link(V.tensor_tensor(buf, buf, c3(tieb[:, 0:n], n), ALU.mult))
                link(V.tensor_reduce(m2, buf, AX.X, ALU.max))
                link(V.tensor_tensor(out, buf, b3(m2, n), ALU.is_equal))

            lgr, ler = logits[:, :, 0:G], logits[:, :, G:NLOG]
            gm, sc0 = sm[:, 0, :], sm[:, 1, :]
            pick_g = gmask
            first_max(pick_g[:], lgr, gm, G, lg[:], sc0)
            le4 = le[:].rearrange("p t (g e) -> p t g e", g=G)
            link(V.tensor_scalar(tmp[:, :, 0:G], pick_g[:], -NEG, NEG, ALU.mult, ALU.add))
            for gi in range(G):
                sl = slice(gi * EPG, (gi + 1) * EPG)
                link(V.tensor_tensor(le[:, :, sl], ler[:, :, sl],
                                     pick_g[:, :, gi:gi + 1].to_broadcast([P, NT, EPG]), ALU.mult))
                link(V.tensor_tensor(le[:, :, sl], le[:, :, sl],
                                     tmp[:, :, gi:gi + 1].to_broadcast([P, NT, EPG]), ALU.add))
            V.tensor_tensor(lg[:], lgr, b3(gm, G), ALU.subtract).then_inc(s["picks"], 1)
            m1, m2_ = sm[:, 4, :], sm[:, 5, :]
            first_max(o1[:], le[:], m1, E, tmp[:], sc0)
            link(V.tensor_scalar(tmp[:], o1[:], 4 * NEG, None, ALU.mult))
            link(V.tensor_tensor(le[:], le[:], tmp[:], ALU.add))
            first_max(o2[:], le[:], m2_, E, tmp[:], sc0)
            dve.wait_ge(s["picks"], 2)
            V.tensor_tensor(sm[:, 2, :], m2_, m1, ALU.subtract).then_inc(s["picks"], 1)
            link(V.tensor_reduce(sm[:, 6, :], gmask[:], AX.X, ALU.add))
            V.tensor_tensor(picked[:], o1[:], o2[:], ALU.add).then_inc(s["ranks"], 1)
            dve.wait_ge(s["picks"], 4)
            link(V.tensor_scalar(sm[:, 7, :], sm[:, 3, :], 1.0, None, ALU.add))
            link(V.tensor_tensor(sm[:, 7, :], sm[:, 7, :], sm[:, 6, :], ALU.mult))
            link(V.reciprocal(wts[:, 0, :], sm[:, 7, :]))
            link(V.tensor_tensor(wts[:, 1, :], wts[:, 0, :], sm[:, 3, :], ALU.mult))
            dve.wait_ge(s["ranks"], 2)
            link(V.tensor_copy(rank[:], ps[:, 0, 0:NT * E].rearrange("p (t e) -> p t e", t=NT)))
            link(V.tensor_copy(tot[:], ps[:, 1, 0:NT * E].rearrange("p (t e) -> p t e", t=NT)))
            link(V.memset(cnt[:], 0.0))
            for t in range(NT):
                link(V.tensor_tensor(rank[:, t, :], rank[:, t, :], cnt[:], ALU.add))
                link(V.tensor_tensor(cnt[:], cnt[:], tot[:, t, :], ALU.add))
            link(V.tensor_scalar(chunk[:], rank[:], float(CAP), None, ALU.is_ge))
            link(V.tensor_scalar(ovc[:], cnt[:], float(CAP), None, ALU.is_gt))
            for j in range(2, -(-T // CAP)):
                link(V.tensor_scalar(tmp[:], rank[:], float(j * CAP), None, ALU.is_ge))
                link(V.tensor_tensor(chunk[:], chunk[:], tmp[:], ALU.add))
                link(V.tensor_scalar(ove[:], cnt[:], float(j * CAP), None, ALU.is_gt))
                link(V.tensor_tensor(ovc[:], ovc[:], ove[:], ALU.add))
            link(V.tensor_copy(ovi[:], ovc[:]))
            for d in (1, 2, 4, 8, 16):
                link(V.tensor_copy(ove[:], ovi[:]))
                link(V.tensor_tensor(ovi[:, d:], ove[:, d:], ove[:, 0:E - d], ALU.add))
            link(V.tensor_tensor(ove[:], ovi[:], ovc[:], ALU.subtract))
            link(V.tensor_tensor(ove[:], ove[:], eidx[:], ALU.subtract))
            link(V.tensor_scalar(ove[:], ove[:], float(E - 1), None, ALU.add))
            link(V.tensor_scalar(tmp[:], chunk[:], 0.5, None, ALU.is_ge))
            link(V.tensor_tensor(slot[:], tmp[:], c3(ove[:], E), ALU.mult))
            link(V.tensor_tensor(slot[:], slot[:], c3(eidx[:], E), ALU.add))
            link(V.scalar_tensor_tensor(out=slot[:], in0=chunk[:], scalar=float(1 - CAP * NBLK), in1=slot[:],
                                        op0=ALU.mult, op1=ALU.add))
            link(V.scalar_tensor_tensor(out=slot[:], in0=rank[:], scalar=float(NBLK), in1=slot[:],
                                        op0=ALU.mult, op1=ALU.add))
            for k, o in enumerate((o1, o2)):
                link(V.tensor_tensor(tmp[:], o[:], slot[:], ALU.mult))
                link(V.tensor_reduce(sm[:, k, :], tmp[:], AX.X, ALU.add))
                ins = V.tensor_copy(dest[:, k, :], sm[:, k, :])
                if k == 0:
                    link(ins)
                else:
                    ins.then_inc(s["route_done"], 1)
            link(V.tensor_tensor(ocmp[:], ovi[:].unsqueeze(1).to_broadcast([P, OVF, E]),
                                 oidx[:].unsqueeze(2).to_broadcast([P, OVF, E]), ALU.is_le))
            link(V.tensor_reduce(ocmp2[:, 0:OVF], ocmp[:], AX.X, ALU.add))
            link(V.tensor_scalar(ocmp2[:, 0:OVF], ocmp2[:, 0:OVF], float(E - 1), None, ALU.min))
            link(V.tensor_copy(ocmp2[:, OVF:], ovi[:, E - 1:E]))
            V.tensor_copy(eids[:], ocmp2[:]).then_inc(s["routed"], 1)

            def hidden(e):
                dve.wait_ge(s["up_mm"], e + 1)
                dve.wait_ge(s["silu_ok"], e + 1)
                wait(dve, s["h_tr"], e)
                V.tensor_tensor(hh[:], sg[:], bank(3), ALU.mult).then_inc(s["h_ok"], 1)

            def hidden_cols(e):
                dve.wait_ge(s["h_tr"], e + 1)
                wait(dve, s["down_mm"], e)
                V.tensor_copy(hhT[:], bank(4)).then_inc(s["hT_ok"], 1)

            def result(e, r):
                dve.wait_ge(s["down_mm"], e + 1)
                if isinstance(e, int):
                    wait(dve, s[f"y_out{r}"], 16 * (e // 2))
                V.tensor_copy(yy[:, r, :], bank(5, 2)).then_inc(s["y_ok"], 1)

            hidden(0)
            hidden_cols(0)
            hidden(1)
            result(0, 0)
            hidden_cols(1)
            hidden(2)
            result(1, 1)
            hidden_cols(2)
            hidden(3)
            dve.wait_ge(s["y_out0"], 16)
            result(2, 0)
            hidden_cols(3)
            with dve.Fori(2, E // 2) as i:
                hidden(i * 2)
                dve.wait_ge(s["y_out1"], (i - 1) * 16)
                result(i * 2 - 1, 1)
                hidden_cols(i * 2)
                hidden(i * 2 + 1)
                dve.wait_ge(s["y_out0"], i * 16)
                result(i * 2, 0)
                hidden_cols(i * 2 + 1)
            result(E - 1, 1)
            for r in range(2):
                dve.wait_ge(s[f"y_out{r}"], 16 * (E // 2))
            dve.wait_ge(s["routed"], 1)
            n_ov = dve.value_load(eids[0:1, OVF:OVF + 1], min_val=0, max_val=OVF)
            with dve.Fori(0, OVF) as o:
                with dve.If(o < n_ov):
                    dve.wait_ge(s["o_u"], o + 1)
                    dve.wait_ge(s["o_s"], o + 1)
                    V.tensor_tensor(hh[:], sg[:], bank(3), ALU.mult).then_inc(s["o_h"], 1)
                    dve.wait_ge(s["o_ht"], o + 1)
                    V.tensor_copy(hhT[:], bank(4)).then_inc(s["o_hT"], 1)
                    dve.wait_ge(s["o_dn"], o + 2)
                    V.tensor_copy(yy[:, 0, :], bank(5, 2)).then_inc(s["o_y"], 1)

            dve.wait_ge(s["mods3"], 16 * 10)
            for t in range(NT):
                r, side = t % 2, int(t == NPT)
                dve.wait_ge(s[f"ya_in{r}"], 32 * (t // 2 + 1))
                link(V.tensor_scalar(ya[:, r, :], ya[:, r, :], wts[:, 0, t:t + 1], None, ALU.mult))
                link(V.scalar_tensor_tensor(out=ya[:, r, :], in0=yb[:, r, :], scalar=wts[:, 1, t:t + 1],
                                            in1=ya[:, r, :], op0=ALU.mult, op1=ALU.add))
                link(V.tensor_tensor(ya[:, r, :], ya[:, r, :], gate2[:, side, :], ALU.mult))
                V.tensor_tensor(x1[:, t, :], x1[:, t, :], ya[:, r, :], ALU.add).then_inc(s["f_sq"], 1)
                dve.wait_ge(s["f_rt"], t + 1)
                if t >= 2:
                    dve.wait_ge(s[f"f_out{r}"], 16 * (t // 2))
                link(V.reciprocal(sumsq[:, 3, t:t + 1], sumsq[:, 3, t:t + 1]))
                V.scalar_tensor_tensor(out=yo[:, r, :], in0=x1[:, t, :], scalar=sumsq[:, 3, t:t + 1],
                                       in1=fg[:], op0=ALU.mult, op1=ALU.mult).then_inc(s["f_done"], 1)

        @block.tensor
        def _(pe):
            mm, tr = nc.tensor.matmul, nc.tensor.transpose
            pe.wait_ge(s["consts"], 1)
            pe.wait_ge(s["c_silu"], 1)
            n = SEQS + 1
            for k in range(KT):
                last = tr(ps[:, 6, k * n:(k + 1) * n], sc_sb[:, k * P:(k + 1) * P], ident[0:n, 0:n])
            last.then_inc(s["cT_ps"], 1)
            pe.wait_ge(s["cT_sb"], 1)
            for u in range(NADA):
                unit_landed(pe, u)
                wait(pe, s["mod_sb"], u - 1)
                for k in range(KT):
                    last = mm(ps[0:n, 4 + u % 2, :], cT[:, k, :], ring[u % 4][:, k, :],
                              start=(k == 0), stop=(k == KT - 1))
                last.then_inc(s["unit_used"], 1)

            for t in range(NT):
                r = t % 2
                pe.wait_ge(s["n1_h"], t + 1)
                wait(pe, s["n1_evac"], t - 1)
                for k in range(KT):
                    last = tr(bank(2 * r, 2)[:, k * P:(k + 1) * P], ht[:, r, k * P:(k + 1) * P], ident[:])
                last.then_inc(s["n1_tr"], 1)
            pe.wait_ge(s["n1_evac"], NT)

            pe.wait_ge(s["n1_evac"], NT)
            pe.wait_ge(s["mod_sb"], NADA)

            owners = []

            def group(owner, count):
                g = len(owners)
                if g >= 4:
                    pe.wait_ge(s[owners[g - 4][0]], owners[g - 4][1])
                owners.append((owner, count))
                return 4 + g % 4

            def project(u, owner, base_count, used=True):
                unit_landed(pe, u)
                done = 0
                for m in range(4):
                    for c0, cn in TOKCH:
                        b = group(owner, base_count + done + 1)
                        done += 1
                        for k in range(KT):
                            last = mm(ps[:, b, 0:cn], ring[u % 4][:, k, m * P:(m + 1) * P], hT[:, k, c0:c0 + cn],
                                      start=(k == 0), stop=(k == KT - 1))
                        last.then_inc(s["gemm"], 1)
                release(u)

            def release(u):
                pe.wait_ge(s["gemm"], len(owners))
                pe.sem_inc(s["unit_used"], 1)

            project(UQ, "gev_qk", 0)
            project(UK, "gev_qk", 12)
            pe.wait_ge(s["gev_qk"], 24)
            for i in range(5):
                b = group("gev_kout", i + 1)
                for m in range(HP):
                    src = kT[:, m, (4 + i) * P:(5 + i) * P] if i < 4 else kTs[:, m, :]
                    last = tr(ps[:, b, m * P:(m + 1) * P], src, ident[:])
                last.then_inc(s["gemm"], 1)
            unit_landed(pe, UV)
            for t in range(NT):
                b = group("gev_v", t + 1)
                for k in range(KT):
                    last = mm(ps[:, b, :], hT[:, k, t * P:(t + 1) * P], ring[UV % 4][:, k, :],
                              start=(k == 0), stop=(k == KT - 1))
                last.then_inc(s["gemm"], 1)
            release(UV)
            pe.wait_ge(s["gev_v"], NT)
            pe.wait_ge(s["gev_kout"], 5)

            NA = H * NPT

            def unit(a):
                pair, hh_ = a // 2, a % 2
                return pair // NPT, pair % NPT, hh_

            def scores(a):
                hp, i, h_ = unit(a)
                rows = slice(HD * h_, HD * h_ + HD)
                j0 = 4 - min(i, 4)
                wait(pe, s["s_sb"], a - 1)
                k0 = (i - 4 + j0) * P
                if j0 < 4:
                    mm(bank(2 * (a % 2))[:, j0 * P:512], qT[rows, hp, i * P:(i + 1) * P],
                       kT[rows, hp, k0:i * P], start=True, stop=True)
                mm(bank(2 * (a % 2) + 1)[:, 0:P], qT[rows, hp, i * P:(i + 1) * P],
                   kT[rows, hp, i * P:(i + 1) * P], start=True, stop=True).then_inc(s["s_scores"], 1)

            def prob_t(a):
                _, i, _ = unit(a)
                pe.wait_ge(s["s_p"], a + 1)
                wait(pe, s["s_ptc"], a)
                for j in range(4 - min(i, 4), 5):
                    last = tr(bank(4, 2)[:, j * P:(j + 1) * P], Pr[:, a % 2, j * P:(j + 1) * P], ident[:])
                last.then_inc(s["s_pt"], 1)

            def values(a):
                hp, i, h_ = unit(a)
                pe.wait_ge(s["s_ptc"], a + 1)
                if h_ == 0:
                    wait(pe, s["s_at"], a // 2)
                j0 = 4 - min(i, 4)
                for j in range(j0, 5):
                    last = mm(ps[:, 6, HD * h_:HD * h_ + HD], PT[:, a % 2, j, :],
                              v[:, i - 4 + j, (2 * hp + h_) * HD:(2 * hp + h_ + 1) * HD],
                              start=(j == j0), stop=(j == 4))
                last.then_inc(s["s_pv"], 1)

            def att_t(pair):
                pe.wait_ge(s["s_at"], pair + 1)
                wait(pe, s["s_attc"], pair)
                tr(ps[:, 7, 0:P], attt[:, pair % 2, :], ident[:]).then_inc(s["s_att"], 1)

            scores(0)
            scores(1)
            for a in range(NA):
                if a + 2 < NA:
                    scores(a + 2)
                prob_t(a)
                if a >= 1:
                    values(a - 1)
                if a % 2 == 1 and a >= 3:
                    att_t(a // 2 - 1)
            values(NA - 1)
            att_t(NA // 2 - 1)
            pe.wait_ge(s["s_attc"], HP * NPT)

            for q in range(SEQS):
                r = q % 2
                pe.wait_ge(s[f"kv_in{r}"], 32 * (q // 2 + 1))
                wait(pe, s["k_trc"], q)
                for m in range(HP):
                    for c in range(4):
                        last = tr(ps[:, m, c * P:(c + 1) * P], kc[:, r, c, m * P:(m + 1) * P], ident[:])
                last.then_inc(s["k_tr"], 1)
                pe.wait_ge(s["k_trc"], q + 1)
                pe.wait_ge(s["qb"], 2 * q + 2)
                wait(pe, s["ks_at"], q)
                qb = qblk[:, r, 0:512].rearrange("p (m c) -> p m c", m=HP)
                for m in range(HP):
                    mm(ps[:, 4, :], qb[:, m, :], kcT[:, m, :], start=(m == 0), stop=(m == HP - 1))
                for m in range(HP):
                    last = mm(ps[:, 5, 0:DEC], qb[:, m, :], kTs[:, m, q * DEC:(q + 1) * DEC],
                              start=(m == 0), stop=(m == HP - 1))
                last.then_inc(s["ks_sc"], 1)
                pe.wait_ge(s["ks_pn"], q + 1)
                wait(pe, s["ks_ptc"], 2 * q)
                for c in range(4):
                    tr(ps[:, 6, c * P:(c + 1) * P], Pn[:, c * P:(c + 1) * P], ident[:])
                tr(ps[0:DEC, 7, 0:P], Pn[:, PAST:NK], ident[:]).then_inc(s["ks_pt"], 1)
                pe.wait_ge(s["ks_ptc"], 2 * q + 2)
                pe.wait_ge(s["ks_sb"], q + 1)
                pe.wait_ge(s[f"v16_in{r}"], 16 * (q // 2 + 1))
                for m in range(HP):
                    out = ps[:, 5, P + m * 32:P + (m + 1) * 32]
                    for c in range(4):
                        mm(out, vc[:, r, c, m * P:(m + 1) * P], PTs[:, c, m * 32:(m + 1) * 32],
                           start=(c == 0), stop=False)
                    last = mm(out, v16[:, r, m * P:(m + 1) * P], PTs[0:DEC, 4, m * 32:(m + 1) * 32],
                              start=False, stop=True)
                last.then_inc(s["ks_pv"], 1)
            pe.wait_ge(s["ks_at"], SEQS)

            g0 = len(owners)
            project(UCC, "gev_conv", 0)
            project(UCV, "cu_done", 0)
            pe.wait_ge(s["prev_in"], 16)
            b = group("gev_prev", 1)
            for m in range(HP):
                last = tr(ps[:, b, m * 16:(m + 1) * 16], st_in[:, m * P:(m + 1) * P], ident[0:16, 0:16])
            last.then_inc(s["gemm"], 1)
            pe.wait_ge(s["conv_last"], 1)
            b = group("newc_sb", 1)
            for m in range(HP):
                last = tr(ps[0:18, b, m * P:(m + 1) * P], lastu[:, m, :], ident[:])
            last.then_inc(s["gemm"], 1)
            project(UCB, "cu_done", 12)
            pe.wait_ge(s["cu_done"], 24)

            for i in range(24):
                f, (c0, cn) = i // 3, TOKCH[i % 3]
                half, m = f // 4, f % 4
                ua, ub, up = [UGATE + 3 * half + j for j in range(3)]
                if f % 4 == 0 and i % 3 == 0:
                    for u in (ua, ub, up):
                        unit_landed(pe, u)
                wait(pe, s["g_done"], i - 1)
                b = 4 * (i % 2)
                lhs = slice(m * P, (m + 1) * P)
                for kind, (u, k0, kn, rhs) in enumerate(((ua, 0, KT, hT), (up, 0, 4, qT), (ub, 0, KT, hT),
                                                         (up, 4, 4, Y))):
                    for k in range(kn):
                        last = mm(ps[:, b + kind, 0:cn], ring[u % 4][:, k0 + k, lhs], rhs[:, k, c0:c0 + cn],
                                  start=(k == 0), stop=(k == kn - 1))
                    last.then_inc(s["g_ready"], 1)
                if i % 12 == 11:
                    pe.wait_ge(s["g_ready"], 4 * (i + 1))
                    pe.sem_inc(s["unit_used"], 3)
            pe.wait_ge(s["g_done"], 24)

            unit_landed(pe, UO)
            unit_landed(pe, UO + 1)

            def out_project(t):
                wait(pe, s["x1_done"], t - 1)
                for h in range(2):
                    for k in range(KT):
                        last = mm(ps[:, 2 * (t % 2) + h, :], mixT[:, k, t * P:(t + 1) * P],
                                  ring[(UO + h) % 4][:, k, :], start=(k == 0), stop=(k == KT - 1))
                last.then_inc(s["o_done"], 1)

            pe.wait_ge(s["wr_in"], 64)
            out_project(0)
            for t in range(NT):
                if t + 1 < NT:
                    out_project(t + 1)
                pe.wait_ge(s["n2_h"], t + 1)
                wait(pe, s["n2_evac"], t)
                for k in range(KT):
                    last = tr(bank(4, 2)[:, k * P:(k + 1) * P], h2[:, t % 2, k * P:(k + 1) * P], ident[:])
                last.then_inc(s["n2_tr"], 1)
                pe.wait_ge(s["n2_evac"], t + 1)
                wait(pe, s["n2_lev"], t)
                for k in range(KT):
                    last = mm(ps[:, 6, 0:NLOG], h2T[:, k * P:(k + 1) * P], wr[:, k, :],
                              start=(k == 0), stop=(k == KT - 1))
                last.then_inc(s["n2_log"], 1)
            pe.wait_ge(s["o_done"], NT)
            pe.sem_inc(s["unit_used"], 2)

            pe.wait_ge(s["ranks"], 1)
            pv = picked[:].rearrange("p t e -> p (t e)")
            mm(ps[:, 0, 0:NT * E], before[:], pv, start=True, stop=True)
            mm(ps[:, 1, 0:NT * E], ones[:], pv, start=True, stop=True).then_inc(s["ranks"], 1)
            pe.wait_ge(s["route_done"], 1)

            def rows_t(e, r, count):
                wait(pe, s["xT_ok"], e)
                pe.wait_ge(s[f"xg_in{r}"], count)
                for k in range(KT):
                    last = tr(bank(0, 2)[:, k * P:(k + 1) * P], xg[:, r, k * P:(k + 1) * P], ident[:])
                last.then_inc(s["xg_tr"], 1)

            def half_mlp(b, r, slot_no, sig):
                w = mring[slot_no][:].rearrange("p (k n) -> p k n", k=KT)
                for k in range(KT):
                    last = mm(bank(b), xT[:, r, k * P:(k + 1) * P], w[:, k, :], start=(k == 0), stop=(k == KT - 1))
                last.then_inc(s[sig], 1)

            def gate_up(e, r, count):
                pe.wait_ge(mlanded[3 * r], count)
                pe.wait_ge(s["xT_ok"], e + 1)
                wait(pe, s["silu_ok"], e)
                half_mlp(2, r, 3 * r, "gate_mm")
                pe.wait_ge(mlanded[3 * r + 1], count)
                wait(pe, s["h_ok"], e)
                half_mlp(3, r, 3 * r + 1, "up_mm")

            def down_mms(slot_no, sig):
                w = mring[slot_no][:].rearrange("p (k n) -> p k n", k=4)
                for h in range(2):
                    for k in range(4):
                        last = mm(bank(5 + h), hhT[:, k * P:(k + 1) * P], w[:, k, h * 512:(h + 1) * 512],
                                  start=(k == 0), stop=(k == 3))
                last.then_inc(s[sig], 1)

            def down(e, r, count):
                pe.wait_ge(mlanded[3 * r + 2], count)
                pe.wait_ge(s["hT_ok"], e + 1)
                wait(pe, s["y_ok"], e)
                down_mms(3 * r + 2, "down_mm")

            def hidden_mms(sig):
                for k in range(4):
                    last = tr(bank(4)[:, k * P:(k + 1) * P], hh[:, k * P:(k + 1) * P], ident[:])
                last.then_inc(s[sig], 1)

            def hidden_t(e):
                pe.wait_ge(s["h_ok"], e + 1)
                wait(pe, s["hT_ok"], e)
                hidden_mms("h_tr")

            rows_t(0, 0, 16)
            gate_up(0, 0, 16)
            rows_t(1, 1, 16)
            hidden_t(0)
            gate_up(1, 1, 16)
            rows_t(2, 0, 32)
            down(0, 0, 16)
            hidden_t(1)
            with pe.Fori(1, E // 2 - 1) as i:
                gate_up(i * 2, 0, (i + 1) * 16)
                rows_t(i * 2 + 1, 1, (i + 1) * 16)
                down(i * 2 - 1, 1, i * 16)
                hidden_t(i * 2)
                gate_up(i * 2 + 1, 1, (i + 1) * 16)
                rows_t(i * 2 + 2, 0, (i + 2) * 16)
                down(i * 2, 0, (i + 1) * 16)
                hidden_t(i * 2 + 1)
            c = 16 * (E // 2)
            gate_up(E - 2, 0, c)
            rows_t(E - 1, 1, c)
            down(E - 3, 1, c - 16)
            hidden_t(E - 2)
            gate_up(E - 1, 1, c)
            down(E - 2, 0, c)
            hidden_t(E - 1)
            down(E - 1, 1, c)

            pe.wait_ge(s["routed"], 1)
            pe.wait_ge(s["y_ok"], E)
            n_ov = pe.value_load(eids[0:1, OVF:OVF + 1], min_val=0, max_val=OVF)
            pe.sem_inc(s["o_dn"], 1)
            with pe.Fori(0, OVF) as o:
                with pe.If(o < n_ov):
                    pe.wait_ge(s["o_xg"], (o + 1) * 16)
                    for k in range(KT):
                        last = tr(bank(0, 2)[:, k * P:(k + 1) * P], xg[:, 0, k * P:(k + 1) * P], ident[:])
                    last.then_inc(s["o_tr"], 1)
                    pe.wait_ge(s["o_xT"], o + 1)
                    pe.wait_ge(s["o_w"], (o + 1) * 48)
                    half_mlp(2, 0, 0, "o_g")
                    half_mlp(3, 0, 1, "o_u")
                    pe.wait_ge(s["o_h"], o + 1)
                    hidden_mms("o_ht")
                    pe.wait_ge(s["o_hT"], o + 1)
                    down_mms(2, "o_dn")



_INS = ['x_prompt', 'x_sample', 'cache_attn_k', 'cache_attn_v', 'state_conv', 'c_prompt', 'c_sample',
        'w_ada', 'b_ada', 'norm1_g', 'norm2_g', 'w_in', 'rel_bias', 'conv_w', 'conv_b', 'w_pa', 'w_pb', 'w_o',
        'w_group', 'b_group', 'w_expert', 'b_expert', 'w_e_gate', 'w_e_up', 'w_e_down', 'final_g']
_OUTS = [(1, NP_TOK, D), (SEQS, DEC, D), (1, 1, 512, H, HD), (1, 1, 512, H, HD), (1, 1, 2, DA),
         (1, SEQS, DEC, H, HD), (1, SEQS, DEC, H, HD), (1, SEQS, 2, DA)]


def kernel(**inputs):
    import numpy as _np
    import concourse.bacc as _bacc
    from concourse import mybir as _mybir
    from concourse.bass_utils import run_bass_kernel_spmd as _run

    nc = _bacc.Bacc("TRN2", target_bir_lowering=False, num_devices=1)
    arrays, args = {}, []
    for name in _INS:
        a = _np.ascontiguousarray(inputs[name])
        arrays[f"in_{name}_dram"] = a
        args.append(nc.dram_tensor(f"in_{name}_dram", a.shape, _mybir.dt.from_np(a.dtype), kind="ExternalInput").ap())
    for i, shape in enumerate(_OUTS):
        args.append(nc.dram_tensor(f"out_{i}_dram", shape, _mybir.dt.float32, kind="ExternalOutput").ap())
    build(nc, *args)
    r = _run(nc, [arrays], core_ids=[0])
    return tuple(r.results[0][f"out_{i}_dram"] for i in range(len(_OUTS)))
```

```python
from contextlib import ExitStack

import concourse.bass as bass
from concourse import mybir

ALU = mybir.AluOpType
ACT = mybir.ActivationFunctionType
AX = mybir.AxisListType
F32 = mybir.dt.float32
F32R = mybir.dt.float32r
I32 = mybir.dt.int32

P = 128
D = 1024
KT = D // P
NP_TOK, SEQS, DEC = 1024, 8, 16
NS_TOK = SEQS * DEC
T = NP_TOK + NS_TOK
NPT = NP_TOK // P
NT = T // P
H, HD = 8, 64
HP = H // 2
DA = H * HD
CW = 3
PAST = 512
MAXREL = 128
NREL = 2 * MAXREL + 1
BAND = 5 * P
NEG = -1e30
EPS = 1e-6
G, EPG = 4, 8
E = G * EPG
DE = 512
NLOG = G + E
CAP = P
OVF = (2 * T) // CAP - 1
NBLK = E + OVF
SEQROW = SEQS
TC = T // 3
TOKCH = [(0, TC), (TC, TC), (2 * TC, TC)]


class Link:

    def __init__(self, eng, sem):
        self.eng, self.sem, self.n = eng, sem, 0

    def __call__(self, ins):
        self.n += 1
        ins.then_inc(self.sem, 1)
        self.eng.wait_ge(self.sem, self.n)


def wait(eng, sem, value):
    if isinstance(value, int) and value <= 0:
        return
    eng.wait_ge(sem, value)


def parts(c0, cn):
    out = []
    if c0 < NP_TOK:
        out.append((c0, min(c0 + cn, NP_TOK) - c0, False))
    if c0 + cn > NP_TOK:
        start = max(c0, NP_TOK)
        out.append((start, c0 + cn - start, True))
    return out


def build(nc, x_prompt, x_sample, cache_attn_k, cache_attn_v, state_conv, c_prompt, c_sample,
          w_ada, b_ada, norm1_g, norm2_g, w_in, rel_bias, conv_w, conv_b, w_pa, w_pb, w_o,
          w_group, b_group, w_expert, b_expert, w_e_gate, w_e_up, w_e_down, final_g,
          y_prompt, y_sample, new_k_prompt, new_v_prompt, new_conv_prompt,
          new_k_sample, new_v_sample, new_conv_sample):
    with ExitStack() as ctx:
        base = (nc.sbuf_base + 63) // 64 * 64
        KB = 1024
        CONST, RING, ARENA = 0, 8 * KB + 512, 56 * KB + 512

        def at(name, shape, offset, dt=F32):
            return nc.alloc_sbuf_tensor_at(name, shape, dt, offset=base + int(offset))

        def sem(name):
            return ctx.enter_context(nc.semaphore(name))

        def psum(name, shape):
            return ctx.enter_context(nc.psum_tensor(name, shape, F32))

        def dram(name, shape, dt=F32):
            return nc.dram_tensor(name, shape, dt).ap()

        mod_d = dram("mod_d", (SEQS + 1, 6 * D))
        relrow_d = dram("relrow_d", (H, P, P - 1 + BAND))
        mix_d = dram("mix_d", (NT, P, KT, P))
        h2_d = dram("h2_d", (T, D))
        y_d = dram("y_d", (P * NBLK, D))

        cur = [CONST]

        def small(name, shape, dt=F32):
            n = 1
            for s in shape[1:]:
                n *= s
            n = (n * 4 + 31) // 32 * 32
            t = at(name, shape, cur[0], dt)
            cur[0] += n
            assert cur[0] <= RING, cur[0]
            return t

        ident = small("ident", [P, P])
        before = small("before", [P, P])
        ones = small("ones", [P, P])
        eps = small("eps", [P, 1])
        tokid = small("tokid", [P, NT])
        sumsq = small("sumsq", [P, 4, NT])
        rowmax = small("rowmax", [P, 72])
        negmax = small("negmax", [P, 72])
        rowsum = small("rowsum", [P, 72])
        rinv = small("rinv", [P, 72])
        convw = small("convw", [P, CW + 1, HP])
        wr = small("wr", [P, KT, NLOG])
        br = small("br", [P, NLOG])
        logits = small("logits", [P, NT, NLOG])
        table = small("table", [P, NBLK], I32)
        dest = small("dest", [P, 2, NT], I32)
        wts = small("wts", [P, 2, NT])
        eids = small("eids", [P, OVF + 1], I32)
        idx = small("idx", [P, 2], I32)
        lastu = small("lastu", [P, HP, 18])

        NSLOT = 6
        UB = 4 * KB
        ring_r = at("ring_r", [P, NSLOT + 2, 2, KT, P], RING, F32R)
        ring_f = at("ring_f", [P, NSLOT + 2, 2, KT, P], RING)
        SLOT = 16 * KB
        MH = 4 * 512
        mhi = [at(f"mhi{j}", [P, MH], RING + j * SLOT, F32R) for j in range(6)]
        mraw = [at(f"mraw{j}", [P, MH], RING + j * SLOT + SLOT // 2) for j in range(6)]
        mlo = [at(f"mlo{j}", [P, MH], RING + j * SLOT + SLOT // 2, F32R) for j in range(6)]

        def A(kb):
            return ARENA + kb * KB

        def X(kb):
            return RING + 8 * 4 * KB + kb * KB

        aring = [at(f"aring{j}", [P, KT, 512], RING + j * SLOT if j < 3 else A(108)) for j in range(4)]
        hTh = at("hTh", [P, KT, T], A(0), F32R)
        hTl = at("hTl", [P, KT, T], A(36), F32R)
        qT = at("qT", [P, HP, T], A(72))
        kT = at("kT", [P, HP, NP_TOK], A(90))
        kTs = at("kTs", [P, HP, NS_TOK], A(106))
        v = at("v", [P, NT, DA], A(108))
        kk = at("kk", [P, 2, DA], A(144))
        zrow = at("zrow", [P, 256], A(149))
        bada0 = at("bada0", [SEQS + 1, 4 * 512], A(60))
        relin = at("relin", [H, NREL], A(148.5))
        relrow = at("relrow", [H, P - 1 + BAND], A(124))
        c_sb = at("c_sb", [SEQS + 1, D], A(124))
        cT = at("cT", [P, KT, SEQS + 1], A(128))
        modc = at("modc", [SEQS + 1, 2, 512], A(128.5))
        bada1 = at("bada1", [SEQS + 1, 8 * 512], A(132.5))
        xt = at("xt", [P, 2, D], A(72))
        ht = at("ht", [P, 2, D], A(80))
        scale1 = at("scale1", [P, 2, D], A(88))
        shift1 = at("shift1", [P, 2, D], A(96))
        g1 = at("g1", [P, D], A(104))
        bias = at("bias", [P, H, BAND], A(128))
        qz = at("qz", [P, 2, 2, P], A(148))
        S = at("S", [P, 2, BAND], X(0))
        Pr = at("Pr", [P, 2, BAND], X(5))
        PT = at("PT", [P, 2, 5, P], X(10))
        attt = at("attt", [P, 2, P], X(15))
        NK = PAST + DEC
        kc = at("kc", [P, 2, 4, DA], A(90))
        vc = at("vc", [P, 2, 4, DA], A(108))
        kcT = at("kcT", [P, HP, PAST], A(128))
        Ps = at("Ps", [P, NK], A(136))
        PTs = at("PTs", [P, 5, P], A(138.5))
        sbias = at("sbias", [P, NK], A(141))
        Ss = at("Ss", [P, NK], X(0))
        atts = at("atts", [P, DA], X(3))
        v16 = at("v16", [DEC, 2, DA], X(5))
        qblk = at("qblk", [P, 2, 640], X(9))
        U = at("U", [P, HP, NP_TOK + 2], A(90))
        Us = at("Us", [P, HP, SEQS, DEC + 2], A(106.25))
        st_in = at("st_in", [SEQS * 2, DA], A(109))
        newc = at("newc", [18, DA], A(111))
        Yh = at("Yh", [P, HP, T], A(114), F32R)
        Y = at("Y", [P, HP, T], A(132.5))
        Yl = at("Yl", [P, HP, T], A(132.5), F32R)
        atth = at("atth", [P, HP, T], A(90), F32R)
        attl = at("attl", [P, HP, T], A(72), F32R)
        sgA = at("sgA", [P, 512], A(108))
        sgB = at("sgB", [P, 512], A(110))
        mixc = at("mixc", [P, 512], A(112))
        mixh = at("mixh", [P, 2, KT, P], A(16), F32R)
        mixr = at("mixr", [P, 2, KT, P], A(24))
        mixl = at("mixl", [P, 2, KT, P], A(24), F32R)
        x1 = at("x1", [P, NT, D], A(48))
        h2 = at("h2", [P, 2, D], A(84))
        h2T = at("h2T", [P, D], A(92))
        sq = at("sq", [P, D], A(96))
        gate1 = at("gate1", [P, 2, D], A(100))
        scale2 = at("scale2", [P, 2, D], A(108))
        shift2 = at("shift2", [P, 2, D], A(116))
        xr = at("xr", [P, 2, D], A(124))
        g2 = at("g2", [P, D], A(132))
        R = 122

        def rt(i, shape, dt=F32):
            return at(f"route{i}", shape, A(R) + i * 1184, dt)

        lg = rt(0, [P, NT, G])
        gmask = rt(1, [P, NT, G])
        le = rt(2, [P, NT, E])
        o1 = rt(3, [P, NT, E])
        o2 = rt(4, [P, NT, E])
        picked = rt(5, [P, NT, E])
        rank = rt(6, [P, NT, E])
        tmp = rt(8, [P, NT, E])
        prefix = rt(9, [P, NT, E])
        picks_of = rt(10, [P, 8, 2, NT])
        tieb = rt(11, [P, 64])
        eidx = rt(12, [P, E])
        cnt = rt(13, [P, E])
        ovc = rt(14, [P, E])
        ovi = rt(15, [P, E])
        ove = rt(16, [P, E])
        sm = rt(17, [P, 8, NT])
        ocmp = rt(18, [P, OVF, E])
        ocmp2 = rt(21, [P, OVF + 1])
        oidx = rt(22, [P, OVF])
        rowi = rt(23, [P, P])
        blki = rt(7, [P, NBLK])
        NBP = NBLK + NBLK % 2
        onerow = at("onerow", [P, 2 * NT, P], A(100), F32R)
        oneblk = at("oneblk", [P, 2 * NT, NBP], A(110), F32R)
        xg = at("xg", [P, 2, D], A(84))
        xTh = at("xTh", [P, 2, D], A(92), F32R)
        xTl = at("xTl", [P, 2, D], A(100), F32R)
        sg = at("sg", [P, DE], A(108))
        hh = at("hh", [P, DE], A(110))
        hhTh = at("hhTh", [P, DE], A(112), F32R)
        hhTl = at("hhTl", [P, DE], A(114), F32R)
        yy = at("yy", [P, 2, D], A(116))
        gate2 = at("gate2", [P, 2, D], A(124))
        fg = at("fg", [P, D], A(132))
        ya = at("ya", [P, NT, D], RING)
        yb = at("yb", [P, NT, D], RING + 36 * KB)
        yo = at("yo", [P, 2, D], RING + 72 * KB)
        yq = at("yq", [P, D], RING + 80 * KB)

        ps = psum("ps", [P, 8, 512])

        def u_part(m, c0, t0, tn, sample, g):
            src = ps[:, 4 + g % 4, t0 - c0:t0 - c0 + tn]
            if sample:
                return Us[:, m, :, 2:], src.rearrange("p (q t) -> p q t", t=DEC)
            return U[:, m, 2 + t0:2 + t0 + tn], src

        def bank(b, n=1):
            return ps[:, b:b + n, :].rearrange("p b c -> p (b c)")

        names = """consts conv_in c_in badain c_silu cT_ps cT_sb unit_used mod_sb mod_out0 mod_out1 rel_in rel_sb rel_out
            mods1 x_in0 x_in1 n1_sq n1_rt n1_h n1_tr n1_evac
            gemm gev_qk gev_kout gev_v gev_prev gev_conv qz_ok kk_out v_out bias_in bias_ok
            s_scores s_sb s_p s_pt s_ptc s_pv s_at s_att s_attc
            k_in0 k_in1 v_in0 v_in1 sb_in w_hi w_lo n1_lo b_hi b_lo mix_out mix_in0 mix_in1 k_tr k_trc qb ks_sc ks_sb ks_p ks_ev ks_pt ks_ptc ks_pv ks_att ks_at
            prev_in conv_last conv_out newc_sb cu_done
            g_ready g_sig g_done wr_in
            mods2 xr_in0 xr_in1 o_done x1_done n2_sq n2_rt n2_h n2_tr n2_evac n2_log n2_lev h2_out0 h2_out1
            picks ranks rconst onehot table_ps route_done routed gathers zrow_ok y_zeroed
            xg_in0 xg_in1 idxc xg_tr xTh_ok xTl_ok gu_hi gu_lo d_hi d_lo gu_used d_used
            silu_ok h_ok h_tr hTh_ok hTl_ok y_ok y_out0 y_out1
            o_w o_idx o_xg o_pe o_act o_dve o_dn o_out
            mods3 ya_in0 ya_in1 ya_in2 ya_in3 f_w f_sq f_rt f_out0 f_out1 f_done
            link_dve link_pool""".split()
        s = {n: sem(n) for n in names}
        landed = [sem(f"landed{i}") for i in range(NSLOT)]

        w_in2 = w_in[0].rearrange("(k p) n -> p k n", p=P)
        w_ada2 = w_ada[0].rearrange("(k p) n -> p k n", p=P)
        w_pa2 = w_pa[0].rearrange("(k p) n -> p k n", p=P)
        w_pb2 = w_pb[0].rearrange("(k p) n -> p k n", p=P)
        w_o2 = w_o[0].rearrange("(k p) n -> p k n", p=P)

        def cols(w, c, n):
            return [w[:, 0:4, c * n:(c + 1) * n], w[:, 4:8, c * n:(c + 1) * n]]

        NADA = 6 * D // 512
        ada_units = [cols(w_ada2, c, 512) for c in range(NADA)]
        units = []
        UQ, UK, UV, UCC, UCV, UCB = [4 * i for i in range(6)]
        for c in (0, 1, 2, 4, 5, 3):
            units += [cols(w_in2, 4 * c + j, P) for j in range(4)]
        UGATE = len(units)
        for f in range(KT):
            units.append(cols(w_in2, 24 + f, P))
            units.append(cols(w_in2, 32 + f, P))
            units.append([w_pa2[:, :, f * P:(f + 1) * P], w_pb2[:, :, f * P:(f + 1) * P]])
        UO = len(units)
        units += [cols(w_o2, j, P) for j in range(KT)]
        NU = len(units)
        ADA_IN = 32 * (NADA // 4)

        def slot_of(u):
            return u % NSLOT if u < NU - 2 else u - (NU - 8)

        def landed_value(u):
            return 32 * (u // NSLOT + 1) + (ADA_IN if u % NSLOT < 4 else 0)

        def unit_in(u):
            return landed[u % NSLOT], landed_value(u)

        LAST_IN = [landed_value(max(u for u in range(NU) if u % NSLOT == j)) for j in range(NSLOT)]

        block = ctx.enter_context(nc.Block())

        def load_mod(eng, dst, part, signal):
            eng.dma_start(dst[:, 0, :], bass.AP(mod_d.tensor, SEQROW * 6 * D + part * D, [[0, P], [1, D]])
                          ).then_inc(signal, 16)
            for q in range(SEQS):
                eng.dma_start(dst[q * DEC:(q + 1) * DEC, 1, :],
                              bass.AP(mod_d.tensor, q * 6 * D + part * D, [[0, DEC], [1, D]])
                              ).then_inc(signal, 16)

        def vec_all(eng, dst, vec, n, signal):
            eng.dma_start(dst, bass.AP(vec.tensor, vec.offset, [[0, P], [1, n]])).then_inc(signal, 16)

        @block.sync
        def _(sp):
            def old_keys(q):
                wait(sp, s["k_tr"], q - 1)
                sp.dma_start(kc[:, q % 2], cache_attn_k[0, q].rearrange("(c p) h d -> p c (h d)", p=P)
                             ).then_inc(s[f"k_in{q % 2}"], 16)

            def load_caches():
                sp.wait_ge(s["v_out"], 32)
                sp.wait_ge(s["s_attc"], HP * NPT)
                old_keys(0)
                for q in range(SEQS):
                    if q + 1 < SEQS:
                        old_keys(q + 1)
                    wait(sp, s["ks_pv"], q - 1)
                    sp.dma_start(vc[:, q % 2], cache_attn_v[0, q].rearrange("(c p) h d -> p c (h d)", p=P)
                                 ).then_inc(s[f"v_in{q % 2}"], 16)
                    sp.dma_start(v16[:, q % 2, :], new_v_sample[0, q].rearrange("t h d -> t (h d)")
                                 ).then_inc(s[f"v_in{q % 2}"], 16)
                sp.wait_ge(s["ks_at"], H * SEQS)

            for u, halves in enumerate(ada_units):
                if u == 8:
                    for r in range(2):
                        sp.wait_ge(s[f"mod_out{r}"], 16 * 2)
                    load_mod(sp, scale1, 1, s["mods1"])
                    load_mod(sp, shift1, 0, s["mods1"])
                wait(sp, s["unit_used"], u - 3)
                for i, src in enumerate(halves):
                    sp.dma_start(aring[u % 4][:, 4 * i:4 * i + 4, :], src).then_inc(landed[u % 4], 16)
            for u, halves in enumerate(units):
                if u == UCV:
                    load_caches()
                if u == NU - 2:
                    sp.wait_ge(s["g_ready"], 4 * 24)
                    for j in range(2):
                        sp.wait_ge(landed[j], landed_value(u - NSLOT + j))
                if u < NSLOT:
                    sp.wait_ge(s["unit_used"], min(9 + u, NADA))
                elif u < NU - 2:
                    sp.wait_ge(s["unit_used"], NADA + u - NSLOT + 1)
                for i, src in enumerate(halves):
                    sp.dma_start(ring_f[:, slot_of(u), 1, 4 * i:4 * i + 4, :], src
                                 ).then_inc(landed[u % NSLOT], 16)

            def mixture(t):
                wait(sp, s["o_done"], t - 1)
                sp.dma_start(mixr[:, t % 2], mix_d[t]).then_inc(s[f"mix_in{t % 2}"], 16)

            sp.wait_ge(s["mix_out"], 16 * 24)
            mixture(0)
            mixture(1)
            for r in range(2):
                sp.wait_ge(s[f"mod_out{r}"], 8 * NADA)
            load_mod(sp, gate1, 2, s["mods2"])
            vec_all(sp, g2[:], norm2_g, D, s["mods2"])
            load_mod(sp, scale2, 4, s["mods2"])
            load_mod(sp, shift2, 3, s["mods2"])
            for t in range(2, NT):
                mixture(t)

            gate_d = w_e_gate[0].rearrange("e (k p) n -> p e k n", p=P)
            up_d = w_e_up[0].rearrange("e (k p) n -> p e k n", p=P)
            down_d = w_e_down[0].rearrange("e (k p) n -> p e k n", p=P)

            def half_of(j, ex):
                w, k0, kn = ((gate_d, 0, 4), (gate_d, 4, 4), (up_d, 0, 4), (up_d, 4, 4),
                             (down_d, 0, 2), (down_d, 2, 2))[j]
                return (w[:, ex, k0:k0 + kn] if isinstance(ex, int)
                        else w[:, bass.ds(ex, 1), k0:k0 + kn].rearrange("p e k n -> p (e k) n"))

            def place_of(j):
                return mraw[j][:].rearrange("p (k n) -> p k n", k=4 if j < 4 else 2)

            def load_gate_up(e):
                for j in range(4):
                    wait(sp, s["gu_used"], e * 4 + (j - 3))
                    sp.dma_start(place_of(j), half_of(j, e)).then_inc(landed[j], 16)

            def load_down(e):
                for j in range(4, 6):
                    wait(sp, s["d_used"], e * 2 + (j - 5))
                    sp.dma_start(place_of(j), half_of(j, e)).then_inc(landed[j], 16)

            sp.wait_ge(s["unit_used"], NADA + NU)
            load_gate_up(0)
            sp.wait_ge(s["routed"], 1)
            load_gate_up(1)
            load_down(0)
            vec_all(sp, fg[:], final_g, D, s["mods3"])
            load_mod(sp, gate2, 5, s["mods3"])
            with sp.Fori(2, E) as e:
                load_gate_up(e)
                load_down(e - 1)
            load_down(E - 1)

            sp.wait_ge(s["d_used"], 2 * E)
            n_ov = sp.value_load(eids[0:1, OVF:OVF + 1], min_val=0, max_val=OVF)
            with sp.If(n_ov > 0):
                with sp.Fori(0, OVF) as o:
                    with sp.If(o < n_ov):
                        ex = sp.value_load(eids[0:1, bass.ds(o, 1)], min_val=0, max_val=E - 1)
                        sp.wait_ge(s["o_dn"], o + 1)
                        for j in range(6):
                            sp.dma_start(place_of(j), half_of(j, ex)).then_inc(s["o_w"], 16)

            for t in range(NT):
                sp.wait_ge(s["f_done"], t + 1)
                dst = y_prompt[0, t * P:(t + 1) * P, :] if t < NPT else y_sample.rearrange("s t d -> (s t) d")
                sp.dma_start(dst, yo[:, t % 2, :]).then_inc(s[f"f_out{t % 2}"], 16)
            sp.wait_ge(s["f_out0"], 16 * 5)
            sp.wait_ge(s["f_out1"], 16 * 4)
            sp.wait_ge(s["conv_out"], 32)
            sp.wait_ge(s["kk_out"], 16 * 5)
            sp.wait_ge(s["v_out"], 16 * 2)

        @block.gpsimd
        def _(pool):
            link = Link(pool, s["link_pool"])

            def row_all(src):
                return src.partition_broadcast(P)

            pool.dma_start(c_sb[0:SEQS, :], c_sample).then_inc(s["c_in"], 16)
            pool.dma_start(c_sb[SEQS:SEQS + 1, :], c_prompt).then_inc(s["c_in"], 16)
            for b, c0 in ((bada0, 0), (bada1, 4 * 512)):
                pool.dma_start(b[:], bass.AP(b_ada.tensor, b_ada.offset + c0, [[0, SEQS + 1], [1, b.shape[1]]])
                               ).then_inc(s["badain"], 16)
            link(nc.gpsimd.memset(ident[:], 0.0))
            link(nc.gpsimd.affine_select(out=ident[:], in_=ident[:], compare_op=ALU.not_equal, fill=1.0,
                                         base=0, pattern=[[-1, P]], channel_multiplier=1))
            link(nc.gpsimd.memset(before[:], 1.0))
            link(nc.gpsimd.affine_select(out=before[:], in_=before[:], compare_op=ALU.is_gt, fill=0.0,
                                         base=0, pattern=[[1, P]], channel_multiplier=-1))
            link(nc.gpsimd.memset(ones[:], 1.0))
            link(nc.gpsimd.memset(eps[:], EPS))
            nc.gpsimd.iota(tokid[:], [[P, NT]], base=0, channel_multiplier=1,
                           allow_small_or_imprecise_dtypes=True).then_inc(s["consts"], 1)

            pool.dma_start(relin[:], rel_bias[0]).then_inc(s["rel_in"], 16)
            with nc.allow_non_contiguous_dma("conv taps, channel-major"):
                for j in range(CW):
                    pool.dma_start(convw[:, j, :], conv_w[0, j].rearrange("(m p) -> p m", p=P)
                                   ).then_inc(s["conv_in"], 16)
                pool.dma_start(convw[:, CW, :], conv_b[0].rearrange("(m p) -> p m", p=P)
                               ).then_inc(s["conv_in"], 16)
                pool.dma_start(wr[:, :, 0:G], w_group[0].rearrange("(k p) g -> p k g", p=P)
                               ).then_inc(s["wr_in"], 16)
                pool.dma_start(wr[:, :, G:NLOG], w_expert[0].rearrange("(k p) g -> p k g", p=P)
                               ).then_inc(s["wr_in"], 16)
            vec_all(pool, br[:, 0:G], b_group, G, s["wr_in"])
            vec_all(pool, br[:, G:NLOG], b_expert, E, s["wr_in"])

            for t in range(2):
                pool.dma_start(xt[:, t, :], x_prompt[0, t * P:(t + 1) * P, :]).then_inc(s[f"x_in{t}"], 16)
            for t in range(2, NT):
                pool.wait_ge(s["n1_h"], t - 1)
                src = x_prompt[0, t * P:(t + 1) * P, :] if t < NPT else x_sample.rearrange("s t d -> (s t) d")
                pool.dma_start(xt[:, t % 2, :], src).then_inc(s[f"x_in{t % 2}"], 16)

            pool.wait_ge(s["rel_sb"], 2)
            pool.dma_start(relrow_d, relrow[:].unsqueeze(1).to_broadcast([H, P, P - 1 + BAND])
                           ).then_inc(s["rel_out"], 16)
            pool.wait_ge(s["rel_out"], 16)
            pool.wait_ge(s["n1_h"], NT)
            pool.wait_ge(s["n1_tr"], NT)
            RW = P - 1 + BAND
            for r in range(2):
                pool.wait_ge(s[f"mod_out{r}"], 8 * NADA)

            def head_bias(h):
                pool.dma_start(bias[:, h, :], bass.AP(relrow_d.tensor, h * P * RW + P - 1, [[RW - 1, P], [1, BAND]])
                               ).then_inc(s["bias_in"], 16)

            for h in range(6):
                head_bias(h)

            nc.gpsimd.memset(zrow[:], 0.0).then_inc(s["zrow_ok"], 1)
            pool.wait_ge(s["zrow_ok"], 1)
            y_rows = y_d.rearrange("(p b) (j c) -> p b j c", b=NBLK, c=256)
            with pool.Fori(E, NBLK) as b:
                for j in range(D // 256):
                    pool.dma_start(y_rows[:, bass.ds(b, 1), j, :].rearrange("p b c -> p (b c)"), zrow[:]
                                   ).then_inc(s["y_zeroed"], 16)

            for i in range(5):
                pool.wait_ge(s["gev_kout"], i + 1)
                dst = (new_k_prompt[0, 0, i * P:(i + 1) * P].rearrange("t h d -> t (h d)") if i < 4
                       else new_k_sample[0].rearrange("s t h d -> (s t) (h d)"))
                pool.dma_start(dst, kk[:, i % 2, :]).then_inc(s["kk_out"], 16)
                pool.wait_ge(s["kk_out"], 16 * (i + 1))
            head_bias(6)
            head_bias(7)
            pool.wait_ge(s["gev_v"], NT)
            pool.dma_start(new_v_prompt[0, 0].rearrange("(i p) h d -> p i (h d)", p=P), v[:, NPT - 4:NPT, :]
                           ).then_inc(s["v_out"], 16)
            pool.dma_start(new_v_sample[0].rearrange("s t h d -> (s t) (h d)"), v[:, NPT, :]
                           ).then_inc(s["v_out"], 16)

            pool.wait_ge(s["y_zeroed"], 16 * OVF * (D // 256))
            nc.gpsimd.memset(qz[:], 0.0).then_inc(s["zrow_ok"], 1)
            pool.wait_ge(s["zrow_ok"], 2)
            for pair in range(HP * NPT):
                hp, i = pair // NPT, pair % NPT
                wait(pool, s["s_scores"], 2 * pair - 2)
                for h_ in range(2):
                    rows = slice(HD * h_, HD * h_ + HD)
                    nc.gpsimd.tensor_copy(qz[rows, pair % 2, h_, :], qT[rows, hp, i * P:(i + 1) * P]
                                          ).then_inc(s["qz_ok"], 1)

            pool.wait_ge(s["s_attc"], HP * NPT)
            pool.wait_ge(s["s_ptc"], H * NPT)
            for h in range(H):
                pool.dma_start(sbias[h * DEC:(h + 1) * DEC, :],
                               bass.AP(relrow_d.tensor, h * P * RW + P - 1, [[RW - 1, DEC], [1, NK]])
                               ).then_inc(s["sb_in"], 16)

            pool.wait_ge(s["ks_at"], H * SEQS)
            pool.dma_start(st_in[:], state_conv[0].rearrange("s j c -> (s j) c")).then_inc(s["prev_in"], 16)
            pool.wait_ge(s["newc_sb"], 1)
            pool.dma_start(new_conv_sample[0].rearrange("s j c -> (s j) c"), newc[0:16, :]
                           ).then_inc(s["conv_out"], 16)
            pool.dma_start(new_conv_prompt[0, 0], newc[16:18, :]).then_inc(s["conv_out"], 16)

            for i in range(24):
                f, (c0, cn) = i // 3, TOKCH[i % 3]
                pool.wait_ge(s["g_done"], i + 1)
                pool.dma_start(mix_d[c0 // P:(c0 + cn) // P, :, f, :].rearrange("t p c -> p t c"),
                               mixc[:, 0:cn].rearrange("p (t c) -> p t c", c=P)).then_inc(s["mix_out"], 16)

            pool.wait_ge(s["g_ready"], 4 * 24)
            for t in range(NT):
                wait(pool, s["x1_done"], t - 1)
                src = x_prompt[0, t * P:(t + 1) * P, :] if t < NPT else x_sample.rearrange("s t d -> (s t) d")
                pool.dma_start(xr[:, t % 2, :], src).then_inc(s[f"xr_in{t % 2}"], 16)
                if t >= 1:
                    pool.wait_ge(s["n2_h"], t)
                    pool.dma_start(h2_d[(t - 1) * P:t * P, :], h2[:, (t - 1) % 2, :]
                                   ).then_inc(s[f"h2_out{(t - 1) % 2}"], 16)
            pool.wait_ge(s["n2_h"], NT)
            pool.dma_start(h2_d[(NT - 1) * P:, :], h2[:, (NT - 1) % 2, :]).then_inc(s["h2_out0"], 16)

            link(nc.gpsimd.iota(tieb[:], [[-1, 64]], base=64, channel_multiplier=0,
                                allow_small_or_imprecise_dtypes=True))
            link(nc.gpsimd.iota(eidx[:], [[1, E]], base=0, channel_multiplier=0,
                                allow_small_or_imprecise_dtypes=True))
            link(nc.gpsimd.iota(oidx[:], [[1, OVF]], base=0, channel_multiplier=0,
                                allow_small_or_imprecise_dtypes=True))
            link(nc.gpsimd.iota(rowi[:], [[1, P]], base=0, channel_multiplier=0,
                                allow_small_or_imprecise_dtypes=True))
            nc.gpsimd.iota(blki[:], [[1, NBLK]], base=0, channel_multiplier=0,
                           allow_small_or_imprecise_dtypes=True).then_inc(s["rconst"], 1)

            pool.wait_ge(s["route_done"], 1)
            pool.wait_ge(s["h2_out0"], 16 * 5)
            pool.wait_ge(s["h2_out1"], 16 * 4)
            pool.wait_ge(s["n2_log"], NT)

            def gather(e, r):
                wait(pool, s["xg_tr"], e - 1)
                col = table[:, e:e + 1] if isinstance(e, int) else table[:, bass.ds(e, 1)]
                nc.gpsimd.tensor_copy(idx[:, r:r + 1], col).then_inc(s["idxc"], 1)
                pool.wait_ge(s["idxc"], e + 1)
                pool.sem_inc(s["gathers"], 1)
                pool.indirect_dma_start(out=xg[:, r, :], out_offset=None, in_=h2_d,
                                        in_offset=bass.IndirectOffsetOnAxis(ap=idx[:, r:r + 1], axis=0)
                                        ).then_inc(s[f"xg_in{r}"], 16)

            gather(0, 0)
            gather(1, 1)
            with pool.Fori(1, E // 2) as i:
                gather(i * 2, 0)
                gather(i * 2 + 1, 1)
            pool.wait_ge(s["routed"], 1)
            pool.wait_ge(s["y_zeroed"], 16 * OVF * (D // 256))
            n_ov = pool.value_load(eids[0:1, OVF:OVF + 1], min_val=0, max_val=OVF)
            pool.wait_ge(s["xg_tr"], E)
            with pool.If(n_ov > 0):
                with pool.Fori(0, OVF) as o:
                    with pool.If(o < n_ov):
                        nc.gpsimd.tensor_copy(idx[:, 0:1], table[:, bass.ds(o + E, 1)]).then_inc(s["o_idx"], 1)
                        pool.wait_ge(s["o_idx"], o + 1)
                        pool.sem_inc(s["gathers"], 1)
                        pool.indirect_dma_start(out=xg[:, 0, :], out_offset=None, in_=h2_d,
                                                in_offset=bass.IndirectOffsetOnAxis(ap=idx[:, 0:1], axis=0)
                                                ).then_inc(s["o_xg"], 16)
                        pool.wait_ge(s["o_out"], (o + 1) * 16)

            pool.wait_ge(s["d_used"], 2 * E)
            for r in range(2):
                pool.wait_ge(s[f"y_out{r}"], 16 * (E // 2))
            for t in range(NT):
                wait(pool, s[f"ya_in{t % 4}"], 32 * (t // 4))
                for k, buf in enumerate((ya, yb)):
                    pool.indirect_dma_start(out=buf[:, t, :], out_offset=None, in_=y_d,
                                            in_offset=bass.IndirectOffsetOnAxis(ap=dest[:, k, t:t + 1], axis=0)
                                            ).then_inc(s[f"ya_in{t % 4}"], 16)

        @block.scalar
        def _(act):
            vec_all(act, g1[:], norm1_g, D, s["mods1"])
            act.wait_ge(s["c_in"], 32)
            nc.scalar.activation(c_sb[:], c_sb[:], ACT.Silu).then_inc(s["c_silu"], 1)

            def modulation_out(u):
                act.wait_ge(s["mod_sb"], u + 1)
                act.dma_start(mod_d[:, u * 512:(u + 1) * 512], modc[:, u % 2, :]
                              ).then_inc(s[f"mod_out{u % 2}"], 16)

            for u in range(4):
                modulation_out(u)
            act.wait_ge(s["consts"], 1)

            def square_root(t):
                r = t % 2
                act.wait_ge(s[f"x_in{r}"], 16 * (t // 2 + 1))
                wait(act, s["n1_tr"], t - 1)
                nc.scalar.activation(ht[:, r, :], xt[:, r, :], ACT.Square, accum_out=sumsq[:, 0, t:t + 1]
                                     ).then_inc(s["n1_sq"], 1)
                act.wait_ge(s["n1_sq"], t + 1)
                nc.scalar.activation(sumsq[:, 1, t:t + 1], sumsq[:, 0, t:t + 1], ACT.Sqrt, scale=1.0 / D,
                                     bias=eps[:, 0:1]).then_inc(s["n1_rt"], 1)

            square_root(0)
            for t in range(NT):
                if t + 1 < NT:
                    square_root(t + 1)
                act.wait_ge(s["n1_tr"], t + 1)
                b = 2 * (t % 2)
                nc.scalar.copy(hTh[:, :, t * P:(t + 1) * P], bank(b, 2).rearrange("p (k c) -> p k c", k=KT)
                               ).then_inc(s["n1_evac"], 1)
                if 4 + t < NADA:
                    modulation_out(4 + t)

            highs = [0]

            def weights_high_to(n):
                for u in range(highs[0], min(n, NU)):
                    act.wait_ge(*unit_in(u))
                    sl = slot_of(u)
                    nc.scalar.copy(ring_r[:, sl, 0], ring_f[:, sl, 1]).then_inc(s["w_hi"], 1)
                highs[0] = max(highs[0], min(n, NU))

            weights_high_to(2)
            act.wait_ge(s["rel_out"], 16)
            for r in range(2):
                act.wait_ge(s[f"mod_out{r}"], 8 * NADA)
            g = 0
            for what in range(2):
                for m in range(HP):
                    for c0, cn in TOKCH:
                        if c0 == 0:
                            weights_high_to(4 * what + m + 3)
                        act.wait_ge(s["gemm"], g + 1)
                        src = ps[:, 4 + g % 4, 0:cn]
                        if what == 0:
                            nc.scalar.mul(qT[:, m, c0:c0 + cn], src, HD ** -0.5).then_inc(s["gev_qk"], 1)
                        else:
                            for t0, tn, sample in parts(c0, cn):
                                dst = kTs[:, m, t0 - NP_TOK:t0 - NP_TOK + tn] if sample else kT[:, m, t0:t0 + tn]
                                nc.scalar.copy(dst, src[:, t0 - c0:t0 - c0 + tn]).then_inc(s["gev_qk"], 1)
                        g += 1
            weights_high_to(UV + 4)
            for i in range(5):
                act.wait_ge(s["gemm"], g + 1)
                if i >= 2:
                    act.wait_ge(s["kk_out"], 16 * (i - 1))
                nc.scalar.copy(kk[:, i % 2, :], ps[:, 4 + g % 4, :]).then_inc(s["gev_kout"], 1)
                g += 1
            for t in range(NT):
                act.wait_ge(s["gemm"], g + 1)
                nc.scalar.copy(v[:, t, :], ps[:, 4 + g % 4, :]).then_inc(s["gev_v"], 1)
                g += 1

            NA = H * NPT

            def exp_rows(a):
                act.wait_ge(s["s_sb"], a + 1)
                wait(act, s["s_pt"], a - 1)
                c0 = P * (4 - min(a // 2 % NPT, 4))
                nc.scalar.activation(Pr[:, a % 2, c0:BAND], S[:, a % 2, c0:BAND], ACT.Exp,
                                     bias=negmax[:, a:a + 1], accum_out=rowsum[:, a:a + 1]
                                     ).then_inc(s["s_p"], 1)

            def prob_cols(a):
                act.wait_ge(s["s_pt"], a + 1)
                wait(act, s["s_pv"], a - 1)
                j0 = 4 - min(a // 2 % NPT, 4)
                nc.scalar.copy(PT[:, a % 2, j0:5, :],
                               bank(4, 2)[:, j0 * P:BAND].rearrange("p (j c) -> p j c", c=P)
                               ).then_inc(s["s_ptc"], 1)

            exp_rows(0)
            for a in range(NA):
                if a + 1 < NA:
                    exp_rows(a + 1)
                prob_cols(a)
                if a in (20, 40):
                    weights_high_to(UCC + a // 20 * 2)

            def old_keys_half(q):
                act.wait_ge(s["k_tr"], q + 1)
                wait(act, s["ks_sc"], q)
                nc.scalar.copy(kcT[:, 0:2, :], bank(0, 2).rearrange("p (m c) -> p m c", m=2)
                               ).then_inc(s["k_trc"], 1)

            old_keys_half(0)
            for q in range(SEQS):
                act.wait_ge(s["ks_sb"], q + 1)
                wait(act, s["ks_pt"], q)
                nc.scalar.activation(Ps[:], Ss[:], ACT.Exp, bias=negmax[:, 64 + q:65 + q],
                                     accum_out=rowsum[:, 64 + q:65 + q]).then_inc(s["ks_p"], 1)
                if q + 1 < SEQS:
                    old_keys_half(q + 1)
                act.wait_ge(s["ks_pt"], q + 1)
                wait(act, s["ks_pv"], q)
                nc.scalar.copy(PTs[:, 0:4, :], ps[:, 6, :].rearrange("p (j c) -> p j c", c=P)
                               ).then_inc(s["ks_ptc"], 1)
                nc.scalar.copy(PTs[0:DEC, 4, :], ps[0:DEC, 5, P:2 * P]).then_inc(s["ks_ptc"], 1)

            g0 = g
            for m in range(HP):
                weights_high_to(UCC + m + 3)
                for c0, cn in TOKCH:
                    act.wait_ge(s["gemm"], g + 1)
                    for t0, tn, sample in parts(c0, cn):
                        nc.scalar.copy(*u_part(m, c0, t0, tn, sample, g)).then_inc(s["gev_conv"], 1)
                    g += 1

            for m in range(4):
                act.wait_ge(s["gemm"], g + 3 * m + 1)
                weights_high_to(UCV + m + 3)
            g += 12 + 2
            act.wait_ge(s["conv_last"], 1)
            act.wait_ge(s["newc_sb"], 1)
            nc.scalar.copy(atth[:], qT[:]).then_inc(s["b_hi"], 1)
            for m in range(HP):
                act.wait_ge(s["gemm"], g + 3 * m + 1)
                weights_high_to(UCB + m + 3)
                act.wait_ge(s["cu_done"], 16 + 3 * (m + 1))
                nc.scalar.copy(Yh[:, m, :], Y[:, m, :]).then_inc(s["b_hi"], 1)

            act.wait_ge(s["conv_out"], 32)
            for i in range(24):
                cn = TOKCH[i % 3][1]
                if i % 3 == 0:
                    weights_high_to(UGATE + i + 3)
                for k, sb_ in ((0, sgA), (2, sgB)):
                    act.wait_ge(s["g_ready"], 4 * i + k + 1)
                    wait(act, s["g_done"], i)
                    nc.scalar.activation(sb_[:, 0:cn], ps[:, 4 * (i % 2) + k, 0:cn], ACT.Sigmoid
                                         ).then_inc(s["g_sig"], 1)
                    if k == 0 and i % 3 == 0:
                        weights_high_to(UGATE + i + 6)

            weights_high_to(NU)

            def mixture_high(t):
                act.wait_ge(s[f"mix_in{t % 2}"], 16 * (t // 2 + 1))
                nc.scalar.copy(mixh[:, t % 2], mixr[:, t % 2]).then_inc(s["w_hi"], 1)

            mixture_high(0)
            mixture_high(1)

            for t in range(NT):
                act.wait_ge(s["x1_done"], t + 1)
                if t + 2 < NT:
                    mixture_high(t + 2)
                nc.scalar.activation(sq[:], x1[:, t, :], ACT.Square, accum_out=sumsq[:, 0, t:t + 1]
                                     ).then_inc(s["n2_sq"], 1)
                act.wait_ge(s["n2_sq"], t + 1)
                nc.scalar.activation(sumsq[:, 1, t:t + 1], sumsq[:, 0, t:t + 1], ACT.Sqrt, scale=1.0 / D,
                                     bias=eps[:, 0:1]).then_inc(s["n2_rt"], 1)
                act.wait_ge(s["n2_tr"], t + 1)
                wait(act, s["n2_log"], t)
                nc.scalar.copy(h2T[:], bank(4, 2)).then_inc(s["n2_evac"], 1)

            act.wait_ge(s["picks"], 1)
            nc.scalar.activation(gmask[:], lg[:], ACT.Exp).then_inc(s["picks"], 1)
            act.wait_ge(s["picks"], 3)
            nc.scalar.activation(sm[:, 3, :], sm[:, 2, :], ACT.Exp).then_inc(s["picks"], 1)

            def weights_high(e, js):
                for j in js:
                    act.wait_ge(landed[j], LAST_IN[j] + (e + 1) * 16)
                    nc.scalar.copy(mhi[j][:], mraw[j][:]).then_inc(s["gu_hi" if j < 4 else "d_hi"], 1)

            def rows_high(e, r):
                act.wait_ge(s["xg_tr"], e + 1)
                wait(act, s["gu_used"], e * 4 - 4)
                nc.scalar.copy(xTh[:, r, :], bank(0, 2)).then_inc(s["xTh_ok"], 1)

            def silu(e):
                act.wait_ge(s["gu_used"], e * 4 + 2)
                wait(act, s["h_ok"], e)
                nc.scalar.activation(sg[:], bank(2), ACT.Silu).then_inc(s["silu_ok"], 1)

            def hidden_high(e):
                act.wait_ge(s["h_tr"], e + 1)
                wait(act, s["d_used"], e * 2)
                nc.scalar.copy(hhTh[:], bank(4)).then_inc(s["hTh_ok"], 1)

            def result(e, r, stored=None):
                act.wait_ge(s["d_used"], e * 2 + 2)
                wait(act, s[f"y_out{r}"], stored)
                nc.scalar.copy(yy[:, r, :], bank(5, 2)).then_inc(s["y_ok"], 1)
                act.wait_ge(s["y_ok"], e + 1)
                dst = y_d.rearrange("(p b) d -> p b d", b=NBLK)
                dst = dst[:, e, :] if isinstance(e, int) else dst[:, bass.ds(e, 1), :].rearrange("p b d -> p (b d)")
                act.dma_start(dst, yy[:, r, :]).then_inc(s[f"y_out{r}"], 16)

            GU0, GU1, DN = (0, 1), (2, 3), (4, 5)
            weights_high(0, GU0 + GU1)
            rows_high(0, 0)

            def act_step(e, r, stored):
                silu(e)
                rows_high(e + 1, 1 - r)
                weights_high(e + 1, GU0)
                if stored is not None:
                    result(e - 1, 1 - r, stored)
                hidden_high(e)
                weights_high(e + 1, GU1)
                weights_high(e, DN)

            act_step(0, 0, None)
            act_step(1, 1, 0)
            act_step(2, 0, 0)
            act_step(3, 1, 16)
            with act.Fori(2, E // 2 - 1) as i:
                act_step(i * 2, 0, (i - 1) * 16)
                act_step(i * 2 + 1, 1, i * 16)
            act_step(E - 2, 0, 16 * (E // 2 - 2))
            silu(E - 1)
            result(E - 2, 0, 16 * (E // 2 - 1))
            hidden_high(E - 1)
            weights_high(E - 1, DN)
            result(E - 1, 1, 16 * (E // 2 - 1))
            act.wait_ge(s["routed"], 1)
            act.wait_ge(s["y_zeroed"], 16 * OVF * (D // 256))
            n_ov = act.value_load(eids[0:1, OVF:OVF + 1], min_val=0, max_val=OVF)
            with act.If(n_ov > 0):
                with act.Fori(0, OVF) as o:
                    with act.If(o < n_ov):
                        act.wait_ge(s["o_w"], (o + 1) * 96)
                        for j in range(6):
                            nc.scalar.copy(mhi[j][:], mraw[j][:]).then_inc(s["o_act"], 1)
                        act.wait_ge(s["o_pe"], o * 4 + 1)
                        nc.scalar.copy(xTh[:, 0, :], bank(0, 2)).then_inc(s["o_act"], 1)
                        act.wait_ge(s["o_pe"], o * 4 + 2)
                        nc.scalar.activation(sg[:], bank(2), ACT.Silu).then_inc(s["o_act"], 1)
                        act.wait_ge(s["o_pe"], o * 4 + 4)
                        nc.scalar.copy(hhTh[:], bank(4)).then_inc(s["o_act"], 1)
                        act.wait_ge(s["o_dve"], o * 10 + 10)
                        dst = y_d.rearrange("(p b) d -> p b d", b=NBLK)[:, bass.ds(o + E, 1), :]
                        act.dma_start(dst.rearrange("p b d -> p (b d)"), yy[:, 0, :]).then_inc(s["o_out"], 16)

            def weigh(t):
                act.wait_ge(s[f"ya_in{t % 4}"], 32 * (t // 4 + 1))
                nc.scalar.activation(ya[:, t, :], ya[:, t, :], ACT.Copy, scale=wts[:, 0, t:t + 1]
                                     ).then_inc(s["f_w"], 1)

            weigh(0)
            weigh(1)
            for t in range(NT):
                if t + 2 < NT:
                    weigh(t + 2)
                act.wait_ge(s["f_sq"], 2 * t + 1)
                nc.scalar.activation(yq[:], x1[:, t, :], ACT.Square, accum_out=sumsq[:, 2, t:t + 1]
                                     ).then_inc(s["f_sq"], 1)
                act.wait_ge(s["f_sq"], 2 * t + 2)
                nc.scalar.activation(sumsq[:, 3, t:t + 1], sumsq[:, 2, t:t + 1], ACT.Sqrt, scale=1.0 / D,
                                     bias=eps[:, 0:1]).then_inc(s["f_rt"], 1)

        @block.vector
        def _(dve):
            link = Link(dve, s["link_dve"])
            V = nc.vector

            dve.wait_ge(s["cT_ps"], 1)
            V.tensor_copy(cT[:], ps[:, 6, 0:KT * (SEQS + 1)].rearrange("p (k s) -> p k s", k=KT)
                          ).then_inc(s["cT_sb"], 1)

            dve.wait_ge(s["badain"], 32)

            def modulation(u):
                dve.wait_ge(s["unit_used"], u + 1)
                wait(dve, s[f"mod_out{u % 2}"], 16 * (u // 2))
                bada, b0 = (bada0, u) if u < 4 else (bada1, u - 4)
                V.tensor_tensor(modc[:, u % 2, :], ps[0:SEQS + 1, 4 + u % 2, :], bada[:, b0 * 512:(b0 + 1) * 512],
                                ALU.add).then_inc(s["mod_sb"], 1)

            for u in range(4):
                modulation(u)
            dve.wait_ge(s["rel_in"], 16)
            link(V.memset(relrow[:, 0:4 * P], 0.0))
            V.tensor_scalar(relrow[:, 0:4 * P], relrow[:, 0:4 * P], relin[:, NREL - 1:NREL], None,
                            ALU.add).then_inc(s["rel_sb"], 1)
            n = P - 1 + BAND - 4 * P
            V.tensor_copy(relrow[:, 4 * P:], bass.AP(relin, n, [[NREL, H], [-1, n]])).then_inc(s["rel_sb"], 1)

            dve.wait_ge(s["mods1"], 16 * (1 + 2 * 9))
            for r in range(2):
                link(V.scalar_tensor_tensor(out=scale1[:, r, :], in0=scale1[:, r, :], scalar=1.0, in1=g1[:],
                                            op0=ALU.add, op1=ALU.mult))

            def rows_rest(t):
                dve.wait_ge(s["n1_evac"], t + 1)
                V.tensor_tensor(hTl[:, :, t * P:(t + 1) * P], bank(2 * (t % 2), 2).rearrange("p (k c) -> p k c", k=KT),
                                hTh[:, :, t * P:(t + 1) * P].bitcast(F32), ALU.subtract).then_inc(s["n1_lo"], 1)

            for t in range(NT):
                r, side = t % 2, int(t == NPT)
                dve.wait_ge(s["n1_rt"], t + 1)
                link(V.reciprocal(sumsq[:, 1, t:t + 1], sumsq[:, 1, t:t + 1]))
                link(V.scalar_tensor_tensor(out=ht[:, r, :], in0=xt[:, r, :], scalar=sumsq[:, 1, t:t + 1],
                                            in1=scale1[:, side, :], op0=ALU.mult, op1=ALU.mult))
                V.tensor_tensor(ht[:, r, :], ht[:, r, :], shift1[:, side, :], ALU.add).then_inc(s["n1_h"], 1)
                if 4 + t < NADA:
                    modulation(4 + t)
                if t == 1:
                    dve.wait_ge(s["mod_sb"], 4)
                if t >= 1:
                    rows_rest(t - 1)
            rows_rest(NT - 1)

            def split_rest(out, value, high, sig):
                V.tensor_tensor(out, value, high.bitcast(F32), ALU.subtract).then_inc(sig, 1)

            rests = [0]

            def weights_rest_to(n):
                for u in range(rests[0], min(n, NU)):
                    dve.wait_ge(s["w_hi"], u + 1)
                    sl = slot_of(u)
                    split_rest(ring_r[:, sl, 1], ring_f[:, sl, 1], ring_r[:, sl, 0], s["w_lo"])
                rests[0] = max(rests[0], min(n, NU))

            weights_rest_to(UV + 4)

            dve.wait_ge(s["bias_in"], 16 * H)
            V.memset(bias[0:HD, :, BAND - 64:BAND], NEG).then_inc(s["bias_ok"], 1)
            V.memset(bias[HD:P, :, 0:64], NEG).then_inc(s["bias_ok"], 1)
            dve.wait_ge(s["bias_ok"], 2)
            NA = H * NPT

            def masked(a):
                i, h = a // 2 % NPT, 2 * (a // 2 // NPT) + a % 2
                c0 = P * (4 - min(i, 4))
                dve.wait_ge(s["s_scores"], a + 1)
                wait(dve, s["s_p"], a - 1)
                link(V.tensor_tensor_reduce(out=S[:, a % 2, c0:BAND], in0=bank(2 * (a % 2), 2)[:, c0:BAND],
                                            in1=bias[:, h, c0:BAND], scale=1.0, scalar=-3e38,
                                            op0=ALU.add, op1=ALU.max, accum_out=rowmax[:, a:a + 1]))
                V.tensor_scalar(negmax[:, a:a + 1], rowmax[:, a:a + 1], -1.0, None, ALU.mult
                                ).then_inc(s["s_sb"], 1)

            def normed(pair):
                a = 2 * pair
                dve.wait_ge(s["s_pv"], a + 2)
                wait(dve, s["s_att"], pair - 1)
                link(V.reciprocal(rinv[:, a:a + 2], rowsum[:, a:a + 2]))
                V.tensor_tensor(attt[:, pair % 2, :].rearrange("p (h d) -> p h d", h=2),
                                ps[:, 6, 0:P].rearrange("p (h d) -> p h d", h=2),
                                rinv[:, a:a + 2].unsqueeze(2).to_broadcast([P, 2, HD]), ALU.mult
                                ).then_inc(s["s_at"], 1)

            def att_cols(pair):
                i, hp = pair % NPT, pair // NPT
                dve.wait_ge(s["s_att"], pair + 1)
                V.tensor_copy(qT[:, hp, i * P:(i + 1) * P], ps[:, 7, 0:P]).then_inc(s["s_attc"], 1)

            masked(0)
            masked(1)
            for a in range(NA):
                if a + 2 < NA:
                    masked(a + 2)
                if a % 2 == 0 and a >= 2:
                    normed(a // 2 - 1)
                if a % 2 == 1 and a >= 3:
                    att_cols(a // 2 - 1)
                if a in (24, 44):
                    weights_rest_to(UCC + (a - 4) // 20 * 2)
            normed(NA // 2 - 1)
            att_cols(NA // 2 - 1)

            link(V.memset(qblk[:, :, :], 0.0))
            dve.wait_ge(s["sb_in"], 16 * H)

            def queries(q):
                wait(dve, s["ks_sc"], q - 1)
                qv = qblk[:, q % 2, :].rearrange("p (a b) -> p a b", b=160)
                V.tensor_copy(qv[0:HD, 0:HP, 0:DEC], qT[0:HD, :, NP_TOK + q * DEC:NP_TOK + (q + 1) * DEC]).then_inc(s["qb"], 1)
                V.tensor_copy(qv[HD:P, 0:HP, DEC:2 * DEC], qT[HD:P, :, NP_TOK + q * DEC:NP_TOK + (q + 1) * DEC]
                              ).then_inc(s["qb"], 1)

            def old_keys_rest(q):
                dve.wait_ge(s["k_tr"], q + 1)
                wait(dve, s["ks_sc"], q)
                V.tensor_copy(kcT[:, 2:4, :], bank(2, 2).rearrange("p (m c) -> p m c", m=2)
                              ).then_inc(s["k_trc"], 1)

            def sample_cols(q):
                dve.wait_ge(s["ks_att"], q + 1)
                for h in range(H):
                    m, rows = h // 2, slice(HD * (h % 2), HD * (h % 2) + HD)
                    c = m * P + h * DEC
                    V.tensor_copy(qT[rows, m, NP_TOK + q * DEC:NP_TOK + (q + 1) * DEC], ps[rows, 6, c:c + DEC]
                                  ).then_inc(s["ks_at"], 1)

            queries(0)
            old_keys_rest(0)
            for q in range(SEQS):
                if q + 1 < SEQS:
                    queries(q + 1)
                dve.wait_ge(s["ks_sc"], q + 1)
                wait(dve, s["ks_p"], q)
                link(V.tensor_tensor_reduce(out=Ss[:], in0=bank(4, 2)[:, 0:NK], in1=sbias[:], scale=1.0,
                                            scalar=-3e38, op0=ALU.add, op1=ALU.max,
                                            accum_out=rowmax[:, 64 + q:65 + q]))
                V.tensor_scalar(negmax[:, 64 + q:65 + q], rowmax[:, 64 + q:65 + q], -1.0, None, ALU.mult
                                ).then_inc(s["ks_sb"], 1)
                if q >= 1:
                    sample_cols(q - 1)
                dve.wait_ge(s["ks_p"], q + 1)
                V.reciprocal(rinv[:, 64 + q:65 + q], rowsum[:, 64 + q:65 + q]).then_inc(s["link_dve"], 1)
                link.n += 1
                if q + 1 < SEQS:
                    old_keys_rest(q + 1)
                dve.wait_ge(s["ks_pv"], q + 1)
                wait(dve, s["ks_att"], q)
                dve.wait_ge(s["link_dve"], link.n)
                V.tensor_scalar(atts[:], bank(7), rinv[:, 64 + q:65 + q], None, ALU.mult
                                ).then_inc(s["ks_ev"], 1)
            sample_cols(SEQS - 1)

            g = 12 + 12 + 5 + NT
            link(V.memset(U[:, :, 0:2], 0.0))
            for m in range(HP):
                dve.wait_ge(s["gemm"], g + 3 * m + 1)
                weights_rest_to(UCC + m + 3)
            g += 12
            for m in range(HP):
                weights_rest_to(UCV + m + 3)
                for n, (c0, cn) in enumerate(TOKCH):
                    dve.wait_ge(s["gemm"], g + 1)
                    for t0, tn, sample in parts(c0, cn):
                        dve.wait_ge(s["gev_conv"], 4 * m + n + 1 + sample)
                        dst, src = u_part(m, c0, t0, tn, sample, g)
                        V.tensor_tensor(dst, dst, src, ALU.mult).then_inc(s["cu_done"], 1)
                    g += 1
            dve.wait_ge(s["cu_done"], 16)
            dve.wait_ge(s["gemm"], g + 1)
            V.tensor_copy(Us[:, :, :, 0:2],
                          ps[:, 4 + g % 4, 0:HP * 16].rearrange("p (m q j) -> p m q j", m=HP, j=2)
                          ).then_inc(s["gev_prev"], 1)
            g += 1
            link(V.tensor_copy(lastu[:, :, 0:16].rearrange("p m (q j) -> p m q j", j=2), Us[:, :, :, DEC:]))
            V.tensor_copy(lastu[:, :, 16:18], U[:, :, NP_TOK:]).then_inc(s["conv_last"], 1)
            dve.wait_ge(s["gev_prev"], 1)
            dve.wait_ge(s["conv_in"], 16 * (CW + 1))
            weights_rest_to(UCB + 2)
            for m in range(HP):
                yp, us = Y[:, m, 0:NP_TOK], Y[:, m, NP_TOK:].rearrange("p (q t) -> p q t", t=DEC)
                w = [convw[:, j, m:m + 1] for j in range(CW + 1)]
                link(V.tensor_scalar(yp, U[:, m, 0:NP_TOK], w[0], w[CW], ALU.mult, ALU.add))
                link(V.tensor_scalar(us, Us[:, m, :, 0:DEC], w[0], w[CW], ALU.mult, ALU.add))
                for j in (1, 2):
                    link(V.scalar_tensor_tensor(out=yp, in0=U[:, m, j:j + NP_TOK], scalar=w[j], in1=yp,
                                                op0=ALU.mult, op1=ALU.add))
                    link(V.scalar_tensor_tensor(out=us, in0=Us[:, m, :, j:j + DEC], scalar=w[j], in1=us,
                                                op0=ALU.mult, op1=ALU.add))
            dve.wait_ge(s["gemm"], g + 1)
            V.tensor_copy(newc[:], ps[0:18, 4 + g % 4, :]).then_inc(s["newc_sb"], 1)
            g += 1
            for m in range(HP):
                for c0, cn in TOKCH:
                    dve.wait_ge(s["gemm"], g + 1)
                    V.tensor_tensor(Y[:, m, c0:c0 + cn], Y[:, m, c0:c0 + cn], ps[:, 4 + g % 4, 0:cn], ALU.mult
                                    ).then_inc(s["cu_done"], 1)
                    if c0 == 0:
                        weights_rest_to(UCB + m + 3)
                    g += 1
                if m == 0:
                    dve.wait_ge(s["b_hi"], 1)
                    split_rest(attl[:], qT[:], atth[:], s["b_lo"])
                if m >= 1:
                    dve.wait_ge(s["b_hi"], m + 1)
                    split_rest(Yl[:, m - 1, :], Y[:, m - 1, :], Yh[:, m - 1, :], s["b_lo"])
            dve.wait_ge(s["b_hi"], HP + 1)
            split_rest(Yl[:, HP - 1, :], Y[:, HP - 1, :], Yh[:, HP - 1, :], s["b_lo"])

            for i in range(24):
                f, (c0, cn) = i // 3, TOKCH[i % 3]
                b = 4 * (i % 2)
                if i % 3 == 0:
                    weights_rest_to(UGATE + i + 3)
                dve.wait_ge(s["g_ready"], 4 * i + 2)
                dve.wait_ge(s["g_sig"], 2 * i + 1)
                link(V.tensor_tensor(sgA[:, 0:cn], sgA[:, 0:cn], ps[:, b + 1, 0:cn], ALU.mult))
                if i % 3 == 0:
                    weights_rest_to(UGATE + i + 6)
                dve.wait_ge(s["g_ready"], 4 * i + 4)
                dve.wait_ge(s["g_sig"], 2 * i + 2)
                link(V.tensor_tensor(sgB[:, 0:cn], sgB[:, 0:cn], ps[:, b + 3, 0:cn], ALU.mult))
                wait(dve, s["mix_out"], 16 * i)
                V.tensor_tensor(mixc[:, 0:cn], sgA[:, 0:cn], sgB[:, 0:cn], ALU.add).then_inc(s["g_done"], 1)

            weights_rest_to(NU)

            def mixture_rest(t):
                dve.wait_ge(s["w_hi"], NU + t + 1)
                split_rest(mixl[:, t % 2], mixr[:, t % 2], mixh[:, t % 2], s["w_lo"])

            mixture_rest(0)
            mixture_rest(1)

            dve.wait_ge(s["mods2"], 16 * (1 + 3 * 9))
            for r in range(2):
                link(V.scalar_tensor_tensor(out=scale2[:, r, :], in0=scale2[:, r, :], scalar=1.0, in1=g2[:],
                                            op0=ALU.add, op1=ALU.mult))

            def residual(t):
                r, side = t % 2, int(t == NPT)
                dve.wait_ge(s["o_done"], t + 1)
                link(V.tensor_tensor(x1[:, t, :], bank(2 * r, 2), gate1[:, side, :], ALU.mult))
                dve.wait_ge(s[f"xr_in{r}"], 16 * (t // 2 + 1))
                V.tensor_tensor(x1[:, t, :], x1[:, t, :], xr[:, r, :], ALU.add).then_inc(s["x1_done"], 1)

            def log_bias(t):
                dve.wait_ge(s["n2_log"], t + 1)
                V.tensor_tensor(logits[:, t, :], ps[:, 6, 0:NLOG], br[:], ALU.add).then_inc(s["n2_lev"], 1)

            dve.wait_ge(s["wr_in"], 64)
            residual(0)
            for t in range(NT):
                r, side = t % 2, int(t == NPT)
                dve.wait_ge(s["n2_rt"], t + 1)
                dve.wait_ge(s["x1_done"], t + 1)
                link(V.reciprocal(sumsq[:, 1, t:t + 1], sumsq[:, 1, t:t + 1]))
                if t >= 2:
                    dve.wait_ge(s[f"h2_out{r}"], 16 * (t // 2))
                    dve.wait_ge(s["n2_tr"], t - 1)
                link(V.scalar_tensor_tensor(out=h2[:, r, :], in0=x1[:, t, :], scalar=sumsq[:, 1, t:t + 1],
                                            in1=scale2[:, side, :], op0=ALU.mult, op1=ALU.mult))
                V.tensor_tensor(h2[:, r, :], h2[:, r, :], shift2[:, side, :], ALU.add).then_inc(s["n2_h"], 1)
                if t + 2 < NT:
                    mixture_rest(t + 2)
                if t + 1 < NT:
                    residual(t + 1)
                log_bias(t)
            dve.wait_ge(s["n2_lev"], NT)

            dve.wait_ge(s["rconst"], 1)

            def b3(x2, n):
                return x2.unsqueeze(2).to_broadcast([P, NT, n])

            def c3(row, n):
                return row.unsqueeze(1).to_broadcast([P, NT, n])

            def first_max(out, src, mx, n, buf, m2):
                link(V.tensor_reduce(mx, src, AX.X, ALU.max))
                link(V.tensor_tensor(buf, src, b3(mx, n), ALU.is_equal))
                link(V.tensor_tensor(buf, buf, c3(tieb[:, 0:n], n), ALU.mult))
                link(V.tensor_reduce(m2, buf, AX.X, ALU.max))
                link(V.tensor_tensor(out, buf, b3(m2, n), ALU.is_equal))

            lgr, ler = logits[:, :, 0:G], logits[:, :, G:NLOG]
            gm, sc0 = sm[:, 0, :], sm[:, 1, :]
            pick_g = gmask
            first_max(pick_g[:], lgr, gm, G, lg[:], sc0)
            le4 = le[:].rearrange("p t (g e) -> p t g e", g=G)
            link(V.tensor_scalar(tmp[:, :, 0:G], pick_g[:], -NEG, NEG, ALU.mult, ALU.add))
            for gi in range(G):
                sl = slice(gi * EPG, (gi + 1) * EPG)
                link(V.tensor_tensor(le[:, :, sl], ler[:, :, sl],
                                     pick_g[:, :, gi:gi + 1].to_broadcast([P, NT, EPG]), ALU.mult))
                link(V.tensor_tensor(le[:, :, sl], le[:, :, sl],
                                     tmp[:, :, gi:gi + 1].to_broadcast([P, NT, EPG]), ALU.add))
            V.tensor_tensor(lg[:], lgr, b3(gm, G), ALU.subtract).then_inc(s["picks"], 1)
            m1, m2_ = sm[:, 4, :], sm[:, 5, :]
            first_max(o1[:], le[:], m1, E, tmp[:], sc0)
            link(V.tensor_scalar(tmp[:], o1[:], 4 * NEG, None, ALU.mult))
            link(V.tensor_tensor(le[:], le[:], tmp[:], ALU.add))
            first_max(o2[:], le[:], m2_, E, tmp[:], sc0)
            dve.wait_ge(s["picks"], 2)
            V.tensor_tensor(sm[:, 2, :], m2_, m1, ALU.subtract).then_inc(s["picks"], 1)
            link(V.tensor_reduce(sm[:, 6, :], gmask[:], AX.X, ALU.add))
            V.tensor_tensor(picked[:], o1[:], o2[:], ALU.add).then_inc(s["ranks"], 1)

            def chosen(out, values):
                for k, o in enumerate((o1, o2)):
                    link(V.tensor_tensor(tmp[:], o[:], values, ALU.mult))
                    link(V.tensor_reduce(out[:, k, :], tmp[:], AX.X, ALU.add))

            ek, rk, vk, ck, bk, wk, xk = [picks_of[:, j] for j in range(7)]
            chosen(ek, c3(eidx[:], E))
            dve.wait_ge(s["ranks"], 2)
            link(V.memset(prefix[:, 0, :], 0.0))
            tots = ps[:, 1, 0:NT * E].rearrange("p (t e) -> p t e", t=NT)
            for t in range(NT):
                link(V.tensor_tensor(prefix[:, t + 1, :] if t + 1 < NT else cnt[:], prefix[:, t, :], tots[:, t, :],
                                     ALU.add))
            link(V.tensor_tensor(rank[:], prefix[:], ps[:, 0, 0:NT * E].rearrange("p (t e) -> p t e", t=NT), ALU.add))
            link(V.tensor_scalar(ovc[:], cnt[:], float(CAP), None, ALU.is_gt))
            for j in range(2, -(-T // CAP)):
                link(V.scalar_tensor_tensor(out=ovc[:], in0=cnt[:], scalar=float(j * CAP), in1=ovc[:],
                                            op0=ALU.is_gt, op1=ALU.add))
            link(V.tensor_copy(ovi[:], ovc[:]))
            for d in (1, 2, 4, 8, 16):
                link(V.tensor_copy(ove[:], ovi[:]))
                link(V.tensor_tensor(ovi[:, d:], ove[:, d:], ove[:, 0:E - d], ALU.add))
            link(V.tensor_tensor(ove[:], ovi[:], ovc[:], ALU.subtract))
            chosen(rk, rank[:])
            chosen(vk, c3(ove[:], E))
            link(V.tensor_scalar(ck, rk, float(CAP), None, ALU.is_ge))
            for j in range(2, -(-T // CAP)):
                link(V.scalar_tensor_tensor(out=ck, in0=rk, scalar=float(j * CAP), in1=ck,
                                            op0=ALU.is_ge, op1=ALU.add))
            link(V.scalar_tensor_tensor(out=wk, in0=ck, scalar=-float(CAP), in1=rk, op0=ALU.mult, op1=ALU.add))
            link(V.tensor_tensor(bk, vk, ek, ALU.subtract))
            link(V.tensor_scalar(bk, bk, float(E - 1), None, ALU.add))
            link(V.scalar_tensor_tensor(out=bk, in0=ck, scalar=0.5, in1=bk, op0=ALU.is_ge, op1=ALU.mult))
            link(V.tensor_tensor(bk, bk, ck, ALU.add))
            link(V.tensor_tensor(bk, bk, ek, ALU.add))
            for k in range(2):
                ch = slice(k * NT, (k + 1) * NT)
                V.tensor_tensor(onerow[:, ch, :], rowi[:].unsqueeze(1).to_broadcast([P, NT, P]),
                                wk[:, k, :].unsqueeze(2).to_broadcast([P, NT, P]), ALU.is_equal
                                ).then_inc(s["onehot"], 1)
                if k == 0:
                    link(V.memset(oneblk[:].bitcast(F32), 0.0))
                link(V.tensor_tensor(oneblk[:, ch, 0:NBLK], blki[:].unsqueeze(1).to_broadcast([P, NT, NBLK]),
                                     bk[:, k, :].unsqueeze(2).to_broadcast([P, NT, NBLK]), ALU.is_equal))
                V.tensor_tensor(oneblk[:, ch, 0:NBLK], oneblk[:, ch, 0:NBLK].bitcast(F32), b3(tokid[:], NBLK),
                                ALU.mult).then_inc(s["onehot"], 1)
            link(V.scalar_tensor_tensor(out=xk, in0=wk, scalar=float(NBLK), in1=bk, op0=ALU.mult, op1=ALU.add))
            link(V.tensor_copy(dest[:], xk))
            dve.wait_ge(s["table_ps"], 1)
            V.tensor_copy(table[:], ps[:, 2, 0:NBLK]).then_inc(s["route_done"], 1)
            dve.wait_ge(s["picks"], 4)
            link(V.tensor_scalar(sm[:, 7, :], sm[:, 3, :], 1.0, None, ALU.add))
            link(V.tensor_tensor(sm[:, 7, :], sm[:, 7, :], sm[:, 6, :], ALU.mult))
            link(V.reciprocal(wts[:, 0, :], sm[:, 7, :]))
            link(V.tensor_tensor(wts[:, 1, :], wts[:, 0, :], sm[:, 3, :], ALU.mult))
            link(V.tensor_tensor(ocmp[:], ovi[:].unsqueeze(1).to_broadcast([P, OVF, E]),
                                 oidx[:].unsqueeze(2).to_broadcast([P, OVF, E]), ALU.is_le))
            link(V.tensor_reduce(ocmp2[:, 0:OVF], ocmp[:], AX.X, ALU.add))
            link(V.tensor_scalar(ocmp2[:, 0:OVF], ocmp2[:, 0:OVF], float(E - 1), None, ALU.min))
            link(V.tensor_copy(ocmp2[:, OVF:], ovi[:, E - 1:E]))
            V.tensor_copy(eids[:], ocmp2[:]).then_inc(s["routed"], 1)

            def weights_low(e, js):
                for j in js:
                    k = "gu" if j < 4 else "d"
                    dve.wait_ge(s[k + "_hi"], e * (4 if j < 4 else 2) + (j % 4 + 1))
                    split_rest(mlo[j][:], mraw[j][:], mhi[j][:], s[k + "_lo"])

            def rows_low(e, r):
                dve.wait_ge(s["xTh_ok"], e + 1)
                split_rest(xTl[:, r, :], bank(0, 2), xTh[:, r, :], s["xTl_ok"])

            def hidden(e):
                dve.wait_ge(s["gu_used"], e * 4 + 4)
                dve.wait_ge(s["silu_ok"], e + 1)
                wait(dve, s["h_tr"], e)
                V.tensor_tensor(hh[:], sg[:], bank(3), ALU.mult).then_inc(s["h_ok"], 1)

            def hidden_low(e):
                dve.wait_ge(s["hTh_ok"], e + 1)
                split_rest(hhTl[:], bank(4), hhTh[:], s["hTl_ok"])

            GU0, GU1, DN = (0, 1), (2, 3), (4, 5)

            def dve_step(e, r):
                rows_low(e + 1, 1 - r)
                hidden(e)
                weights_low(e + 1, GU0)
                hidden_low(e)
                weights_low(e + 1, GU1)
                weights_low(e, DN)

            weights_low(0, GU0 + GU1)
            rows_low(0, 0)
            dve_step(0, 0)
            dve_step(1, 1)
            with dve.Fori(1, E // 2 - 1) as i:
                dve_step(i * 2, 0)
                dve_step(i * 2 + 1, 1)
            dve_step(E - 2, 0)
            hidden(E - 1)
            hidden_low(E - 1)
            weights_low(E - 1, DN)
            for r in range(2):
                dve.wait_ge(s[f"y_out{r}"], 16 * (E // 2))
            dve.wait_ge(s["routed"], 1)
            n_ov = dve.value_load(eids[0:1, OVF:OVF + 1], min_val=0, max_val=OVF)
            with dve.If(n_ov > 0):
                with dve.Fori(0, OVF) as o:
                    with dve.If(o < n_ov):
                        dve.wait_ge(s["o_act"], o * 9 + 6)
                        for j in range(6):
                            split_rest(mlo[j][:], mraw[j][:], mhi[j][:], s["o_dve"])
                        dve.wait_ge(s["o_act"], o * 9 + 7)
                        split_rest(xTl[:, 0, :], bank(0, 2), xTh[:, 0, :], s["o_dve"])
                        dve.wait_ge(s["o_pe"], o * 4 + 3)
                        dve.wait_ge(s["o_act"], o * 9 + 8)
                        V.tensor_tensor(hh[:], sg[:], bank(3), ALU.mult).then_inc(s["o_dve"], 1)
                        dve.wait_ge(s["o_act"], o * 9 + 9)
                        split_rest(hhTl[:], bank(4), hhTh[:], s["o_dve"])
                        dve.wait_ge(s["o_dn"], o + 2)
                        V.tensor_copy(yy[:, 0, :], bank(5, 2)).then_inc(s["o_dve"], 1)

            dve.wait_ge(s["mods3"], 16 * 10)

            def combine(t):
                side = int(t == NPT)
                dve.wait_ge(s[f"ya_in{t % 4}"], 32 * (t // 4 + 1))
                dve.wait_ge(s["f_w"], t + 1)
                link(V.scalar_tensor_tensor(out=ya[:, t, :], in0=yb[:, t, :], scalar=wts[:, 1, t:t + 1],
                                            in1=ya[:, t, :], op0=ALU.mult, op1=ALU.add))
                link(V.tensor_tensor(ya[:, t, :], ya[:, t, :], gate2[:, side, :], ALU.mult))
                wait(dve, s["f_sq"], 2 * t)
                V.tensor_tensor(x1[:, t, :], x1[:, t, :], ya[:, t, :], ALU.add).then_inc(s["f_sq"], 1)

            combine(0)
            for t in range(NT):
                r = t % 2
                if t + 1 < NT:
                    combine(t + 1)
                dve.wait_ge(s["f_rt"], t + 1)
                if t >= 2:
                    dve.wait_ge(s[f"f_out{r}"], 16 * (t // 2))
                link(V.reciprocal(sumsq[:, 3, t:t + 1], sumsq[:, 3, t:t + 1]))
                V.scalar_tensor_tensor(out=yo[:, r, :], in0=x1[:, t, :], scalar=sumsq[:, 3, t:t + 1],
                                       in1=fg[:], op0=ALU.mult, op1=ALU.mult).then_inc(s["f_done"], 1)

        @block.tensor
        def _(pe):
            mm, tr = nc.tensor.matmul, nc.tensor.transpose
            pe.wait_ge(s["consts"], 1)
            pe.wait_ge(s["c_silu"], 1)
            n = SEQS + 1
            for k in range(KT):
                last = tr(ps[:, 6, k * n:(k + 1) * n], c_sb[:, k * P:(k + 1) * P], ident[0:n, 0:n])
            last.then_inc(s["cT_ps"], 1)
            pe.wait_ge(s["cT_sb"], 1)

            def modulation(u):
                pe.wait_ge(landed[u % 4], 32 * (u // 4 + 1))
                wait(pe, s["mod_sb"], u - 1)
                for k in range(KT):
                    last = mm(ps[0:n, 4 + u % 2, :], cT[:, k, :], aring[u % 4][:, k, :],
                              start=(k == 0), stop=(k == KT - 1))
                last.then_inc(s["unit_used"], 1)

            for u in range(4):
                modulation(u)
            for t in range(NT):
                r = t % 2
                if 4 + t < NADA:
                    modulation(4 + t)
                pe.wait_ge(s["n1_h"], t + 1)
                wait(pe, s["n1_lo"], t - 1)
                for k in range(KT):
                    last = tr(bank(2 * r, 2)[:, k * P:(k + 1) * P], ht[:, r, k * P:(k + 1) * P], ident[:])
                last.then_inc(s["n1_tr"], 1)
            pe.wait_ge(s["n1_lo"], NT)
            pe.wait_ge(s["mod_sb"], NADA)

            owners = []

            def group(owner, count):
                g = len(owners)
                if g >= 4:
                    pe.wait_ge(s[owners[g - 4][0]], owners[g - 4][1])
                owners.append((owner, count))
                return 4 + g % 4

            def product(out, xh, xl, wh, wl, start, stop):
                mm(out, xh, wh, start=start, stop=False)
                mm(out, xh, wl, start=False, stop=False)
                return mm(out, xl, wh, start=False, stop=stop)

            used = [0, 0]

            def release(u):
                pe.wait_ge(s["gemm"], used[1])
                if u + 1 > used[0]:
                    pe.sem_inc(s["unit_used"], u + 1 - used[0])
                    used[0] = u + 1

            def project(u0, owner, base_count, split=False):
                done = 0
                for m in range(4):
                    sl = slot_of(u0 + m)
                    pe.wait_ge(s["w_lo"], u0 + m + 1)
                    for c0, cn in TOKCH:
                        done += len(parts(c0, cn)) if split else 1
                        b = group(owner, base_count + done)
                        for k in range(KT):
                            last = product(ps[:, b, 0:cn], ring_r[:, sl, 0, k, :], ring_r[:, sl, 1, k, :],
                                           hTh[:, k, c0:c0 + cn], hTl[:, k, c0:c0 + cn], k == 0, k == KT - 1)
                        last.then_inc(s["gemm"], 1)
                        if c0 == 0:
                            release(u0 + m - 1)
                    used[1] = len(owners)

            project(UQ, "gev_qk", 0)
            project(UK, "gev_qk", 12, True)
            pe.wait_ge(s["gev_qk"], 28)
            for i in range(5):
                b = group("gev_kout", i + 1)
                for m in range(HP):
                    src = kT[:, m, (4 + i) * P:(5 + i) * P] if i < 4 else kTs[:, m, :]
                    last = tr(ps[:, b, m * P:(m + 1) * P], src, ident[:])
                last.then_inc(s["gemm"], 1)
            pe.wait_ge(s["w_lo"], UV + 4)
            wv0 = slot_of(UV)
            for t in range(NT):
                b = group("gev_v", t + 1)
                for k in range(KT):
                    tile = slice(t * P, (t + 1) * P)
                    last = product(ps[:, b, :], hTh[:, k, tile], hTl[:, k, tile], ring_r[:, wv0:wv0 + 4, 0, k, :],
                                   ring_r[:, wv0:wv0 + 4, 1, k, :], k == 0, k == KT - 1)
                last.then_inc(s["gemm"], 1)
                if t == 0:
                    release(UV - 1)
            used[1] = len(owners)
            release(UV + 3)
            pe.wait_ge(s["gev_v"], NT)
            pe.wait_ge(s["gev_kout"], 5)

            NA = H * NPT

            def unit(a):
                pair, hh_ = a // 2, a % 2
                return pair // NPT, pair % NPT, hh_

            def scores(a):
                hp, i, h_ = unit(a)
                q = qz[:, (a // 2) % 2, h_, :]
                j0 = 4 - min(i, 4)
                pe.wait_ge(s["qz_ok"], 2 * (a // 2) + 2)
                wait(pe, s["s_sb"], a - 1)
                k0 = (i - 4 + j0) * P
                if j0 < 4:
                    mm(bank(2 * (a % 2))[:, j0 * P:512], q, kT[:, hp, k0:i * P], start=True, stop=True)
                mm(bank(2 * (a % 2) + 1)[:, 0:P], q, kT[:, hp, i * P:(i + 1) * P], start=True, stop=True
                   ).then_inc(s["s_scores"], 1)

            def prob_t(a):
                _, i, _ = unit(a)
                pe.wait_ge(s["s_p"], a + 1)
                wait(pe, s["s_ptc"], a)
                for j in range(4 - min(i, 4), 5):
                    last = tr(bank(4, 2)[:, j * P:(j + 1) * P], Pr[:, a % 2, j * P:(j + 1) * P], ident[:])
                last.then_inc(s["s_pt"], 1)

            def values(a):
                hp, i, h_ = unit(a)
                pe.wait_ge(s["s_ptc"], a + 1)
                if h_ == 0:
                    wait(pe, s["s_at"], a // 2)
                j0 = 4 - min(i, 4)
                for j in range(j0, 5):
                    last = mm(ps[:, 6, HD * h_:HD * h_ + HD], PT[:, a % 2, j, :],
                              v[:, i - 4 + j, (2 * hp + h_) * HD:(2 * hp + h_ + 1) * HD],
                              start=(j == j0), stop=(j == 4))
                last.then_inc(s["s_pv"], 1)

            def att_t(pair):
                pe.wait_ge(s["s_at"], pair + 1)
                wait(pe, s["s_attc"], pair)
                tr(ps[:, 7, 0:P], attt[:, pair % 2, :], ident[:]).then_inc(s["s_att"], 1)

            scores(0)
            scores(1)
            for a in range(NA):
                if a + 2 < NA:
                    scores(a + 2)
                prob_t(a)
                if a >= 1:
                    values(a - 1)
                if a % 2 == 1 and a >= 3:
                    att_t(a // 2 - 1)
            values(NA - 1)
            att_t(NA // 2 - 1)
            pe.wait_ge(s["s_attc"], HP * NPT)

            def old_keys_t(q):
                r = q % 2
                pe.wait_ge(s[f"k_in{r}"], 16 * (q // 2 + 1))
                wait(pe, s["k_trc"], 2 * q)
                for m in range(HP):
                    for c in range(4):
                        last = tr(ps[:, m, c * P:(c + 1) * P], kc[:, r, c, m * P:(m + 1) * P], ident[:])
                last.then_inc(s["k_tr"], 1)

            def sample_scores(q):
                pe.wait_ge(s["k_trc"], 2 * q + 2)
                pe.wait_ge(s["qb"], 2 * q + 2)
                wait(pe, s["ks_sb"], q)
                qb = qblk[:, q % 2, 0:512].rearrange("p (m c) -> p m c", m=HP)
                for m in range(HP):
                    mm(ps[:, 4, :], qb[:, m, :], kcT[:, m, :], start=(m == 0), stop=(m == HP - 1))
                for m in range(HP):
                    last = mm(ps[:, 5, 0:DEC], qb[:, m, :], kTs[:, m, q * DEC:(q + 1) * DEC],
                              start=(m == 0), stop=(m == HP - 1))
                last.then_inc(s["ks_sc"], 1)

            old_keys_t(0)
            sample_scores(0)
            for q in range(SEQS):
                r = q % 2
                if q + 1 < SEQS:
                    old_keys_t(q + 1)
                pe.wait_ge(s["ks_p"], q + 1)
                wait(pe, s["ks_ptc"], 2 * q)
                wait(pe, s["ks_at"], H * q)
                for c in range(4):
                    tr(ps[:, 6, c * P:(c + 1) * P], Ps[:, c * P:(c + 1) * P], ident[:])
                tr(ps[0:DEC, 5, P:2 * P], Ps[:, PAST:NK], ident[:]).then_inc(s["ks_pt"], 1)
                pe.wait_ge(s["ks_ptc"], 2 * q + 2)
                wait(pe, s["ks_ev"], q)
                pe.wait_ge(s[f"v_in{r}"], 32 * (q // 2 + 1))
                for c in range(4):
                    mm(ps[:, 7, :], PTs[:, c, :], vc[:, r, c, :], start=(c == 0), stop=False)
                mm(ps[:, 7, :], PTs[0:DEC, 4, :], v16[:, r, :], start=False, stop=True).then_inc(s["ks_pv"], 1)
                if q + 1 < SEQS:
                    sample_scores(q + 1)
                pe.wait_ge(s["ks_ev"], q + 1)
                for m in range(HP):
                    last = tr(ps[:, 6, m * P:(m + 1) * P], atts[:, m * P:(m + 1) * P], ident[:])
                last.then_inc(s["ks_att"], 1)
            pe.wait_ge(s["ks_at"], H * SEQS)

            g0 = len(owners)
            project(UCC, "gev_conv", 0, True)
            project(UCV, "cu_done", 0, True)
            pe.wait_ge(s["prev_in"], 16)
            b = group("gev_prev", 1)
            for m in range(HP):
                last = tr(ps[:, b, m * 16:(m + 1) * 16], st_in[:, m * P:(m + 1) * P], ident[0:16, 0:16])
            last.then_inc(s["gemm"], 1)
            pe.wait_ge(s["conv_last"], 1)
            b = group("newc_sb", 1)
            for m in range(HP):
                last = tr(ps[0:18, b, m * P:(m + 1) * P], lastu[:, m, :], ident[:])
            last.then_inc(s["gemm"], 1)
            project(UCB, "cu_done", 16)

            for i in range(24):
                f, (c0, cn) = i // 3, TOKCH[i % 3]
                if i == 1:
                    pe.wait_ge(s["cu_done"], 28)
                ua, ub, up = [slot_of(UGATE + 3 * f + j) for j in range(3)]
                wait(pe, s["g_done"], i - 1)
                b = 4 * (i % 2)
                for kind, (sl, un, k0, kn, xh, xl, br) in enumerate((
                        (ua, 0, 0, KT, hTh, hTl, 0), (up, 2, 0, 4, atth, attl, 1),
                        (ub, 1, 0, KT, hTh, hTl, 0), (up, 2, 4, 4, Yh, Yl, HP + 1))):
                    if i % 3 == 0:
                        pe.wait_ge(s["w_lo"], UGATE + 3 * f + un + 1)
                        wait(pe, s["b_lo"], br)
                    for k in range(kn):
                        last = product(ps[:, b + kind, 0:cn], ring_r[:, sl, 0, k0 + k, :],
                                       ring_r[:, sl, 1, k0 + k, :], xh[:, k, c0:c0 + cn], xl[:, k, c0:c0 + cn],
                                       k == 0, k == kn - 1)
                    last.then_inc(s["g_ready"], 1)
                    if i == 0 and kind == 0:
                        release(UCB + 3)
                    if i % 3 == 0 and f > 0 and kind == 0:
                        pe.wait_ge(s["g_ready"], 4 * i)
                        pe.sem_inc(s["unit_used"], 3)
            pe.wait_ge(s["g_ready"], 4 * 24)
            pe.sem_inc(s["unit_used"], 3)
            pe.wait_ge(s["g_done"], 24)

            def out_project(t):
                pe.wait_ge(s["w_lo"], NU + t + 1)
                wait(pe, s["x1_done"], t - 1)
                for h in range(2):
                    for k in range(KT):
                        last = product(ps[:, 2 * (t % 2) + h, :], mixh[:, t % 2, k, :], mixl[:, t % 2, k, :],
                                       ring_r[:, 4 * h:4 * h + 4, 0, k, :], ring_r[:, 4 * h:4 * h + 4, 1, k, :],
                                       k == 0, k == KT - 1)
                last.then_inc(s["o_done"], 1)

            pe.wait_ge(s["wr_in"], 64)
            out_project(0)
            for t in range(NT):
                if t + 1 < NT:
                    out_project(t + 1)
                pe.wait_ge(s["n2_h"], t + 1)
                wait(pe, s["n2_evac"], t)
                for k in range(KT):
                    last = tr(bank(4, 2)[:, k * P:(k + 1) * P], h2[:, t % 2, k * P:(k + 1) * P], ident[:])
                last.then_inc(s["n2_tr"], 1)
                pe.wait_ge(s["n2_evac"], t + 1)
                wait(pe, s["n2_lev"], t)
                for k in range(KT):
                    last = mm(ps[:, 6, 0:NLOG], h2T[:, k * P:(k + 1) * P], wr[:, k, :],
                              start=(k == 0), stop=(k == KT - 1))
                last.then_inc(s["n2_log"], 1)
                if t + 2 == NT:
                    pe.wait_ge(s["o_done"], NT)
                    pe.sem_inc(s["unit_used"], KT)

            pe.wait_ge(s["ranks"], 1)
            pv = picked[:].rearrange("p t e -> p (t e)")
            mm(ps[:, 0, 0:NT * E], before[:], pv, start=True, stop=True)
            mm(ps[:, 1, 0:NT * E], ones[:], pv, start=True, stop=True).then_inc(s["ranks"], 1)
            for j in range(2 * NT):
                if j % NT == 0:
                    pe.wait_ge(s["onehot"], 2 * (j // NT) + 2)
                last = mm(ps[:, 2, 0:NBP], onerow[:, j, :], oneblk[:, j, :], start=(j == 0), stop=(j == 2 * NT - 1))
            last.then_inc(s["table_ps"], 1)
            pe.wait_ge(s["route_done"], 1)

            def rows_t(e, r, count):
                wait(pe, s["xTl_ok"], e)
                pe.wait_ge(s[f"xg_in{r}"], count)
                for k in range(KT):
                    last = tr(bank(0, 2)[:, k * P:(k + 1) * P], xg[:, r, k * P:(k + 1) * P], ident[:])
                last.then_inc(s["xg_tr"], 1)

            def gate_up_half(j, r, sig):
                for k in range(4):
                    c = slice(((j % 2) * 4 + k) * P, ((j % 2) * 4 + k + 1) * P)
                    n = slice(k * 512, (k + 1) * 512)
                    last = product(bank(2 + j // 2), xTh[:, r, c], xTl[:, r, c], mhi[j][:, n], mlo[j][:, n],
                                   j % 2 == 0 and k == 0, j % 2 == 1 and k == 3)
                if sig is not None:
                    last.then_inc(sig, 1)

            def gate_up(e, r):
                pe.wait_ge(s["xTl_ok"], e + 1)
                for j in range(4):
                    if j == 0:
                        wait(pe, s["silu_ok"], e)
                    if j == 2:
                        wait(pe, s["h_ok"], e)
                    pe.wait_ge(s["gu_lo"], e * 4 + (j + 1))
                    gate_up_half(j, r, s["gu_used"])

            def down_half(j, sig):
                for k in range(2):
                    c = slice(((j - 4) * 2 + k) * P, ((j - 4) * 2 + k + 1) * P)
                    for h in range(2):
                        n = slice(k * D + h * 512, k * D + (h + 1) * 512)
                        last = product(bank(5 + h), hhTh[:, c], hhTl[:, c], mhi[j][:, n], mlo[j][:, n],
                                       j == 4 and k == 0, j == 5 and k == 1)
                if sig is not None:
                    last.then_inc(sig, 1)

            def down(e):
                pe.wait_ge(s["hTl_ok"], e + 1)
                wait(pe, s["y_ok"], e)
                for j in (4, 5):
                    pe.wait_ge(s["d_lo"], e * 2 + (j - 3))
                    down_half(j, s["d_used"])

            def hidden_mms(sig):
                for k in range(4):
                    last = tr(bank(4)[:, k * P:(k + 1) * P], hh[:, k * P:(k + 1) * P], ident[:])
                last.then_inc(s[sig], 1)

            def hidden_t(e):
                pe.wait_ge(s["h_ok"], e + 1)
                wait(pe, s["hTl_ok"], e)
                hidden_mms("h_tr")

            rows_t(0, 0, 16)
            gate_up(0, 0)
            rows_t(1, 1, 16)
            hidden_t(0)
            gate_up(1, 1)
            rows_t(2, 0, 32)
            down(0)
            hidden_t(1)
            with pe.Fori(1, E // 2 - 1) as i:
                gate_up(i * 2, 0)
                rows_t(i * 2 + 1, 1, (i + 1) * 16)
                down(i * 2 - 1)
                hidden_t(i * 2)
                gate_up(i * 2 + 1, 1)
                rows_t(i * 2 + 2, 0, (i + 2) * 16)
                down(i * 2)
                hidden_t(i * 2 + 1)
            gate_up(E - 2, 0)
            rows_t(E - 1, 1, 16 * (E // 2))
            down(E - 3)
            hidden_t(E - 2)
            gate_up(E - 1, 1)
            down(E - 2)
            hidden_t(E - 1)
            down(E - 1)

            pe.wait_ge(s["routed"], 1)
            pe.wait_ge(s["y_ok"], E)
            n_ov = pe.value_load(eids[0:1, OVF:OVF + 1], min_val=0, max_val=OVF)
            pe.sem_inc(s["o_dn"], 1)
            with pe.If(n_ov > 0):
                with pe.Fori(0, OVF) as o:
                    with pe.If(o < n_ov):
                        pe.wait_ge(s["o_xg"], (o + 1) * 16)
                        for k in range(KT):
                            last = tr(bank(0, 2)[:, k * P:(k + 1) * P], xg[:, 0, k * P:(k + 1) * P], ident[:])
                        last.then_inc(s["o_pe"], 1)
                        pe.wait_ge(s["o_dve"], o * 10 + 7)
                        for j in range(4):
                            gate_up_half(j, 0, s["o_pe"] if j % 2 == 1 else None)
                        pe.wait_ge(s["o_dve"], o * 10 + 8)
                        hidden_mms("o_pe")
                        pe.wait_ge(s["o_dve"], o * 10 + 9)
                        down_half(4, None)
                        down_half(5, s["o_dn"])


_INS = ['x_prompt', 'x_sample', 'cache_attn_k', 'cache_attn_v', 'state_conv', 'c_prompt', 'c_sample',
        'w_ada', 'b_ada', 'norm1_g', 'norm2_g', 'w_in', 'rel_bias', 'conv_w', 'conv_b', 'w_pa', 'w_pb', 'w_o',
        'w_group', 'b_group', 'w_expert', 'b_expert', 'w_e_gate', 'w_e_up', 'w_e_down', 'final_g']
_OUTS = [(1, NP_TOK, D), (SEQS, DEC, D), (1, 1, 512, H, HD), (1, 1, 512, H, HD), (1, 1, 2, DA),
         (1, SEQS, DEC, H, HD), (1, SEQS, DEC, H, HD), (1, SEQS, 2, DA)]


def kernel(**inputs):
    import numpy as _np
    import concourse.bacc as _bacc
    from concourse import mybir as _mybir
    from concourse.bass_utils import run_bass_kernel_spmd as _run

    nc = _bacc.Bacc("TRN2", target_bir_lowering=False, num_devices=1)
    arrays, args = {}, []
    for name in _INS:
        a = _np.ascontiguousarray(inputs[name])
        arrays[f"in_{name}_dram"] = a
        args.append(nc.dram_tensor(f"in_{name}_dram", a.shape, _mybir.dt.from_np(a.dtype), kind="ExternalInput").ap())
    for i, shape in enumerate(_OUTS):
        args.append(nc.dram_tensor(f"out_{i}_dram", shape, _mybir.dt.float32, kind="ExternalOutput").ap())
    build(nc, *args)
    r = _run(nc, [arrays], core_ids=[0])
    return tuple(r.results[0][f"out_{i}_dram"] for i in range(len(_OUTS)))
```

```python
from contextlib import ExitStack

import concourse.bass as bass
from concourse import mybir

ALU = mybir.AluOpType
ACT = mybir.ActivationFunctionType
AX = mybir.AxisListType
F32 = mybir.dt.float32
F32R = mybir.dt.float32r
I32 = mybir.dt.int32

P = 128
D = 1024
KT = D // P
NP_TOK, SEQS, DEC = 1024, 8, 16
NS_TOK = SEQS * DEC
T = NP_TOK + NS_TOK
NPT = NP_TOK // P
NT = T // P
H, HD = 8, 64
HP = H // 2
DA = H * HD
CW = 3
PAST = 512
MAXREL = 128
NREL = 2 * MAXREL + 1
BAND = 5 * P
NEG = -1e30
EPS = 1e-6
G, EPG = 4, 8
E = G * EPG
DE = 512
NLOG = G + E
CAP = P
OVF = (2 * T) // CAP - 1
NBLK = E + OVF
SEQROW = SEQS
TC = T // 3
TOKCH = [(0, TC), (TC, TC), (2 * TC, TC)]


class Link:

    def __init__(self, eng, sem):
        self.eng, self.sem, self.n = eng, sem, 0

    def start(self, ins):
        self.n += 1
        ins.then_inc(self.sem, 1)

    def finish(self):
        self.eng.wait_ge(self.sem, self.n)

    def __call__(self, ins):
        self.start(ins)
        self.finish()


def wait(eng, sem, value):
    if isinstance(value, int) and value <= 0:
        return
    eng.wait_ge(sem, value)


def parts(c0, cn):
    out = []
    if c0 < NP_TOK:
        out.append((c0, min(c0 + cn, NP_TOK) - c0, False))
    if c0 + cn > NP_TOK:
        start = max(c0, NP_TOK)
        out.append((start, c0 + cn - start, True))
    return out


def build(nc, x_prompt, x_sample, cache_attn_k, cache_attn_v, state_conv, c_prompt, c_sample,
          w_ada, b_ada, norm1_g, norm2_g, w_in, rel_bias, conv_w, conv_b, w_pa, w_pb, w_o,
          w_group, b_group, w_expert, b_expert, w_e_gate, w_e_up, w_e_down, final_g,
          y_prompt, y_sample, new_k_prompt, new_v_prompt, new_conv_prompt,
          new_k_sample, new_v_sample, new_conv_sample):
    with ExitStack() as ctx:
        base = (nc.sbuf_base + 63) // 64 * 64
        KB = 1024
        CONST, RING, ARENA = 0, 8 * KB + 512, 56 * KB + 512

        def at(name, shape, offset, dt=F32):
            return nc.alloc_sbuf_tensor_at(name, shape, dt, offset=base + int(offset))

        def sem(name):
            return ctx.enter_context(nc.semaphore(name))

        def psum(name, shape):
            return ctx.enter_context(nc.psum_tensor(name, shape, F32))

        def dram(name, shape, dt=F32):
            return nc.dram_tensor(name, shape, dt).ap()

        mod_d = dram("mod_d", (SEQS + 1, 6 * D))
        modrep_d = dram("modrep_d", (NS_TOK, 4 * D))
        relrow_d = dram("relrow_d", (H, P, P - 1 + BAND))
        mix_d = dram("mix_d", (NT, P, KT, P))
        h2_d = dram("h2_d", (T, D))
        y_d = dram("y_d", (P * NBLK, D))

        cur = [CONST]

        def small(name, shape, dt=F32):
            n = 1
            for s in shape[1:]:
                n *= s
            n = (n * 4 + 31) // 32 * 32
            t = at(name, shape, cur[0], dt)
            cur[0] += n
            assert cur[0] <= RING, cur[0]
            return t

        ident = small("ident", [P, P])
        before = small("before", [P, P])
        ones = small("ones", [P, P])
        eps = small("eps", [P, 1])
        tokid = small("tokid", [P, NT])
        sumsq = small("sumsq", [P, 4, NT])
        rowmax = small("rowmax", [P, 72])
        negmax = small("negmax", [P, 72])
        rowsum = small("rowsum", [P, 72])
        rinv = small("rinv", [P, 72])
        convw = small("convw", [P, CW + 1, HP])
        wr = small("wr", [P, KT, NLOG])
        br = small("br", [P, NLOG])
        logits = small("logits", [P, NT, NLOG])
        table = small("table", [P, NBLK], I32)
        dest = small("dest", [P, 2, NT], I32)
        wts = small("wts", [P, 2, NT])
        eids = small("eids", [P, OVF + 1], I32)
        idx = small("idx", [P, 2], I32)
        lastu = small("lastu", [P, HP, 18])

        NSLOT = 6
        ring_r = at("ring_r", [P, NSLOT + 2, 2, KT, P], RING, F32R)
        ring_f = at("ring_f", [P, NSLOT + 2, 2, KT, P], RING)
        SLOT = 16 * KB
        MH = 4 * 512
        mhi = [at(f"mhi{j}", [P, MH], RING + j * SLOT, F32R) for j in range(6)]
        mraw = [at(f"mraw{j}", [P, MH], RING + j * SLOT + SLOT // 2) for j in range(6)]
        mlo = [at(f"mlo{j}", [P, MH], RING + j * SLOT + SLOT // 2, F32R) for j in range(6)]

        def A(kb):
            return ARENA + kb * KB

        def X(kb):
            return RING + 8 * 4 * KB + kb * KB

        aring = [at(f"aring{j}", [P, KT, 512], RING + j * SLOT if j < 3 else A(108)) for j in range(4)]
        hTh = at("hTh", [P, KT, T], A(0), F32R)
        hTl = at("hTl", [P, KT, T], A(36), F32R)
        hTlf = at("hTlf", [P, KT, T], A(36))
        qT = at("qT", [P, HP, T], A(72))
        kT = at("kT", [P, HP, NP_TOK], A(90))
        kTs = at("kTs", [P, HP, NS_TOK], A(106))
        v = at("v", [P, NT, DA], A(108))
        kk = at("kk", [P, 2, DA], A(144))
        zrow = at("zrow", [P, 256], A(149))
        relin = at("relin", [H, NREL], A(127))
        relrow = at("relrow", [H, P - 1 + BAND], A(124))
        c_sb = at("c_sb", [SEQS + 1, D], A(124))
        cT = at("cT", [P, KT, SEQS + 1], A(128.0625))
        modc = at("modc", [SEQS + 1, 3, 512], A(128.5))
        bada = at("bada", [SEQS + 1, 3, 512], A(134.5))
        spread = at("spread", [SEQS + 1, 2, P], A(149.5))
        xts = [at(f"xt{j}", [P, D], A(72 + 4 * j) if j < 2 else A(140.5 + 4 * (j - 2))) for j in range(4)]
        ht = at("ht", [P, 2, D], A(80))
        scale1 = at("scale1", [P, 2, D], A(88))
        shift1 = at("shift1", [P, 2, D], A(96))
        g1 = at("g1", [P, D], A(104))
        bias = at("bias", [P, H, BAND], A(128.125))
        qz = at("qz", [P, 2, 2, P], A(148.25))
        S = at("S", [P, 2, BAND], X(0))
        Pr = at("Pr", [P, 2, BAND], X(5))
        PT = at("PT", [P, 2, 5, P], X(10))
        attt = at("attt", [P, 2, P], X(15))
        NK = PAST + DEC
        kc = at("kc", [P, 2, 4, DA], RING + 2 * 8 * KB)
        vc = at("vc", [P, 2, 4, DA], A(108))
        kcT = at("kcT", [P, HP, PAST], A(128.125))
        Ps = at("Ps", [P, NK], A(136.25))
        PTs = at("PTs", [P, 5, P], A(138.5))
        sbias = at("sbias", [P, NK], A(126))
        Ss = at("Ss", [P, NK], X(0))
        atts = at("atts", [P, DA], X(3))
        v16 = at("v16", [DEC, 2, DA], X(5))
        qblk = at("qblk", [P, 2, 640], X(9))
        U = at("U", [P, HP, NP_TOK + 2], A(90))
        Us = at("Us", [P, HP, SEQS, DEC + 2], A(106.25))
        st_in = at("st_in", [SEQS * 2, DA], A(109))
        newc = at("newc", [18, DA], A(111))
        Yh = at("Yh", [P, HP, T], A(114), F32R)
        Y = at("Y", [P, HP, T], A(132.5))
        Yl = at("Yl", [P, HP, T], A(132.5), F32R)
        atth = at("atth", [P, HP, T], A(90), F32R)
        attl = at("attl", [P, HP, T], A(72), F32R)
        sgA = at("sgA", [P, 512], A(108))
        sgB = at("sgB", [P, 512], A(110))
        mixc = at("mixc", [P, 512], A(112))
        mixh = at("mixh", [P, 2, KT, P], A(16), F32R)
        mixr = at("mixr", [P, 2, KT, P], A(24))
        mixl = at("mixl", [P, 2, KT, P], A(24), F32R)

        def mix_parts(t):
            if t == 0:
                return hTl[:, :, 0:P], hTlf[:, :, P:2 * P], hTl[:, :, P:2 * P]
            return mixh[:, t % 2], mixr[:, t % 2], mixl[:, t % 2]

        x1 = at("x1", [P, NT, D], A(48))
        h2 = at("h2", [P, 2, D], A(84))
        h2T = at("h2T", [P, 2, D], A(92))
        sq = at("sq", [P, D], A(136))
        logT = at("logT", [NLOG, P], A(140))
        gate1 = at("gate1", [P, 2, D], A(100))
        scale2 = at("scale2", [P, 2, D], A(108))
        shift2 = at("shift2", [P, 2, D], A(116))
        xr = at("xr", [P, 2, D], A(124))
        g2 = at("g2", [P, D], A(132))
        R = 122

        def rt(i, shape, dt=F32):
            return at(f"route{i}", shape, A(R) + i * 1184, dt)

        lg = rt(0, [P, NT, G])
        gmask = rt(1, [P, NT, G])
        le = rt(2, [P, NT, E])
        o1 = rt(3, [P, NT, E])
        o2 = rt(4, [P, NT, E])
        picked = rt(5, [P, NT, E])
        rank = rt(6, [P, NT, E])
        tmp = rt(8, [P, NT, E])
        prefix = rt(9, [P, NT, E])
        picks_of = rt(10, [P, 8, 2, NT])
        tieb = rt(11, [P, 64])
        eidx = rt(12, [P, E])
        cnt = rt(13, [P, E])
        ovc = rt(14, [P, E])
        ovi = rt(15, [P, E])
        ove = rt(16, [P, E])
        sm = rt(17, [P, 8, NT])
        ocmp = rt(18, [P, OVF, E])
        ocmp2 = rt(21, [P, OVF + 1])
        oidx = rt(22, [P, OVF])
        rowi = rt(23, [P, P])
        blki = rt(7, [P, NBLK])
        NBP = NBLK + NBLK % 2
        onerow = at("onerow", [P, 2 * NT, P], A(100), F32R)
        oneblk = at("oneblk", [P, 2 * NT, NBP], A(110), F32R)
        xg = at("xg", [P, 2, D], A(84))
        xTh = at("xTh", [P, 2, D], A(92), F32R)
        xTl = at("xTl", [P, 2, D], A(100), F32R)
        sg = at("sg", [P, DE], A(108))
        hh = at("hh", [P, DE], A(110))
        hhTh = at("hhTh", [P, DE], A(112), F32R)
        hhTl = at("hhTl", [P, DE], A(114), F32R)
        yy = at("yy", [P, 2, D], A(116))
        gate2 = at("gate2", [P, 2, D], A(124))
        fg = at("fg", [P, D], A(132))
        ya = at("ya", [P, NT, D], RING)
        yb = at("yb", [P, NT, D], RING + 36 * KB)
        yo = at("yo", [P, 2, D], RING + 72 * KB)
        yq = at("yq", [P, D], RING + 80 * KB)
        ys = at("ys", [P, 2, D], RING + 84 * KB)

        ps = psum("ps", [P, 8, 512])

        def u_part(m, c0, t0, tn, sample, g):
            src = ps[:, 4 + g % 4, t0 - c0:t0 - c0 + tn]
            if sample:
                return Us[:, m, :, 2:], src.rearrange("p (q t) -> p q t", t=DEC)
            return U[:, m, 2 + t0:2 + t0 + tn], src

        def bank(b, n=1):
            return ps[:, b:b + n, :].rearrange("p b c -> p (b c)")

        names = """consts conv_in c_in c_silu cT_ps cT_sb unit_used mod_sb mod_out0 mod_out1 mod_out2 mod_rep bc_ps bc_sb rel_in rel_sb rel_out
            mods1 x_in0 x_in1 x_in2 x_in3 n1_sq n1_rt n1_h n1_tr n1_evac
            gemm gev_qk gev_kout gev_v gev_prev gev_conv qz_ok kk_out v_out bias_in bias_ok
            s_scores s_sb s_p s_pt s_ptc s_pv s_at s_att s_attc
            k_in0 k_in1 v_in0 v_in1 sb_in w_hi w_lo n1_lo b_hi b_lo mix_out mix_in0 mix_in1 k_tr k_trc qb ks_sc ks_sb ks_p ks_ev ks_pt ks_ptc ks_pv ks_att ks_at
            prev_in conv_last conv_out newc_sb cu_done
            g_ready g_sig g_done wr_in
            mods2 gates_in xr_in0 xr_in1 o_done x1_done n2_sq n2_rt n2_h n2_tr n2_evac n2_log n2_lt n2_ltr n2_lev h2_out0 h2_out1
            picks ranks rconst onehot table_ps route_done routed gathers zrow_ok y_zeroed
            xg_in0 xg_in1 idxc xg_tr xTh_ok xTl_ok gu_hi gu_lo d_hi d_lo gu_used d_used
            silu_ok h_ok h_tr hTh_ok hTl_ok y_ok y_out0 y_out1
            o_w o_idx o_xg o_pe o_act o_dve o_dn o_out
            mods3 ya_in0 ya_in1 ya_in2 ya_in3 f_w f_sq f_rt f_ri f_sc f_out0 f_out1 f_done
            link_dve link_pool""".split()
        s = {n: sem(n) for n in names}
        landed = [sem(f"landed{i}") for i in range(NSLOT)]

        w_in2 = w_in[0].rearrange("(k p) n -> p k n", p=P)
        w_ada2 = w_ada[0].rearrange("(k p) n -> p k n", p=P)
        w_pa2 = w_pa[0].rearrange("(k p) n -> p k n", p=P)
        w_pb2 = w_pb[0].rearrange("(k p) n -> p k n", p=P)
        w_o2 = w_o[0].rearrange("(k p) n -> p k n", p=P)

        def cols(w, c, n):
            return [w[:, 0:4, c * n:(c + 1) * n], w[:, 4:8, c * n:(c + 1) * n]]

        NADA = 6 * D // 512
        ada_units = [cols(w_ada2, c, 512) for c in range(NADA)]
        units = []
        UQ, UK, UV, UCC, UCV, UCB = [4 * i for i in range(6)]
        for c in (0, 1, 2, 4, 5, 3):
            units += [cols(w_in2, 4 * c + j, P) for j in range(4)]
        UGATE = len(units)
        for f in range(KT):
            units.append(cols(w_in2, 24 + f, P))
            units.append(cols(w_in2, 32 + f, P))
            units.append([w_pa2[:, :, f * P:(f + 1) * P], w_pb2[:, :, f * P:(f + 1) * P]])
        UO = len(units)
        units += [cols(w_o2, j, P) for j in range(KT)]
        NU = len(units)
        MIX0 = UO + 3

        def turn(u):
            return u + 1 + (u >= MIX0)

        LEAD = 5
        MOD_OUT = [16 * len([u for u in range(4, NADA) if u % 3 == r]) for r in range(3)]
        ADA_IN = 48 * (NADA // 4)

        def slot_of(u):
            return u % NSLOT if u < NU - 2 else u - (NU - 8)

        def landed_value(u):
            return 32 * (u // NSLOT + 1) + (ADA_IN if u % NSLOT < 4 else 0)

        def unit_in(u):
            return landed[u % NSLOT], landed_value(u)

        LAST_IN = [landed_value(max(u for u in range(NU) if u % NSLOT == j)) for j in range(NSLOT)]

        block = ctx.enter_context(nc.Block())

        def load_mod(eng, dst, part, signal):
            eng.dma_start(dst[:, 0, :], bass.AP(mod_d.tensor, SEQROW * 6 * D + part * D, [[0, P], [1, D]])
                          ).then_inc(signal, 16)
            eng.dma_start(dst[:, 1, :], modrep_d[:, (part - 2) * D:(part - 1) * D]).then_inc(signal, 16)

        def vec_all(eng, dst, vec, n, signal):
            eng.dma_start(dst, bass.AP(vec.tensor, vec.offset, [[0, P], [1, n]])).then_inc(signal, 16)

        @block.sync
        def _(sp):
            def old_keys(q):
                wait(sp, s["k_tr"], q - 1)
                sp.dma_start(kc[:, q % 2], cache_attn_k[0, q].rearrange("(c p) h d -> p c (h d)", p=P)
                             ).then_inc(s[f"k_in{q % 2}"], 16)

            def load_caches():
                sp.wait_ge(s["unit_used"], NADA + UV + 4)
                old_keys(0)
                old_keys(1)
                sp.wait_ge(s["v_out"], 32)
                sp.wait_ge(s["s_attc"], HP * NPT)
                for q in range(SEQS):
                    if 1 <= q < SEQS - 1:
                        old_keys(q + 1)
                    wait(sp, s["ks_pv"], q - 1)
                    sp.dma_start(vc[:, q % 2], cache_attn_v[0, q].rearrange("(c p) h d -> p c (h d)", p=P)
                                 ).then_inc(s[f"v_in{q % 2}"], 16)
                    sp.dma_start(v16[:, q % 2, :], new_v_sample[0, q].rearrange("t h d -> t (h d)")
                                 ).then_inc(s[f"v_in{q % 2}"], 16)
                sp.wait_ge(s["ks_at"], H * SEQS)

            for u, halves in enumerate(ada_units):
                wait(sp, s["unit_used"], u - 3)
                for i, src in enumerate(halves):
                    sp.dma_start(aring[u % 4][:, 4 * i:4 * i + 4, :], src).then_inc(landed[u % 4], 16)
                wait(sp, s["mod_sb"], u - 2)
                sp.dma_start(bada[:, u % 3, :],
                             bass.AP(b_ada.tensor, b_ada.offset + u * 512, [[0, SEQS + 1], [1, 512]])
                             ).then_inc(landed[u % 4], 16)
            def mixture(t):
                wait(sp, s["o_done"], t - 1)
                sp.dma_start(mix_parts(t)[1], mix_d[t]).then_inc(s[f"mix_in{t % 2}"], 16)

            for u, halves in enumerate(units):
                if u == UK + 2:
                    for r in range(3):
                        sp.wait_ge(s[f"mod_out{r}"], MOD_OUT[r])
                    sp.dma_start(modrep_d.rearrange("(q t) c -> q t c", t=DEC),
                                 bass.AP(mod_d.tensor, 2 * D, [[6 * D, SEQS], [0, DEC], [1, 4 * D]])
                                 ).then_inc(s["mod_rep"], 16)
                if u == UCC + 2:
                    load_caches()
                if u == MIX0:
                    sp.wait_ge(s["g_ready"], 4 * 22)
                    sp.wait_ge(s["mix_out"], 16 * 22)
                    mixture(0)
                if u == NU - 2:
                    sp.wait_ge(s["g_ready"], 4 * 24)
                    for j in range(2):
                        sp.wait_ge(landed[j], landed_value(u - NSLOT + j))
                if u < NSLOT:
                    sp.wait_ge(s["unit_used"], min(9 + u, NADA))
                elif u < NU - 2:
                    sp.wait_ge(s["unit_used"], NADA + u - NSLOT + 1)
                for i, src in enumerate(halves):
                    sp.dma_start(ring_f[:, slot_of(u), 1, 4 * i:4 * i + 4, :], src
                                 ).then_inc(landed[u % NSLOT], 16)

            sp.wait_ge(s["mod_rep"], 16)
            sp.wait_ge(s["mix_out"], 16 * 24)
            mixture(1)
            load_mod(sp, gate1, 2, s["gates_in"])
            vec_all(sp, g2[:], norm2_g, D, s["mods2"])
            load_mod(sp, scale2, 4, s["mods2"])
            load_mod(sp, shift2, 3, s["mods2"])
            for t in range(2, NT):
                mixture(t)

            gate_d = w_e_gate[0].rearrange("e (k p) n -> p e k n", p=P)
            up_d = w_e_up[0].rearrange("e (k p) n -> p e k n", p=P)
            down_d = w_e_down[0].rearrange("e (k p) n -> p e k n", p=P)

            def half_of(j, ex):
                w, k0, kn = ((gate_d, 0, 4), (gate_d, 4, 4), (up_d, 0, 4), (up_d, 4, 4),
                             (down_d, 0, 2), (down_d, 2, 2))[j]
                return (w[:, ex, k0:k0 + kn] if isinstance(ex, int)
                        else w[:, bass.ds(ex, 1), k0:k0 + kn].rearrange("p e k n -> p (e k) n"))

            def place_of(j):
                return mraw[j][:].rearrange("p (k n) -> p k n", k=4 if j < 4 else 2)

            def load_gate_up(e):
                for j in range(4):
                    wait(sp, s["gu_used"], e * 4 + (j - 3))
                    sp.dma_start(place_of(j), half_of(j, e)).then_inc(landed[j], 16)

            def load_down(e):
                for j in range(4, 6):
                    wait(sp, s["d_used"], e * 2 + (j - 5))
                    sp.dma_start(place_of(j), half_of(j, e)).then_inc(landed[j], 16)

            sp.wait_ge(s["unit_used"], NADA + NU)
            load_gate_up(0)
            sp.wait_ge(s["routed"], 1)
            load_gate_up(1)
            load_down(0)
            vec_all(sp, fg[:], final_g, D, s["mods3"])
            load_mod(sp, gate2, 5, s["mods3"])
            with sp.Fori(2, E) as e:
                load_gate_up(e)
                load_down(e - 1)
            load_down(E - 1)

            sp.wait_ge(s["d_used"], 2 * E)
            n_ov = sp.value_load(eids[0:1, OVF:OVF + 1], min_val=0, max_val=OVF)
            with sp.If(n_ov > 0):
                with sp.Fori(0, OVF) as o:
                    with sp.If(o < n_ov):
                        ex = sp.value_load(eids[0:1, bass.ds(o, 1)], min_val=0, max_val=E - 1)
                        sp.wait_ge(s["o_dn"], o + 1)
                        for j in range(6):
                            sp.dma_start(place_of(j), half_of(j, ex)).then_inc(s["o_w"], 16)

            for t in range(NT):
                sp.wait_ge(s["f_done"], t + 1)
                dst = y_prompt[0, t * P:(t + 1) * P, :] if t < NPT else y_sample.rearrange("s t d -> (s t) d")
                sp.dma_start(dst, yo[:, t % 2, :]).then_inc(s[f"f_out{t % 2}"], 16)
            sp.wait_ge(s["f_out0"], 16 * 5)
            sp.wait_ge(s["f_out1"], 16 * 4)
            sp.wait_ge(s["conv_out"], 32)
            sp.wait_ge(s["kk_out"], 16 * 5)
            sp.wait_ge(s["v_out"], 16 * 2)

        @block.gpsimd
        def _(pool):
            link = Link(pool, s["link_pool"])

            def row_all(src):
                return src.partition_broadcast(P)

            link(nc.gpsimd.memset(ident[:], 0.0))
            nc.gpsimd.affine_select(out=ident[:], in_=ident[:], compare_op=ALU.not_equal, fill=1.0,
                                    base=0, pattern=[[-1, P]], channel_multiplier=1).then_inc(s["consts"], 1)

            def x_rows(t):
                src = x_prompt[0, t * P:(t + 1) * P, :] if t < NPT else x_sample.rearrange("s t d -> (s t) d")
                pool.dma_start(xts[t % 4][:], src).then_inc(s[f"x_in{t % 4}"], 16)

            for t in range(4):
                x_rows(t)
            link(nc.gpsimd.memset(spread[:], 1.0))
            link(nc.gpsimd.affine_select(out=spread[:, 0, :], in_=spread[:, 0, :], compare_op=ALU.is_ge, fill=0.0,
                                         base=-SEQROW, pattern=[[0, P]], channel_multiplier=1))
            link(nc.gpsimd.affine_select(out=spread[:, 1, :], in_=spread[:, 1, :], compare_op=ALU.is_ge, fill=0.0,
                                         base=0, pattern=[[1, P]], channel_multiplier=-DEC))
            nc.gpsimd.affine_select(out=spread[:, 1, :], in_=spread[:, 1, :], compare_op=ALU.is_ge, fill=0.0,
                                    base=DEC - 1, pattern=[[-1, P]], channel_multiplier=DEC
                                    ).then_inc(s["consts"], 1)
            link(nc.gpsimd.memset(before[:], 1.0))
            link(nc.gpsimd.affine_select(out=before[:], in_=before[:], compare_op=ALU.is_gt, fill=0.0,
                                         base=0, pattern=[[1, P]], channel_multiplier=-1))
            link(nc.gpsimd.memset(ones[:], 1.0))
            link(nc.gpsimd.memset(eps[:], EPS))
            nc.gpsimd.iota(tokid[:], [[P, NT]], base=0, channel_multiplier=1,
                           allow_small_or_imprecise_dtypes=True).then_inc(s["consts"], 1)

            pool.wait_ge(s["cT_ps"], 1)
            pool.dma_start(relin[:], rel_bias[0]).then_inc(s["rel_in"], 16)
            with nc.allow_non_contiguous_dma("conv taps, channel-major"):
                for j in range(CW):
                    pool.dma_start(convw[:, j, :], conv_w[0, j].rearrange("(m p) -> p m", p=P)
                                   ).then_inc(s["conv_in"], 16)
                pool.dma_start(convw[:, CW, :], conv_b[0].rearrange("(m p) -> p m", p=P)
                               ).then_inc(s["conv_in"], 16)
                pool.dma_start(wr[:, :, 0:G], w_group[0].rearrange("(k p) g -> p k g", p=P)
                               ).then_inc(s["wr_in"], 16)
                pool.dma_start(wr[:, :, G:NLOG], w_expert[0].rearrange("(k p) g -> p k g", p=P)
                               ).then_inc(s["wr_in"], 16)
            vec_all(pool, br[:, 0:G], b_group, G, s["wr_in"])
            vec_all(pool, br[:, G:NLOG], b_expert, E, s["wr_in"])

            for t in range(4, NT):
                pool.wait_ge(s["n1_h"], t - 3)
                x_rows(t)

            pool.wait_ge(s["rel_sb"], 2)
            pool.dma_start(relrow_d, relrow[:].unsqueeze(1).to_broadcast([H, P, P - 1 + BAND])
                           ).then_inc(s["rel_out"], 16)
            pool.wait_ge(s["rel_out"], 16)
            pool.wait_ge(s["n1_h"], NT)
            pool.wait_ge(s["n1_tr"], NT)
            RW = P - 1 + BAND
            for r in range(3):
                pool.wait_ge(s[f"mod_out{r}"], MOD_OUT[r])

            def head_bias(h):
                pool.dma_start(bias[:, h, :], bass.AP(relrow_d.tensor, h * P * RW + P - 1, [[RW - 1, P], [1, BAND]])
                               ).then_inc(s["bias_in"], 16)

            for h in range(6):
                head_bias(h)

            for h in range(H):
                pool.dma_start(sbias[h * DEC:(h + 1) * DEC, :],
                               bass.AP(relrow_d.tensor, h * P * RW + P - 1, [[RW - 1, DEC], [1, NK]])
                               ).then_inc(s["sb_in"], 16)

            nc.gpsimd.memset(zrow[:], 0.0).then_inc(s["zrow_ok"], 1)
            pool.wait_ge(s["zrow_ok"], 1)
            y_rows = y_d.rearrange("(p b) (j c) -> p b j c", b=NBLK, c=256)
            with pool.Fori(E, NBLK) as b:
                for j in range(D // 256):
                    pool.dma_start(y_rows[:, bass.ds(b, 1), j, :].rearrange("p b c -> p (b c)"), zrow[:]
                                   ).then_inc(s["y_zeroed"], 16)

            for i in range(5):
                pool.wait_ge(s["gev_kout"], i + 1)
                dst = (new_k_prompt[0, 0, i * P:(i + 1) * P].rearrange("t h d -> t (h d)") if i < 4
                       else new_k_sample[0].rearrange("s t h d -> (s t) (h d)"))
                pool.dma_start(dst, kk[:, i % 2, :]).then_inc(s["kk_out"], 16)
                pool.wait_ge(s["kk_out"], 16 * (i + 1))
            head_bias(6)
            head_bias(7)
            pool.wait_ge(s["gev_v"], NT)
            pool.dma_start(new_v_prompt[0, 0].rearrange("(i p) h d -> p i (h d)", p=P), v[:, NPT - 4:NPT, :]
                           ).then_inc(s["v_out"], 16)
            pool.dma_start(new_v_sample[0].rearrange("s t h d -> (s t) (h d)"), v[:, NPT, :]
                           ).then_inc(s["v_out"], 16)

            pool.wait_ge(s["y_zeroed"], 16 * OVF * (D // 256))
            nc.gpsimd.memset(qz[:], 0.0).then_inc(s["zrow_ok"], 1)
            pool.wait_ge(s["zrow_ok"], 2)
            for pair in range(HP * NPT):
                hp, i = pair // NPT, pair % NPT
                wait(pool, s["s_scores"], 2 * pair - 2)
                for h_ in range(2):
                    rows = slice(HD * h_, HD * h_ + HD)
                    nc.gpsimd.tensor_copy(qz[rows, pair % 2, h_, :], qT[rows, hp, i * P:(i + 1) * P]
                                          ).then_inc(s["qz_ok"], 1)

            pool.wait_ge(s["ks_at"], H * SEQS)
            pool.dma_start(st_in[:], state_conv[0].rearrange("s j c -> (s j) c")).then_inc(s["prev_in"], 16)
            pool.wait_ge(s["newc_sb"], 1)
            pool.dma_start(new_conv_sample[0].rearrange("s j c -> (s j) c"), newc[0:16, :]
                           ).then_inc(s["conv_out"], 16)
            pool.dma_start(new_conv_prompt[0, 0], newc[16:18, :]).then_inc(s["conv_out"], 16)

            for i in range(24):
                f, (c0, cn) = i // 3, TOKCH[i % 3]
                pool.wait_ge(s["g_done"], i + 1)
                if i == 22:
                    pool.wait_ge(s["mix_out"], 16 * 22)
                pool.dma_start(mix_d[c0 // P:(c0 + cn) // P, :, f, :].rearrange("t p c -> p t c"),
                               mixc[:, 0:cn].rearrange("p (t c) -> p t c", c=P)).then_inc(s["mix_out"], 16)

            pool.wait_ge(s["g_ready"], 4 * 24)
            for t in range(NT):
                wait(pool, s["x1_done"], t - 1)
                src = x_prompt[0, t * P:(t + 1) * P, :] if t < NPT else x_sample.rearrange("s t d -> (s t) d")
                pool.dma_start(xr[:, t % 2, :], src).then_inc(s[f"xr_in{t % 2}"], 16)
                if t >= 1:
                    pool.wait_ge(s["n2_h"], t)
                    pool.dma_start(h2_d[(t - 1) * P:t * P, :], h2[:, (t - 1) % 2, :]
                                   ).then_inc(s[f"h2_out{(t - 1) % 2}"], 16)
            pool.wait_ge(s["n2_h"], NT)
            pool.dma_start(h2_d[(NT - 1) * P:, :], h2[:, (NT - 1) % 2, :]).then_inc(s["h2_out0"], 16)

            link(nc.gpsimd.iota(tieb[:], [[-1, 64]], base=64, channel_multiplier=0,
                                allow_small_or_imprecise_dtypes=True))
            link(nc.gpsimd.iota(eidx[:], [[1, E]], base=0, channel_multiplier=0,
                                allow_small_or_imprecise_dtypes=True))
            link(nc.gpsimd.iota(oidx[:], [[1, OVF]], base=0, channel_multiplier=0,
                                allow_small_or_imprecise_dtypes=True))
            link(nc.gpsimd.iota(rowi[:], [[1, P]], base=0, channel_multiplier=0,
                                allow_small_or_imprecise_dtypes=True))
            nc.gpsimd.iota(blki[:], [[1, NBLK]], base=0, channel_multiplier=0,
                           allow_small_or_imprecise_dtypes=True).then_inc(s["rconst"], 1)

            for j in range(4):
                pool.wait_ge(s["gu_hi"], j + 1)
                nc.gpsimd.tensor_tensor(out=mlo[j][:], in0=mraw[j][:], in1=mhi[j][:].bitcast(F32), op=ALU.subtract
                                        ).then_inc(s["gu_lo"], 1)

            pool.wait_ge(s["route_done"], 1)
            pool.wait_ge(s["h2_out0"], 16 * 5)
            pool.wait_ge(s["h2_out1"], 16 * 4)
            pool.wait_ge(s["n2_log"], NT)

            def gather(e, r):
                wait(pool, s["xg_tr"], e - 1)
                col = table[:, e:e + 1] if isinstance(e, int) else table[:, bass.ds(e, 1)]
                nc.gpsimd.tensor_copy(idx[:, r:r + 1], col).then_inc(s["idxc"], 1)
                pool.wait_ge(s["idxc"], e + 1)
                pool.sem_inc(s["gathers"], 1)
                pool.indirect_dma_start(out=xg[:, r, :], out_offset=None, in_=h2_d,
                                        in_offset=bass.IndirectOffsetOnAxis(ap=idx[:, r:r + 1], axis=0)
                                        ).then_inc(s[f"xg_in{r}"], 16)

            gather(0, 0)
            gather(1, 1)
            with pool.Fori(1, E // 2) as i:
                gather(i * 2, 0)
                gather(i * 2 + 1, 1)
            pool.wait_ge(s["routed"], 1)
            pool.wait_ge(s["y_zeroed"], 16 * OVF * (D // 256))
            n_ov = pool.value_load(eids[0:1, OVF:OVF + 1], min_val=0, max_val=OVF)
            pool.wait_ge(s["xg_tr"], E)
            with pool.If(n_ov > 0):
                with pool.Fori(0, OVF) as o:
                    with pool.If(o < n_ov):
                        nc.gpsimd.tensor_copy(idx[:, 0:1], table[:, bass.ds(o + E, 1)]).then_inc(s["o_idx"], 1)
                        pool.wait_ge(s["o_idx"], o + 1)
                        pool.sem_inc(s["gathers"], 1)
                        pool.indirect_dma_start(out=xg[:, 0, :], out_offset=None, in_=h2_d,
                                                in_offset=bass.IndirectOffsetOnAxis(ap=idx[:, 0:1], axis=0)
                                                ).then_inc(s["o_xg"], 16)
                        pool.wait_ge(s["o_out"], (o + 1) * 16)

            pool.wait_ge(s["d_used"], 2 * E)
            for r in range(2):
                pool.wait_ge(s[f"y_out{r}"], 16 * (E // 2))
            for t in range(NT):
                wait(pool, s[f"ya_in{t % 4}"], 32 * (t // 4))
                for k, buf in enumerate((ya, yb)):
                    pool.indirect_dma_start(out=buf[:, t, :], out_offset=None, in_=y_d,
                                            in_offset=bass.IndirectOffsetOnAxis(ap=dest[:, k, t:t + 1], axis=0)
                                            ).then_inc(s[f"ya_in{t % 4}"], 16)
            for t in range(NT):
                pool.wait_ge(s["f_sc"], t + 1)
                if t >= 2:
                    pool.wait_ge(s[f"f_out{t % 2}"], 16 * (t // 2))
                nc.gpsimd.tensor_tensor(out=yo[:, t % 2, :], in0=ys[:, t % 2, :], in1=fg[:], op=ALU.mult
                                        ).then_inc(s["f_done"], 1)

        @block.scalar
        def _(act):
            act.dma_start(c_sb[0:SEQS, :], c_sample).then_inc(s["c_in"], 16)
            act.dma_start(c_sb[SEQS:SEQS + 1, :], c_prompt).then_inc(s["c_in"], 16)
            vec_all(act, g1[:], norm1_g, D, s["mods1"])
            act.wait_ge(s["c_in"], 32)
            nc.scalar.activation(c_sb[:], c_sb[:], ACT.Silu).then_inc(s["c_silu"], 1)

            def modulation_out(u):
                act.wait_ge(s["mod_sb"], u + 1)
                act.dma_start(mod_d[:, u * 512:(u + 1) * 512], modc[:, u % 3, :]
                              ).then_inc(s[f"mod_out{u % 3}"], 16)

            for u in range(2):
                act.wait_ge(s["bc_ps"], u + 1)
                for side in range(2):
                    nc.scalar.copy(shift1[:, side, u * 512:(u + 1) * 512], bank(6 + side)).then_inc(s["bc_sb"], 1)
            modulation_out(4)
            act.wait_ge(s["consts"], 3)

            highs = [0]

            def weights_high_to(n):
                for u in range(highs[0], min(n, NU)):
                    act.wait_ge(*unit_in(u))
                    sl = slot_of(u)
                    nc.scalar.copy(ring_r[:, sl, 0], ring_f[:, sl, 1]).then_inc(s["w_hi"], 1)
                highs[0] = max(highs[0], min(n, NU))

            def square_root(t):
                r = t % 2
                act.wait_ge(s[f"x_in{t % 4}"], 16 * (t // 4 + 1))
                wait(act, s["n1_tr"], t - 1)
                nc.scalar.activation(ht[:, r, :], xts[t % 4][:], ACT.Square, accum_out=sumsq[:, 0, t:t + 1]
                                     ).then_inc(s["n1_sq"], 1)
                act.wait_ge(s["n1_sq"], t + 1)
                nc.scalar.activation(sumsq[:, 1, t:t + 1], sumsq[:, 0, t:t + 1], ACT.Sqrt, scale=1.0 / D,
                                     bias=eps[:, 0:1]).then_inc(s["n1_rt"], 1)

            square_root(0)
            for t in range(NT):
                if t + 1 < NT:
                    square_root(t + 1)
                act.wait_ge(s["n1_tr"], t + 1)
                b = 2 * (t % 2)
                if t == 5:
                    weights_high_to(1)
                nc.scalar.copy(hTh[:, :, t * P:(t + 1) * P], bank(b, 2).rearrange("p (k c) -> p k c", k=KT)
                               ).then_inc(s["n1_evac"], 1)
                if LEAD + t < NADA:
                    modulation_out(LEAD + t)

            weights_high_to(2)
            act.wait_ge(s["rel_out"], 16)
            for r in range(3):
                act.wait_ge(s[f"mod_out{r}"], MOD_OUT[r])
            g = 0
            for what in range(2):
                for m in range(HP):
                    for c0, cn in TOKCH:
                        if c0 == 0:
                            weights_high_to(4 * what + m + 3)
                        act.wait_ge(s["gemm"], g + 1)
                        src = ps[:, 4 + g % 4, 0:cn]
                        if what == 0:
                            nc.scalar.mul(qT[:, m, c0:c0 + cn], src, HD ** -0.5).then_inc(s["gev_qk"], 1)
                        else:
                            for t0, tn, sample in parts(c0, cn):
                                dst = kTs[:, m, t0 - NP_TOK:t0 - NP_TOK + tn] if sample else kT[:, m, t0:t0 + tn]
                                nc.scalar.copy(dst, src[:, t0 - c0:t0 - c0 + tn]).then_inc(s["gev_qk"], 1)
                        g += 1
            weights_high_to(UV + 4)
            for i in range(5):
                act.wait_ge(s["gemm"], g + 1)
                if i >= 2:
                    act.wait_ge(s["kk_out"], 16 * (i - 1))
                nc.scalar.copy(kk[:, i % 2, :], ps[:, 4 + g % 4, :]).then_inc(s["gev_kout"], 1)
                g += 1
            for t in range(NT):
                act.wait_ge(s["gemm"], g + 1)
                nc.scalar.copy(v[:, t, :], ps[:, 4 + g % 4, :]).then_inc(s["gev_v"], 1)
                g += 1

            NA = H * NPT

            def exp_rows(a):
                act.wait_ge(s["s_sb"], a + 1)
                wait(act, s["s_pt"], a - 1)
                c0 = P * (4 - min(a // 2 % NPT, 4))
                nc.scalar.activation(Pr[:, a % 2, c0:BAND], S[:, a % 2, c0:BAND], ACT.Exp,
                                     bias=negmax[:, a:a + 1], accum_out=rowsum[:, a:a + 1]
                                     ).then_inc(s["s_p"], 1)

            def prob_cols(a):
                act.wait_ge(s["s_pt"], a + 1)
                wait(act, s["s_pv"], a - 1)
                j0 = 4 - min(a // 2 % NPT, 4)
                nc.scalar.copy(PT[:, a % 2, j0:5, :],
                               bank(4, 2)[:, j0 * P:BAND].rearrange("p (j c) -> p j c", c=P)
                               ).then_inc(s["s_ptc"], 1)

            exp_rows(0)
            for a in range(NA):
                if a + 1 < NA:
                    exp_rows(a + 1)
                prob_cols(a)
                if a in (20, 40):
                    weights_high_to(UCC + a // 20)

            def old_keys_half(q):
                act.wait_ge(s["k_tr"], q + 1)
                wait(act, s["ks_sc"], q)
                nc.scalar.copy(kcT[:, 0:2, :], bank(0, 2).rearrange("p (m c) -> p m c", m=2)
                               ).then_inc(s["k_trc"], 1)

            old_keys_half(0)
            for q in range(SEQS):
                act.wait_ge(s["ks_sb"], q + 1)
                wait(act, s["ks_pt"], q)
                nc.scalar.activation(Ps[:], Ss[:], ACT.Exp, bias=negmax[:, 64 + q:65 + q],
                                     accum_out=rowsum[:, 64 + q:65 + q]).then_inc(s["ks_p"], 1)
                act.wait_ge(s["ks_pt"], q + 1)
                wait(act, s["ks_pv"], q)
                nc.scalar.copy(PTs[:, 0:4, :], ps[:, 6, :].rearrange("p (j c) -> p j c", c=P)
                               ).then_inc(s["ks_ptc"], 1)
                nc.scalar.copy(PTs[0:DEC, 4, :], ps[0:DEC, 5, P:2 * P]).then_inc(s["ks_ptc"], 1)
                if q + 1 < SEQS:
                    old_keys_half(q + 1)

            for m in range(HP):
                weights_high_to(UCC + m + 2)
                for c0, cn in TOKCH:
                    act.wait_ge(s["gemm"], g + 1)
                    for t0, tn, sample in parts(c0, cn):
                        nc.scalar.copy(*u_part(m, c0, t0, tn, sample, g)).then_inc(s["gev_conv"], 1)
                    g += 1

            for m in range(4):
                if m == 0:
                    weights_high_to(UCV + 2)
                act.wait_ge(s["gemm"], g + 3 * m + 1)
                weights_high_to(UCV + m + 3)
            g += 12 + 2
            act.wait_ge(s["conv_last"], 1)
            act.wait_ge(s["cu_done"], 17)
            nc.scalar.copy(atth[:], qT[:]).then_inc(s["b_hi"], 1)
            for m in range(HP):
                act.wait_ge(s["gemm"], g + 3 * m + 1)
                weights_high_to(UCB + m + 3)
                act.wait_ge(s["cu_done"], 16 + 3 * (m + 1))
                nc.scalar.copy(Yh[:, m, :], Y[:, m, :]).then_inc(s["b_hi"], 1)

            def mixture_high(t):
                act.wait_ge(s[f"mix_in{t % 2}"], 16 * (t // 2 + 1))
                high, values, _ = mix_parts(t)
                nc.scalar.copy(high, values).then_inc(s["w_hi"], 1)

            act.wait_ge(s["conv_out"], 32)
            for i in range(24):
                cn = TOKCH[i % 3][1]
                if i % 3 == 0:
                    weights_high_to(UGATE + i + 3)
                if i == 23:
                    mixture_high(0)
                for k, sb_ in ((0, sgA), (2, sgB)):
                    act.wait_ge(s["g_ready"], 4 * i + k + 1)
                    wait(act, s["g_done"], i)
                    nc.scalar.activation(sb_[:, 0:cn], ps[:, 4 * (i % 2) + k, 0:cn], ACT.Sigmoid
                                         ).then_inc(s["g_sig"], 1)
                    if k == 0 and i % 3 == 0:
                        weights_high_to(UGATE + i + 6)

            weights_high_to(NU)
            mixture_high(1)

            def logits_out(t):
                act.wait_ge(s["n2_log"], t + 1)
                wait(act, s["n2_ltr"], t)
                nc.scalar.copy(logT[:], ps[0:NLOG, 7, 0:P]).then_inc(s["n2_lt"], 1)

            for t in range(NT):
                act.wait_ge(s["x1_done"], t + 1)
                if t + 2 < NT:
                    mixture_high(t + 2)
                nc.scalar.activation(sq[:], x1[:, t, :], ACT.Square, accum_out=sumsq[:, 0, t:t + 1]
                                     ).then_inc(s["n2_sq"], 1)
                act.wait_ge(s["n2_sq"], t + 1)
                nc.scalar.activation(sumsq[:, 1, t:t + 1], sumsq[:, 0, t:t + 1], ACT.Sqrt, scale=1.0 / D,
                                     bias=eps[:, 0:1]).then_inc(s["n2_rt"], 1)
                act.wait_ge(s["n2_tr"], t + 1)
                wait(act, s["n2_log"], t - 1)
                nc.scalar.copy(h2T[:, t % 2, :], bank(4, 2)).then_inc(s["n2_evac"], 1)
                if t >= 1:
                    logits_out(t - 1)
            logits_out(NT - 1)

            act.wait_ge(s["picks"], 1)
            nc.scalar.activation(gmask[:], lg[:], ACT.Exp).then_inc(s["picks"], 1)
            act.wait_ge(s["picks"], 3)
            nc.scalar.activation(sm[:, 3, :], sm[:, 2, :], ACT.Exp).then_inc(s["picks"], 1)

            def weights_high(e, js):
                for j in js:
                    act.wait_ge(landed[j], LAST_IN[j] + (e + 1) * 16)
                    nc.scalar.copy(mhi[j][:], mraw[j][:]).then_inc(s["gu_hi" if j < 4 else "d_hi"], 1)

            def rows_high(e, r):
                act.wait_ge(s["xg_tr"], e + 1)
                wait(act, s["gu_used"], e * 4 - 4)
                nc.scalar.copy(xTh[:, r, :], bank(0, 2)).then_inc(s["xTh_ok"], 1)

            def silu(e):
                act.wait_ge(s["gu_used"], e * 4 + 2)
                wait(act, s["h_ok"], e)
                nc.scalar.activation(sg[:], bank(2), ACT.Silu).then_inc(s["silu_ok"], 1)

            def hidden_high(e):
                act.wait_ge(s["h_tr"], e + 1)
                wait(act, s["d_used"], e * 2)
                nc.scalar.copy(hhTh[:], bank(4)).then_inc(s["hTh_ok"], 1)

            def result(e, r, stored=None):
                act.wait_ge(s["d_used"], e * 2 + 2)
                wait(act, s[f"y_out{r}"], stored)
                nc.scalar.copy(yy[:, r, :], bank(5, 2)).then_inc(s["y_ok"], 1)
                act.wait_ge(s["y_ok"], e + 1)
                dst = y_d.rearrange("(p b) d -> p b d", b=NBLK)
                dst = dst[:, e, :] if isinstance(e, int) else dst[:, bass.ds(e, 1), :].rearrange("p b d -> p (b d)")
                act.dma_start(dst, yy[:, r, :]).then_inc(s[f"y_out{r}"], 16)

            GU0, GU1, DN = (0, 1), (2, 3), (4, 5)
            weights_high(0, GU0 + GU1)
            rows_high(0, 0)

            def act_step(e, r, stored):
                silu(e)
                rows_high(e + 1, 1 - r)
                weights_high(e + 1, GU0)
                if stored is not None:
                    result(e - 1, 1 - r, stored)
                hidden_high(e)
                weights_high(e + 1, GU1)
                weights_high(e, DN)

            act_step(0, 0, None)
            act_step(1, 1, 0)
            act_step(2, 0, 0)
            act_step(3, 1, 16)
            with act.Fori(2, E // 2 - 1) as i:
                act_step(i * 2, 0, (i - 1) * 16)
                act_step(i * 2 + 1, 1, i * 16)
            act_step(E - 2, 0, 16 * (E // 2 - 2))
            silu(E - 1)
            result(E - 2, 0, 16 * (E // 2 - 1))
            hidden_high(E - 1)
            weights_high(E - 1, DN)
            result(E - 1, 1, 16 * (E // 2 - 1))
            act.wait_ge(s["routed"], 1)
            act.wait_ge(s["y_zeroed"], 16 * OVF * (D // 256))
            n_ov = act.value_load(eids[0:1, OVF:OVF + 1], min_val=0, max_val=OVF)
            with act.If(n_ov > 0):
                with act.Fori(0, OVF) as o:
                    with act.If(o < n_ov):
                        act.wait_ge(s["o_w"], (o + 1) * 96)
                        for j in range(6):
                            nc.scalar.copy(mhi[j][:], mraw[j][:]).then_inc(s["o_act"], 1)
                        act.wait_ge(s["o_pe"], o * 4 + 1)
                        nc.scalar.copy(xTh[:, 0, :], bank(0, 2)).then_inc(s["o_act"], 1)
                        act.wait_ge(s["o_pe"], o * 4 + 2)
                        nc.scalar.activation(sg[:], bank(2), ACT.Silu).then_inc(s["o_act"], 1)
                        act.wait_ge(s["o_pe"], o * 4 + 4)
                        nc.scalar.copy(hhTh[:], bank(4)).then_inc(s["o_act"], 1)
                        act.wait_ge(s["o_dve"], o * 10 + 10)
                        dst = y_d.rearrange("(p b) d -> p b d", b=NBLK)[:, bass.ds(o + E, 1), :]
                        act.dma_start(dst.rearrange("p b d -> p (b d)"), yy[:, 0, :]).then_inc(s["o_out"], 16)

            def weigh(t):
                act.wait_ge(s[f"ya_in{t % 4}"], 32 * (t // 4 + 1))
                nc.scalar.activation(ya[:, t, :], ya[:, t, :], ACT.Copy, scale=wts[:, 0, t:t + 1]
                                     ).then_inc(s["f_w"], 1)

            def scaled(t):
                act.wait_ge(s["f_ri"], t + 1)
                wait(act, s["f_done"], t - 1)
                nc.scalar.activation(ys[:, t % 2, :], x1[:, t, :], ACT.Copy, scale=sumsq[:, 3, t:t + 1]
                                     ).then_inc(s["f_sc"], 1)

            weigh(0)
            weigh(1)
            for t in range(NT):
                if t + 2 < NT:
                    weigh(t + 2)
                if t >= 1:
                    scaled(t - 1)
                act.wait_ge(s["f_sq"], 2 * t + 1)
                nc.scalar.activation(yq[:], x1[:, t, :], ACT.Square, accum_out=sumsq[:, 2, t:t + 1]
                                     ).then_inc(s["f_sq"], 1)
                act.wait_ge(s["f_sq"], 2 * t + 2)
                nc.scalar.activation(sumsq[:, 3, t:t + 1], sumsq[:, 2, t:t + 1], ACT.Sqrt, scale=1.0 / D,
                                     bias=eps[:, 0:1]).then_inc(s["f_rt"], 1)
            scaled(NT - 1)

        @block.vector
        def _(dve):
            link = Link(dve, s["link_dve"])
            V = nc.vector

            dve.wait_ge(s["cT_ps"], 1)
            V.tensor_copy(cT[:], ps[:, 6, 0:KT * (SEQS + 1)].rearrange("p (k s) -> p k s", k=KT)
                          ).then_inc(s["cT_sb"], 1)


            def modulation(u):
                dve.wait_ge(s["unit_used"], u + 1)
                if u >= 7:
                    dve.wait_ge(s[f"mod_out{u % 3}"], 16 * len(range(4 + (u - 4) % 3, u, 3)))
                elif u >= 3:
                    dve.wait_ge(s["bc_ps"], min(u - 2, 4))
                V.tensor_tensor(modc[:, u % 3, :], ps[0:SEQS + 1, 4 + u % 2, :], bada[:, u % 3, :],
                                ALU.add).then_inc(s["mod_sb"], 1)

            for u in range(4):
                modulation(u)
            dve.wait_ge(s["rel_in"], 16)
            link(V.memset(relrow[:, 0:4 * P], 0.0))
            V.tensor_scalar(relrow[:, 0:4 * P], relrow[:, 0:4 * P], relin[:, NREL - 1:NREL], None,
                            ALU.add).then_inc(s["rel_sb"], 1)
            n = P - 1 + BAND - 4 * P
            V.tensor_copy(relrow[:, 4 * P:], bass.AP(relin, n, [[NREL, H], [-1, n]])).then_inc(s["rel_sb"], 1)

            modulation(4)

            dve.wait_ge(s["mods1"], 16)
            for u in range(2, 4):
                dve.wait_ge(s["bc_ps"], u + 1)
                half = slice((u - 2) * 512, (u - 1) * 512)
                for side in range(2):
                    V.scalar_tensor_tensor(out=scale1[:, side, half], in0=bank(6 + side), scalar=1.0,
                                           in1=g1[:, half], op0=ALU.add, op1=ALU.mult).then_inc(s["bc_sb"], 1)
            dve.wait_ge(s["bc_sb"], 8)


            def split_rest(out, value, high, sig):
                V.tensor_tensor(out, value, high.bitcast(F32), ALU.subtract).then_inc(sig, 1)

            rests = [0]

            def weights_rest_to(n):
                for u in range(rests[0], min(n, NU)):
                    dve.wait_ge(s["w_hi"], turn(u))
                    sl = slot_of(u)
                    split_rest(ring_r[:, sl, 1], ring_f[:, sl, 1], ring_r[:, sl, 0], s["w_lo"])
                rests[0] = max(rests[0], min(n, NU))

            def rows_rest(t):
                dve.wait_ge(s["n1_evac"], t + 1)
                V.tensor_tensor(hTl[:, :, t * P:(t + 1) * P], bank(2 * (t % 2), 2).rearrange("p (k c) -> p k c", k=KT),
                                hTh[:, :, t * P:(t + 1) * P].bitcast(F32), ALU.subtract).then_inc(s["n1_lo"], 1)

            for t in range(NT):
                r, side = t % 2, int(t == NPT)
                dve.wait_ge(s["n1_rt"], t + 1)
                link(V.reciprocal(sumsq[:, 1, t:t + 1], sumsq[:, 1, t:t + 1]))
                link(V.scalar_tensor_tensor(out=ht[:, r, :], in0=xts[t % 4][:], scalar=sumsq[:, 1, t:t + 1],
                                            in1=scale1[:, side, :], op0=ALU.mult, op1=ALU.mult))
                V.tensor_tensor(ht[:, r, :], ht[:, r, :], shift1[:, side, :], ALU.add).then_inc(s["n1_h"], 1)
                if LEAD + t < NADA:
                    modulation(LEAD + t)
                if t >= 1:
                    rows_rest(t - 1)
                if t == 6:
                    weights_rest_to(1)
            rows_rest(NT - 1)

            weights_rest_to(UV + 4)

            dve.wait_ge(s["bias_in"], 16 * H)
            V.memset(bias[0:HD, :, BAND - 64:BAND], NEG).then_inc(s["bias_ok"], 1)
            V.memset(bias[HD:P, :, 0:64], NEG).then_inc(s["bias_ok"], 1)
            dve.wait_ge(s["bias_ok"], 2)
            NA = H * NPT

            def masked(a):
                i, h = a // 2 % NPT, 2 * (a // 2 // NPT) + a % 2
                c0 = P * (4 - min(i, 4))
                dve.wait_ge(s["s_scores"], a + 1)
                wait(dve, s["s_p"], a - 1)
                link(V.tensor_tensor_reduce(out=S[:, a % 2, c0:BAND], in0=bank(2 * (a % 2), 2)[:, c0:BAND],
                                            in1=bias[:, h, c0:BAND], scale=1.0, scalar=-3e38,
                                            op0=ALU.add, op1=ALU.max, accum_out=rowmax[:, a:a + 1]))
                V.tensor_scalar(negmax[:, a:a + 1], rowmax[:, a:a + 1], -1.0, None, ALU.mult
                                ).then_inc(s["s_sb"], 1)

            def normed(pair):
                a = 2 * pair
                dve.wait_ge(s["s_pv"], a + 2)
                wait(dve, s["s_att"], pair - 1)
                link(V.reciprocal(rinv[:, a:a + 2], rowsum[:, a:a + 2]))
                V.tensor_tensor(attt[:, pair % 2, :].rearrange("p (h d) -> p h d", h=2),
                                ps[:, 6, 0:P].rearrange("p (h d) -> p h d", h=2),
                                rinv[:, a:a + 2].unsqueeze(2).to_broadcast([P, 2, HD]), ALU.mult
                                ).then_inc(s["s_at"], 1)

            def att_cols(pair):
                i, hp = pair % NPT, pair // NPT
                dve.wait_ge(s["s_att"], pair + 1)
                V.tensor_copy(qT[:, hp, i * P:(i + 1) * P], ps[:, 7, 0:P]).then_inc(s["s_attc"], 1)

            masked(0)
            masked(1)
            for a in range(NA):
                if a + 2 < NA:
                    masked(a + 2)
                if a % 2 == 0 and a >= 2:
                    normed(a // 2 - 1)
                if a % 2 == 1 and a >= 3:
                    att_cols(a // 2 - 1)
                if a in (24, 44):
                    weights_rest_to(UCC + (a - 4) // 20)
            normed(NA // 2 - 1)
            att_cols(NA // 2 - 1)

            link(V.memset(qblk[:, :, :], 0.0))
            dve.wait_ge(s["sb_in"], 16 * H)

            def queries(q):
                wait(dve, s["ks_sc"], q - 1)
                qv = qblk[:, q % 2, :].rearrange("p (a b) -> p a b", b=160)
                V.tensor_copy(qv[0:HD, 0:HP, 0:DEC], qT[0:HD, :, NP_TOK + q * DEC:NP_TOK + (q + 1) * DEC]).then_inc(s["qb"], 1)
                V.tensor_copy(qv[HD:P, 0:HP, DEC:2 * DEC], qT[HD:P, :, NP_TOK + q * DEC:NP_TOK + (q + 1) * DEC]
                              ).then_inc(s["qb"], 1)

            def old_keys_rest(q):
                dve.wait_ge(s["k_tr"], q + 1)
                wait(dve, s["ks_sc"], q)
                V.tensor_copy(kcT[:, 2:4, :], bank(2, 2).rearrange("p (m c) -> p m c", m=2)
                              ).then_inc(s["k_trc"], 1)

            def sample_cols(q):
                dve.wait_ge(s["ks_att"], q + 1)
                for h in range(H):
                    m, rows = h // 2, slice(HD * (h % 2), HD * (h % 2) + HD)
                    c = m * P + h * DEC
                    V.tensor_copy(qT[rows, m, NP_TOK + q * DEC:NP_TOK + (q + 1) * DEC], ps[rows, 6, c:c + DEC]
                                  ).then_inc(s["ks_at"], 1)

            queries(0)
            old_keys_rest(0)
            for q in range(SEQS):
                if q + 1 < SEQS:
                    queries(q + 1)
                dve.wait_ge(s["ks_sc"], q + 1)
                wait(dve, s["ks_p"], q)
                link(V.tensor_tensor_reduce(out=Ss[:], in0=bank(4, 2)[:, 0:NK], in1=sbias[:], scale=1.0,
                                            scalar=-3e38, op0=ALU.add, op1=ALU.max,
                                            accum_out=rowmax[:, 64 + q:65 + q]))
                V.tensor_scalar(negmax[:, 64 + q:65 + q], rowmax[:, 64 + q:65 + q], -1.0, None, ALU.mult
                                ).then_inc(s["ks_sb"], 1)
                if q >= 1:
                    sample_cols(q - 1)
                dve.wait_ge(s["ks_p"], q + 1)
                link.start(V.reciprocal(rinv[:, 64 + q:65 + q], rowsum[:, 64 + q:65 + q]))
                if q + 1 < SEQS:
                    old_keys_rest(q + 1)
                dve.wait_ge(s["ks_pv"], q + 1)
                wait(dve, s["ks_att"], q)
                link.finish()
                V.tensor_scalar(atts[:], bank(7), rinv[:, 64 + q:65 + q], None, ALU.mult
                                ).then_inc(s["ks_ev"], 1)
            sample_cols(SEQS - 1)

            g = 12 + 12 + 5 + NT
            link(V.memset(U[:, :, 0:2], 0.0))
            for m in range(HP):
                dve.wait_ge(s["gemm"], g + 3 * m + 1)
                weights_rest_to(UCC + m + 3)
            g += 12
            for m in range(HP):
                weights_rest_to(UCV + m + 3)
                for n, (c0, cn) in enumerate(TOKCH):
                    dve.wait_ge(s["gemm"], g + 1)
                    for t0, tn, sample in parts(c0, cn):
                        dve.wait_ge(s["gev_conv"], 4 * m + n + 1 + sample)
                        dst, src = u_part(m, c0, t0, tn, sample, g)
                        V.tensor_tensor(dst, dst, src, ALU.mult).then_inc(s["cu_done"], 1)
                    g += 1
            dve.wait_ge(s["cu_done"], 16)
            dve.wait_ge(s["gemm"], g + 1)
            V.tensor_copy(Us[:, :, :, 0:2],
                          ps[:, 4 + g % 4, 0:HP * 16].rearrange("p (m q j) -> p m q j", m=HP, j=2)
                          ).then_inc(s["gev_prev"], 1)
            g += 1
            link(V.tensor_copy(lastu[:, :, 0:16].rearrange("p m (q j) -> p m q j", j=2), Us[:, :, :, DEC:]))
            V.tensor_copy(lastu[:, :, 16:18], U[:, :, NP_TOK:]).then_inc(s["conv_last"], 1)
            dve.wait_ge(s["gemm"], g + 1)
            V.tensor_copy(newc[:], ps[0:18, 4 + g % 4, :]).then_inc(s["newc_sb"], 1)
            g += 1
            dve.wait_ge(s["gev_prev"], 1)
            dve.wait_ge(s["conv_in"], 16 * (CW + 1))
            weights_rest_to(UCB + 2)
            for m in range(HP):
                yp, us = Y[:, m, 0:NP_TOK], Y[:, m, NP_TOK:].rearrange("p (q t) -> p q t", t=DEC)
                w = [convw[:, j, m:m + 1] for j in range(CW + 1)]
                link(V.tensor_scalar(yp, U[:, m, 0:NP_TOK], w[0], w[CW], ALU.mult, ALU.add))
                link(V.tensor_scalar(us, Us[:, m, :, 0:DEC], w[0], w[CW], ALU.mult, ALU.add))
                for j in (1, 2):
                    link(V.scalar_tensor_tensor(out=yp, in0=U[:, m, j:j + NP_TOK], scalar=w[j], in1=yp,
                                                op0=ALU.mult, op1=ALU.add))
                    link(V.scalar_tensor_tensor(out=us, in0=Us[:, m, :, j:j + DEC], scalar=w[j], in1=us,
                                                op0=ALU.mult, op1=ALU.add))
            for m in range(HP):
                for c0, cn in TOKCH:
                    dve.wait_ge(s["gemm"], g + 1)
                    V.tensor_tensor(Y[:, m, c0:c0 + cn], Y[:, m, c0:c0 + cn], ps[:, 4 + g % 4, 0:cn], ALU.mult
                                    ).then_inc(s["cu_done"], 1)
                    if c0 == 0:
                        weights_rest_to(UCB + m + 3)
                    g += 1
                if m == 0:
                    dve.wait_ge(s["b_hi"], 1)
                    split_rest(attl[:], qT[:], atth[:], s["b_lo"])
                if m >= 1:
                    dve.wait_ge(s["b_hi"], m + 1)
                    split_rest(Yl[:, m - 1, :], Y[:, m - 1, :], Yh[:, m - 1, :], s["b_lo"])
            dve.wait_ge(s["b_hi"], HP + 1)
            split_rest(Yl[:, HP - 1, :], Y[:, HP - 1, :], Yh[:, HP - 1, :], s["b_lo"])

            def mixture_rest(t):
                dve.wait_ge(s["w_hi"], NU + t + 1 if t else MIX0 + 1)
                high, values, low = mix_parts(t)
                split_rest(low, values, high, s["w_lo"])

            for i in range(24):
                f, (c0, cn) = i // 3, TOKCH[i % 3]
                b = 4 * (i % 2)
                if i % 3 == 0:
                    weights_rest_to(UGATE + i + 3)
                if i == 23:
                    mixture_rest(0)
                dve.wait_ge(s["g_ready"], 4 * i + 2)
                dve.wait_ge(s["g_sig"], 2 * i + 1)
                link(V.tensor_tensor(sgA[:, 0:cn], sgA[:, 0:cn], ps[:, b + 1, 0:cn], ALU.mult))
                if i % 3 == 0:
                    weights_rest_to(UGATE + i + 6)
                dve.wait_ge(s["g_ready"], 4 * i + 4)
                dve.wait_ge(s["g_sig"], 2 * i + 2)
                link(V.tensor_tensor(sgB[:, 0:cn], sgB[:, 0:cn], ps[:, b + 3, 0:cn], ALU.mult))
                wait(dve, s["mix_out"], 16 * i)
                V.tensor_tensor(mixc[:, 0:cn], sgA[:, 0:cn], sgB[:, 0:cn], ALU.add).then_inc(s["g_done"], 1)

            weights_rest_to(NU)
            mixture_rest(1)

            dve.wait_ge(s["gates_in"], 32)

            def residual(t):
                r, side = t % 2, int(t == NPT)
                dve.wait_ge(s["o_done"], t + 1)
                link(V.tensor_tensor(x1[:, t, :], bank(2 * r, 2), gate1[:, side, :], ALU.mult))
                dve.wait_ge(s[f"xr_in{r}"], 16 * (t // 2 + 1))
                V.tensor_tensor(x1[:, t, :], x1[:, t, :], xr[:, r, :], ALU.add).then_inc(s["x1_done"], 1)

            def log_bias(t):
                dve.wait_ge(s["n2_ltr"], t + 1)
                V.tensor_tensor(logits[:, t, :], ps[:, 6, 0:NLOG], br[:], ALU.add).then_inc(s["n2_lev"], 1)

            dve.wait_ge(s["wr_in"], 64)
            residual(0)
            dve.wait_ge(s["mods2"], 16 * (1 + 2 * 2))
            for r in range(2):
                link(V.scalar_tensor_tensor(out=scale2[:, r, :], in0=scale2[:, r, :], scalar=1.0, in1=g2[:],
                                            op0=ALU.add, op1=ALU.mult))
            for t in range(NT):
                r, side = t % 2, int(t == NPT)
                dve.wait_ge(s["n2_rt"], t + 1)
                dve.wait_ge(s["x1_done"], t + 1)
                link(V.reciprocal(sumsq[:, 1, t:t + 1], sumsq[:, 1, t:t + 1]))
                if t >= 2:
                    dve.wait_ge(s[f"h2_out{r}"], 16 * (t // 2))
                    dve.wait_ge(s["n2_tr"], t - 1)
                link(V.scalar_tensor_tensor(out=h2[:, r, :], in0=x1[:, t, :], scalar=sumsq[:, 1, t:t + 1],
                                            in1=scale2[:, side, :], op0=ALU.mult, op1=ALU.mult))
                V.tensor_tensor(h2[:, r, :], h2[:, r, :], shift2[:, side, :], ALU.add).then_inc(s["n2_h"], 1)
                if t + 2 < NT:
                    mixture_rest(t + 2)
                if t + 1 < NT:
                    residual(t + 1)
                if t >= 2:
                    log_bias(t - 2)
            log_bias(NT - 2)
            log_bias(NT - 1)
            dve.wait_ge(s["n2_lev"], NT)

            dve.wait_ge(s["rconst"], 1)
            dve.wait_ge(s["consts"], 3)

            def b3(x2, n):
                return x2.unsqueeze(2).to_broadcast([P, NT, n])

            def c3(row, n):
                return row.unsqueeze(1).to_broadcast([P, NT, n])

            def first_max(out, src, mx, n, buf, m2):
                link(V.tensor_reduce(mx, src, AX.X, ALU.max))
                link(V.tensor_tensor(buf, src, b3(mx, n), ALU.is_equal))
                link(V.tensor_tensor(buf, buf, c3(tieb[:, 0:n], n), ALU.mult))
                link(V.tensor_reduce(m2, buf, AX.X, ALU.max))
                link(V.tensor_tensor(out, buf, b3(m2, n), ALU.is_equal))

            lgr, ler = logits[:, :, 0:G], logits[:, :, G:NLOG]
            gm, sc0 = sm[:, 0, :], sm[:, 1, :]
            pick_g = gmask
            first_max(pick_g[:], lgr, gm, G, lg[:], sc0)
            le4 = le[:].rearrange("p t (g e) -> p t g e", g=G)
            link(V.tensor_scalar(tmp[:, :, 0:G], pick_g[:], -NEG, NEG, ALU.mult, ALU.add))
            for gi in range(G):
                sl = slice(gi * EPG, (gi + 1) * EPG)
                link(V.tensor_tensor(le[:, :, sl], ler[:, :, sl],
                                     pick_g[:, :, gi:gi + 1].to_broadcast([P, NT, EPG]), ALU.mult))
                link(V.tensor_tensor(le[:, :, sl], le[:, :, sl],
                                     tmp[:, :, gi:gi + 1].to_broadcast([P, NT, EPG]), ALU.add))
            V.tensor_tensor(lg[:], lgr, b3(gm, G), ALU.subtract).then_inc(s["picks"], 1)
            m1, m2_ = sm[:, 4, :], sm[:, 5, :]
            first_max(o1[:], le[:], m1, E, tmp[:], sc0)
            link(V.tensor_scalar(tmp[:], o1[:], 4 * NEG, None, ALU.mult))
            link(V.tensor_tensor(le[:], le[:], tmp[:], ALU.add))
            first_max(o2[:], le[:], m2_, E, tmp[:], sc0)
            dve.wait_ge(s["picks"], 2)
            V.tensor_tensor(sm[:, 2, :], m2_, m1, ALU.subtract).then_inc(s["picks"], 1)
            link(V.tensor_reduce(sm[:, 6, :], gmask[:], AX.X, ALU.add))
            V.tensor_tensor(picked[:], o1[:], o2[:], ALU.add).then_inc(s["ranks"], 1)

            def chosen(out, values):
                for k, o in enumerate((o1, o2)):
                    link(V.tensor_tensor(tmp[:], o[:], values, ALU.mult))
                    link(V.tensor_reduce(out[:, k, :], tmp[:], AX.X, ALU.add))

            ek, rk, vk, ck, bk, wk, xk = [picks_of[:, j] for j in range(7)]
            chosen(ek, c3(eidx[:], E))
            link(V.memset(oneblk[:].bitcast(F32), 0.0))
            dve.wait_ge(s["ranks"], 2)
            link(V.memset(prefix[:, 0, :], 0.0))
            tots = ps[:, 1, 0:NT * E].rearrange("p (t e) -> p t e", t=NT)
            for t in range(NT):
                link(V.tensor_tensor(prefix[:, t + 1, :] if t + 1 < NT else cnt[:], prefix[:, t, :], tots[:, t, :],
                                     ALU.add))
            link(V.tensor_tensor(rank[:], prefix[:], ps[:, 0, 0:NT * E].rearrange("p (t e) -> p t e", t=NT), ALU.add))
            link(V.tensor_scalar(ovc[:], cnt[:], float(CAP), None, ALU.is_gt))
            for j in range(2, -(-T // CAP)):
                link(V.scalar_tensor_tensor(out=ovc[:], in0=cnt[:], scalar=float(j * CAP), in1=ovc[:],
                                            op0=ALU.is_gt, op1=ALU.add))
            link(V.tensor_copy(ovi[:], ovc[:]))
            for d in (1, 2, 4, 8, 16):
                link(V.tensor_copy(ove[:], ovi[:]))
                link(V.tensor_tensor(ovi[:, d:], ove[:, d:], ove[:, 0:E - d], ALU.add))
            link(V.tensor_tensor(ove[:], ovi[:], ovc[:], ALU.subtract))
            chosen(rk, rank[:])
            chosen(vk, c3(ove[:], E))
            link(V.tensor_scalar(ck, rk, float(CAP), None, ALU.is_ge))
            for j in range(2, -(-T // CAP)):
                link(V.scalar_tensor_tensor(out=ck, in0=rk, scalar=float(j * CAP), in1=ck,
                                            op0=ALU.is_ge, op1=ALU.add))
            link(V.scalar_tensor_tensor(out=wk, in0=ck, scalar=-float(CAP), in1=rk, op0=ALU.mult, op1=ALU.add))
            link(V.tensor_tensor(bk, vk, ek, ALU.subtract))
            link(V.tensor_scalar(bk, bk, float(E - 1), None, ALU.add))
            link(V.scalar_tensor_tensor(out=bk, in0=ck, scalar=0.5, in1=bk, op0=ALU.is_ge, op1=ALU.mult))
            link(V.tensor_tensor(bk, bk, ck, ALU.add))
            link(V.tensor_tensor(bk, bk, ek, ALU.add))
            for k in range(2):
                ch = slice(k * NT, (k + 1) * NT)
                V.tensor_tensor(onerow[:, ch, :], rowi[:].unsqueeze(1).to_broadcast([P, NT, P]),
                                wk[:, k, :].unsqueeze(2).to_broadcast([P, NT, P]), ALU.is_equal
                                ).then_inc(s["onehot"], 1)
                link(V.tensor_tensor(oneblk[:, ch, 0:NBLK], blki[:].unsqueeze(1).to_broadcast([P, NT, NBLK]),
                                     bk[:, k, :].unsqueeze(2).to_broadcast([P, NT, NBLK]), ALU.is_equal))
                V.tensor_tensor(oneblk[:, ch, 0:NBLK], oneblk[:, ch, 0:NBLK].bitcast(F32), b3(tokid[:], NBLK),
                                ALU.mult).then_inc(s["onehot"], 1)
            link(V.scalar_tensor_tensor(out=xk, in0=wk, scalar=float(NBLK), in1=bk, op0=ALU.mult, op1=ALU.add))
            link(V.tensor_copy(dest[:], xk))
            dve.wait_ge(s["table_ps"], 1)
            V.tensor_copy(table[:], ps[:, 2, 0:NBLK]).then_inc(s["route_done"], 1)
            dve.wait_ge(s["picks"], 4)
            link(V.tensor_scalar(sm[:, 7, :], sm[:, 3, :], 1.0, None, ALU.add))
            link(V.tensor_tensor(sm[:, 7, :], sm[:, 7, :], sm[:, 6, :], ALU.mult))
            link(V.reciprocal(wts[:, 0, :], sm[:, 7, :]))
            link(V.tensor_tensor(wts[:, 1, :], wts[:, 0, :], sm[:, 3, :], ALU.mult))
            link(V.tensor_tensor(ocmp[:], ovi[:].unsqueeze(1).to_broadcast([P, OVF, E]),
                                 oidx[:].unsqueeze(2).to_broadcast([P, OVF, E]), ALU.is_le))
            link(V.tensor_reduce(ocmp2[:, 0:OVF], ocmp[:], AX.X, ALU.add))
            link(V.tensor_scalar(ocmp2[:, 0:OVF], ocmp2[:, 0:OVF], float(E - 1), None, ALU.min))
            link(V.tensor_copy(ocmp2[:, OVF:], ovi[:, E - 1:E]))
            V.tensor_copy(eids[:], ocmp2[:]).then_inc(s["routed"], 1)

            def weights_low(e, js):
                for j in js:
                    k = "gu" if j < 4 else "d"
                    dve.wait_ge(s[k + "_hi"], e * (4 if j < 4 else 2) + (j % 4 + 1))
                    split_rest(mlo[j][:], mraw[j][:], mhi[j][:], s[k + "_lo"])

            def rows_low(e, r):
                dve.wait_ge(s["xTh_ok"], e + 1)
                split_rest(xTl[:, r, :], bank(0, 2), xTh[:, r, :], s["xTl_ok"])

            def hidden(e):
                dve.wait_ge(s["gu_used"], e * 4 + 4)
                dve.wait_ge(s["silu_ok"], e + 1)
                wait(dve, s["h_tr"], e)
                V.tensor_tensor(hh[:], sg[:], bank(3), ALU.mult).then_inc(s["h_ok"], 1)

            def hidden_low(e):
                dve.wait_ge(s["hTh_ok"], e + 1)
                split_rest(hhTl[:], bank(4), hhTh[:], s["hTl_ok"])

            GU0, GU1, DN = (0, 1), (2, 3), (4, 5)

            def dve_step(e, r):
                rows_low(e + 1, 1 - r)
                hidden(e)
                weights_low(e + 1, GU0)
                hidden_low(e)
                weights_low(e + 1, GU1)
                weights_low(e, DN)

            rows_low(0, 0)
            dve_step(0, 0)
            dve_step(1, 1)
            with dve.Fori(1, E // 2 - 1) as i:
                dve_step(i * 2, 0)
                dve_step(i * 2 + 1, 1)
            dve_step(E - 2, 0)
            hidden(E - 1)
            hidden_low(E - 1)
            weights_low(E - 1, DN)
            for r in range(2):
                dve.wait_ge(s[f"y_out{r}"], 16 * (E // 2))
            dve.wait_ge(s["routed"], 1)
            n_ov = dve.value_load(eids[0:1, OVF:OVF + 1], min_val=0, max_val=OVF)
            with dve.If(n_ov > 0):
                with dve.Fori(0, OVF) as o:
                    with dve.If(o < n_ov):
                        dve.wait_ge(s["o_act"], o * 9 + 6)
                        for j in range(6):
                            split_rest(mlo[j][:], mraw[j][:], mhi[j][:], s["o_dve"])
                        dve.wait_ge(s["o_act"], o * 9 + 7)
                        split_rest(xTl[:, 0, :], bank(0, 2), xTh[:, 0, :], s["o_dve"])
                        dve.wait_ge(s["o_pe"], o * 4 + 3)
                        dve.wait_ge(s["o_act"], o * 9 + 8)
                        V.tensor_tensor(hh[:], sg[:], bank(3), ALU.mult).then_inc(s["o_dve"], 1)
                        dve.wait_ge(s["o_act"], o * 9 + 9)
                        split_rest(hhTl[:], bank(4), hhTh[:], s["o_dve"])
                        dve.wait_ge(s["o_dn"], o + 2)
                        V.tensor_copy(yy[:, 0, :], bank(5, 2)).then_inc(s["o_dve"], 1)

            dve.wait_ge(s["mods3"], 16 * 3)

            def combine(t):
                side = int(t == NPT)
                dve.wait_ge(s[f"ya_in{t % 4}"], 32 * (t // 4 + 1))
                dve.wait_ge(s["f_w"], t + 1)
                link(V.scalar_tensor_tensor(out=ya[:, t, :], in0=yb[:, t, :], scalar=wts[:, 1, t:t + 1],
                                            in1=ya[:, t, :], op0=ALU.mult, op1=ALU.add))
                link(V.tensor_tensor(ya[:, t, :], ya[:, t, :], gate2[:, side, :], ALU.mult))
                wait(dve, s["f_sq"], 2 * t)
                V.tensor_tensor(x1[:, t, :], x1[:, t, :], ya[:, t, :], ALU.add).then_inc(s["f_sq"], 1)

            combine(0)
            for t in range(NT):
                if t + 1 < NT:
                    combine(t + 1)
                dve.wait_ge(s["f_rt"], t + 1)
                V.reciprocal(sumsq[:, 3, t:t + 1], sumsq[:, 3, t:t + 1]).then_inc(s["f_ri"], 1)

        @block.tensor
        def _(pe):
            mm, tr = nc.tensor.matmul, nc.tensor.transpose
            pe.wait_ge(s["consts"], 1)
            pe.wait_ge(s["c_silu"], 1)
            n = SEQS + 1
            for k in range(KT):
                last = tr(ps[:, 6, k * n:(k + 1) * n], c_sb[:, k * P:(k + 1) * P], ident[0:n, 0:n])
            last.then_inc(s["cT_ps"], 1)
            pe.wait_ge(s["cT_sb"], 1)

            def modulation(u):
                pe.wait_ge(landed[u % 4], 48 * (u // 4 + 1))
                wait(pe, s["mod_sb"], u - 1)
                for k in range(KT):
                    last = mm(ps[0:n, 4 + u % 2, :], cT[:, k, :], aring[u % 4][:, k, :],
                              start=(k == 0), stop=(k == KT - 1))
                last.then_inc(s["unit_used"], 1)

            owners = []

            def group(owner, count):
                g = len(owners)
                if g >= 4:
                    pe.wait_ge(s[owners[g - 4][0]], owners[g - 4][1])
                owners.append((owner, count))
                return 4 + g % 4

            def product(out, xh, xl, wh, wl, start, stop):
                mm(out, xh, wh, start=start, stop=False)
                mm(out, xh, wl, start=False, stop=False)
                return mm(out, xl, wh, start=False, stop=stop)

            used = [0, 0]

            def release(u):
                pe.wait_ge(s["gemm"], used[1])
                if u + 1 > used[0]:
                    pe.sem_inc(s["unit_used"], u + 1 - used[0])
                    used[0] = u + 1

            def chunk_of(u, c, owner, count):
                sl, (c0, cn) = slot_of(u), TOKCH[c]
                if c == 0:
                    pe.wait_ge(s["w_lo"], turn(u))
                b = group(owner, count)
                for k in range(KT):
                    last = product(ps[:, b, 0:cn], ring_r[:, sl, 0, k, :], ring_r[:, sl, 1, k, :],
                                   hTh[:, k, c0:c0 + cn], hTl[:, k, c0:c0 + cn], k == 0, k == KT - 1)
                last.then_inc(s["gemm"], 1)

            def project(u0, owner, base_count, split=False):
                done = 0
                for m in range(4):
                    for c, (c0, cn) in enumerate(TOKCH):
                        done += len(parts(c0, cn)) if split else 1
                        if u0 > 0 or m > 0 or c == len(TOKCH) - 1:
                            chunk_of(u0 + m, c, owner, base_count + done)
                        if c0 == 0:
                            release(u0 + m - 1)
                    used[1] = len(owners)


            def spread_rows(u):
                if u == 0:
                    pe.wait_ge(s["consts"], 2)
                pe.wait_ge(s["mod_sb"], u + 1)
                wait(pe, s["bc_sb"], 2 * u)
                for side in range(2):
                    last = mm(ps[:, 6 + side, :], spread[:, side, :], modc[:, u % 3, :], start=True, stop=True)
                last.then_inc(s["bc_ps"], 1)

            for u in range(LEAD + 1):
                modulation(u)
                if 1 <= u <= 4:
                    spread_rows(u - 1)
            for t in range(NT):
                r = t % 2
                if 1 <= t < NADA - LEAD:
                    modulation(LEAD + t)
                if t >= NT - 2:
                    c = t - (NT - 2)
                    pe.wait_ge(s["mod_sb"], NADA)
                    pe.wait_ge(s["n1_lo"], (c + 1) * TC // P)
                    chunk_of(UQ, c, "gev_qk", c + 1)
                pe.wait_ge(s["n1_h"], t + 1)
                wait(pe, s["n1_lo"], t - 1)
                for k in range(KT):
                    last = tr(bank(2 * r, 2)[:, k * P:(k + 1) * P], ht[:, r, k * P:(k + 1) * P], ident[:])
                last.then_inc(s["n1_tr"], 1)
            pe.wait_ge(s["n1_lo"], NT)
            pe.wait_ge(s["mod_sb"], NADA)

            project(UQ, "gev_qk", 0)
            project(UK, "gev_qk", 12, True)
            pe.wait_ge(s["gev_qk"], 28)
            for i in range(5):
                b = group("gev_kout", i + 1)
                for m in range(HP):
                    src = kT[:, m, (4 + i) * P:(5 + i) * P] if i < 4 else kTs[:, m, :]
                    last = tr(ps[:, b, m * P:(m + 1) * P], src, ident[:])
                last.then_inc(s["gemm"], 1)
            pe.wait_ge(s["w_lo"], UV + 4)
            wv0 = slot_of(UV)
            for t in range(NT):
                b = group("gev_v", t + 1)
                for k in range(KT):
                    tile = slice(t * P, (t + 1) * P)
                    last = product(ps[:, b, :], hTh[:, k, tile], hTl[:, k, tile], ring_r[:, wv0:wv0 + 4, 0, k, :],
                                   ring_r[:, wv0:wv0 + 4, 1, k, :], k == 0, k == KT - 1)
                last.then_inc(s["gemm"], 1)
                if t == 0:
                    release(UV - 1)
            used[1] = len(owners)
            release(UV + 3)
            pe.wait_ge(s["gev_v"], NT)
            pe.wait_ge(s["gev_kout"], 5)

            NA = H * NPT

            def unit(a):
                pair, hh_ = a // 2, a % 2
                return pair // NPT, pair % NPT, hh_

            def scores(a):
                hp, i, h_ = unit(a)
                q = qz[:, (a // 2) % 2, h_, :]
                j0 = 4 - min(i, 4)
                pe.wait_ge(s["qz_ok"], 2 * (a // 2) + 2)
                wait(pe, s["s_sb"], a - 1)
                k0 = (i - 4 + j0) * P
                if j0 < 4:
                    mm(bank(2 * (a % 2))[:, j0 * P:512], q, kT[:, hp, k0:i * P], start=True, stop=True)
                mm(bank(2 * (a % 2) + 1)[:, 0:P], q, kT[:, hp, i * P:(i + 1) * P], start=True, stop=True
                   ).then_inc(s["s_scores"], 1)

            def prob_t(a):
                _, i, _ = unit(a)
                pe.wait_ge(s["s_p"], a + 1)
                wait(pe, s["s_ptc"], a)
                for j in range(4 - min(i, 4), 5):
                    last = tr(bank(4, 2)[:, j * P:(j + 1) * P], Pr[:, a % 2, j * P:(j + 1) * P], ident[:])
                last.then_inc(s["s_pt"], 1)

            def values(a):
                hp, i, h_ = unit(a)
                pe.wait_ge(s["s_ptc"], a + 1)
                if h_ == 0:
                    wait(pe, s["s_at"], a // 2)
                j0 = 4 - min(i, 4)
                for j in range(j0, 5):
                    last = mm(ps[:, 6, HD * h_:HD * h_ + HD], PT[:, a % 2, j, :],
                              v[:, i - 4 + j, (2 * hp + h_) * HD:(2 * hp + h_ + 1) * HD],
                              start=(j == j0), stop=(j == 4))
                last.then_inc(s["s_pv"], 1)

            def att_t(pair):
                pe.wait_ge(s["s_at"], pair + 1)
                wait(pe, s["s_attc"], pair)
                tr(ps[:, 7, 0:P], attt[:, pair % 2, :], ident[:]).then_inc(s["s_att"], 1)

            scores(0)
            scores(1)
            for a in range(NA):
                if a + 2 < NA:
                    scores(a + 2)
                prob_t(a)
                if a >= 1:
                    values(a - 1)
                if a % 2 == 1 and a >= 3:
                    att_t(a // 2 - 1)
            values(NA - 1)
            att_t(NA // 2 - 1)
            pe.wait_ge(s["s_attc"], HP * NPT)

            def old_keys_t(q):
                r = q % 2
                pe.wait_ge(s[f"k_in{r}"], 16 * (q // 2 + 1))
                wait(pe, s["k_trc"], 2 * q)
                for m in range(HP):
                    for c in range(4):
                        last = tr(ps[:, m, c * P:(c + 1) * P], kc[:, r, c, m * P:(m + 1) * P], ident[:])
                last.then_inc(s["k_tr"], 1)

            def sample_scores(q):
                pe.wait_ge(s["k_trc"], 2 * q + 2)
                pe.wait_ge(s["qb"], 2 * q + 2)
                wait(pe, s["ks_sb"], q)
                qb = qblk[:, q % 2, 0:512].rearrange("p (m c) -> p m c", m=HP)
                for m in range(HP):
                    mm(ps[:, 4, :], qb[:, m, :], kcT[:, m, :], start=(m == 0), stop=(m == HP - 1))
                for m in range(HP):
                    last = mm(ps[:, 5, 0:DEC], qb[:, m, :], kTs[:, m, q * DEC:(q + 1) * DEC],
                              start=(m == 0), stop=(m == HP - 1))
                last.then_inc(s["ks_sc"], 1)

            old_keys_t(0)
            sample_scores(0)
            for q in range(SEQS):
                r = q % 2
                if q + 1 < SEQS:
                    old_keys_t(q + 1)
                pe.wait_ge(s["ks_p"], q + 1)
                wait(pe, s["ks_ptc"], 2 * q)
                wait(pe, s["ks_at"], H * q)
                for c in range(4):
                    tr(ps[:, 6, c * P:(c + 1) * P], Ps[:, c * P:(c + 1) * P], ident[:])
                tr(ps[0:DEC, 5, P:2 * P], Ps[:, PAST:NK], ident[:]).then_inc(s["ks_pt"], 1)
                pe.wait_ge(s["ks_ptc"], 2 * q + 2)
                wait(pe, s["ks_ev"], q)
                pe.wait_ge(s[f"v_in{r}"], 32 * (q // 2 + 1))
                for c in range(4):
                    mm(ps[:, 7, :], PTs[:, c, :], vc[:, r, c, :], start=(c == 0), stop=False)
                mm(ps[:, 7, :], PTs[0:DEC, 4, :], v16[:, r, :], start=False, stop=True).then_inc(s["ks_pv"], 1)
                if q + 1 < SEQS:
                    sample_scores(q + 1)
                pe.wait_ge(s["ks_ev"], q + 1)
                for m in range(HP):
                    last = tr(ps[:, 6, m * P:(m + 1) * P], atts[:, m * P:(m + 1) * P], ident[:])
                last.then_inc(s["ks_att"], 1)
            pe.wait_ge(s["ks_at"], H * SEQS)

            project(UCC, "gev_conv", 0, True)
            project(UCV, "cu_done", 0, True)
            pe.wait_ge(s["prev_in"], 16)
            b = group("gev_prev", 1)
            for m in range(HP):
                last = tr(ps[:, b, m * 16:(m + 1) * 16], st_in[:, m * P:(m + 1) * P], ident[0:16, 0:16])
            last.then_inc(s["gemm"], 1)
            pe.wait_ge(s["conv_last"], 1)
            b = group("newc_sb", 1)
            for m in range(HP):
                last = tr(ps[0:18, b, m * P:(m + 1) * P], lastu[:, m, :], ident[:])
            last.then_inc(s["gemm"], 1)
            project(UCB, "cu_done", 16)

            for i in range(24):
                f, (c0, cn) = i // 3, TOKCH[i % 3]
                if i == 1:
                    pe.wait_ge(s["cu_done"], 28)
                ua, ub, up = [slot_of(UGATE + 3 * f + j) for j in range(3)]
                wait(pe, s["g_done"], i - 1)
                b = 4 * (i % 2)
                for kind, (sl, un, k0, kn, xh, xl, br) in enumerate((
                        (ua, 0, 0, KT, hTh, hTl, 0), (up, 2, 0, 4, atth, attl, 1),
                        (ub, 1, 0, KT, hTh, hTl, 0), (up, 2, 4, 4, Yh, Yl, HP + 1))):
                    if i % 3 == 0:
                        pe.wait_ge(s["w_lo"], UGATE + 3 * f + un + 1)
                        wait(pe, s["b_lo"], br)
                    for k in range(kn):
                        last = product(ps[:, b + kind, 0:cn], ring_r[:, sl, 0, k0 + k, :],
                                       ring_r[:, sl, 1, k0 + k, :], xh[:, k, c0:c0 + cn], xl[:, k, c0:c0 + cn],
                                       k == 0, k == kn - 1)
                    last.then_inc(s["g_ready"], 1)
                    if i == 0 and kind == 0:
                        release(UCB + 3)
                    if i == 23 and kind in (1, 3):
                        pe.wait_ge(s["g_ready"], 4 * i + kind)
                        pe.sem_inc(s["unit_used"], 1)
                    if i % 3 == 0 and f > 0 and kind == 0:
                        pe.wait_ge(s["g_ready"], 4 * i)
                        pe.sem_inc(s["unit_used"], 3)
            pe.wait_ge(s["g_ready"], 4 * 24)
            pe.sem_inc(s["unit_used"], 1)
            pe.wait_ge(s["g_done"], 23)

            def out_project(t):
                pe.wait_ge(s["w_lo"], NU + t + 1 if t else turn(UO + 3))
                wait(pe, s["x1_done"], t - 1)
                for h in range(2):
                    if t == 0 and h == 1:
                        pe.wait_ge(s["w_lo"], turn(NU - 1))
                    for k in range(KT):
                        high, _, low = mix_parts(t)
                        last = product(ps[:, 2 * (t % 2) + h, :], high[:, k, :], low[:, k, :],
                                       ring_r[:, 4 * h:4 * h + 4, 0, k, :], ring_r[:, 4 * h:4 * h + 4, 1, k, :],
                                       k == 0, k == KT - 1)
                last.then_inc(s["o_done"], 1)

            def router(t):
                pe.wait_ge(s["n2_evac"], t + 1)
                wait(pe, s["n2_lt"], t)
                for k in range(KT):
                    last = mm(ps[0:NLOG, 7, 0:P], wr[:, k, :], h2T[:, t % 2, k * P:(k + 1) * P],
                              start=(k == 0), stop=(k == KT - 1))
                last.then_inc(s["n2_log"], 1)

            def router_t(t):
                pe.wait_ge(s["n2_lt"], t + 1)
                wait(pe, s["n2_lev"], t)
                tr(ps[:, 6, 0:NLOG], logT[:], ident[0:NLOG, 0:NLOG]).then_inc(s["n2_ltr"], 1)

            pe.wait_ge(s["wr_in"], 64)
            out_project(0)
            for t in range(NT):
                if t + 1 < NT:
                    out_project(t + 1)
                if t == 0:
                    pe.wait_ge(s["g_done"], 24)
                pe.wait_ge(s["n2_h"], t + 1)
                wait(pe, s["n2_evac"], t)
                for k in range(KT):
                    last = tr(bank(4, 2)[:, k * P:(k + 1) * P], h2[:, t % 2, k * P:(k + 1) * P], ident[:])
                last.then_inc(s["n2_tr"], 1)
                if t >= 1:
                    router(t - 1)
                if t >= 2:
                    router_t(t - 2)
                if t + 2 == NT:
                    pe.wait_ge(s["o_done"], NT)
                    pe.sem_inc(s["unit_used"], KT)
            router(NT - 1)
            router_t(NT - 2)
            router_t(NT - 1)

            pe.wait_ge(s["consts"], 3)
            pe.wait_ge(s["ranks"], 1)
            pv = picked[:].rearrange("p t e -> p (t e)")
            mm(ps[:, 0, 0:NT * E], before[:], pv, start=True, stop=True)
            mm(ps[:, 1, 0:NT * E], ones[:], pv, start=True, stop=True).then_inc(s["ranks"], 1)
            for j in range(2 * NT):
                if j % NT == 0:
                    pe.wait_ge(s["onehot"], 2 * (j // NT) + 2)
                last = mm(ps[:, 2, 0:NBP], onerow[:, j, :], oneblk[:, j, :], start=(j == 0), stop=(j == 2 * NT - 1))
            last.then_inc(s["table_ps"], 1)
            pe.wait_ge(s["route_done"], 1)

            def rows_t(e, r, count):
                wait(pe, s["xTl_ok"], e)
                pe.wait_ge(s[f"xg_in{r}"], count)
                for k in range(KT):
                    last = tr(bank(0, 2)[:, k * P:(k + 1) * P], xg[:, r, k * P:(k + 1) * P], ident[:])
                last.then_inc(s["xg_tr"], 1)

            def gate_up_half(j, r, sig):
                for k in range(4):
                    c = slice(((j % 2) * 4 + k) * P, ((j % 2) * 4 + k + 1) * P)
                    n = slice(k * 512, (k + 1) * 512)
                    last = product(bank(2 + j // 2), xTh[:, r, c], xTl[:, r, c], mhi[j][:, n], mlo[j][:, n],
                                   j % 2 == 0 and k == 0, j % 2 == 1 and k == 3)
                if sig is not None:
                    last.then_inc(sig, 1)

            def gate_up(e, r):
                pe.wait_ge(s["xTl_ok"], e + 1)
                for j in range(4):
                    if j == 0:
                        wait(pe, s["silu_ok"], e)
                    if j == 2:
                        wait(pe, s["h_ok"], e)
                    pe.wait_ge(s["gu_lo"], e * 4 + (j + 1))
                    gate_up_half(j, r, s["gu_used"])

            def down_half(j, sig):
                for k in range(2):
                    c = slice(((j - 4) * 2 + k) * P, ((j - 4) * 2 + k + 1) * P)
                    for h in range(2):
                        n = slice(k * D + h * 512, k * D + (h + 1) * 512)
                        last = product(bank(5 + h), hhTh[:, c], hhTl[:, c], mhi[j][:, n], mlo[j][:, n],
                                       j == 4 and k == 0, j == 5 and k == 1)
                if sig is not None:
                    last.then_inc(sig, 1)

            def down(e):
                pe.wait_ge(s["hTl_ok"], e + 1)
                wait(pe, s["y_ok"], e)
                for j in (4, 5):
                    pe.wait_ge(s["d_lo"], e * 2 + (j - 3))
                    down_half(j, s["d_used"])

            def hidden_mms(sig):
                for k in range(4):
                    last = tr(bank(4)[:, k * P:(k + 1) * P], hh[:, k * P:(k + 1) * P], ident[:])
                last.then_inc(s[sig], 1)

            def hidden_t(e):
                pe.wait_ge(s["h_ok"], e + 1)
                wait(pe, s["hTl_ok"], e)
                hidden_mms("h_tr")

            rows_t(0, 0, 16)
            gate_up(0, 0)
            rows_t(1, 1, 16)
            hidden_t(0)
            gate_up(1, 1)
            rows_t(2, 0, 32)
            down(0)
            hidden_t(1)
            with pe.Fori(1, E // 2 - 1) as i:
                gate_up(i * 2, 0)
                rows_t(i * 2 + 1, 1, (i + 1) * 16)
                down(i * 2 - 1)
                hidden_t(i * 2)
                gate_up(i * 2 + 1, 1)
                rows_t(i * 2 + 2, 0, (i + 2) * 16)
                down(i * 2)
                hidden_t(i * 2 + 1)
            gate_up(E - 2, 0)
            rows_t(E - 1, 1, 16 * (E // 2))
            down(E - 3)
            hidden_t(E - 2)
            gate_up(E - 1, 1)
            down(E - 2)
            hidden_t(E - 1)
            down(E - 1)

            pe.wait_ge(s["routed"], 1)
            pe.wait_ge(s["y_ok"], E)
            n_ov = pe.value_load(eids[0:1, OVF:OVF + 1], min_val=0, max_val=OVF)
            pe.sem_inc(s["o_dn"], 1)
            with pe.If(n_ov > 0):
                with pe.Fori(0, OVF) as o:
                    with pe.If(o < n_ov):
                        pe.wait_ge(s["o_xg"], (o + 1) * 16)
                        for k in range(KT):
                            last = tr(bank(0, 2)[:, k * P:(k + 1) * P], xg[:, 0, k * P:(k + 1) * P], ident[:])
                        last.then_inc(s["o_pe"], 1)
                        pe.wait_ge(s["o_dve"], o * 10 + 7)
                        for j in range(4):
                            gate_up_half(j, 0, s["o_pe"] if j % 2 == 1 else None)
                        pe.wait_ge(s["o_dve"], o * 10 + 8)
                        hidden_mms("o_pe")
                        pe.wait_ge(s["o_dve"], o * 10 + 9)
                        down_half(4, None)
                        down_half(5, s["o_dn"])


_INS = ['x_prompt', 'x_sample', 'cache_attn_k', 'cache_attn_v', 'state_conv', 'c_prompt', 'c_sample',
        'w_ada', 'b_ada', 'norm1_g', 'norm2_g', 'w_in', 'rel_bias', 'conv_w', 'conv_b', 'w_pa', 'w_pb', 'w_o',
        'w_group', 'b_group', 'w_expert', 'b_expert', 'w_e_gate', 'w_e_up', 'w_e_down', 'final_g']
_OUTS = [(1, NP_TOK, D), (SEQS, DEC, D), (1, 1, 512, H, HD), (1, 1, 512, H, HD), (1, 1, 2, DA),
         (1, SEQS, DEC, H, HD), (1, SEQS, DEC, H, HD), (1, SEQS, 2, DA)]


def kernel(**inputs):
    import numpy as _np
    import concourse.bacc as _bacc
    from concourse import mybir as _mybir
    from concourse.bass_utils import run_bass_kernel_spmd as _run

    nc = _bacc.Bacc("TRN2", target_bir_lowering=False, num_devices=1)
    arrays, args = {}, []
    for name in _INS:
        a = _np.ascontiguousarray(inputs[name])
        arrays[f"in_{name}_dram"] = a
        args.append(nc.dram_tensor(f"in_{name}_dram", a.shape, _mybir.dt.from_np(a.dtype), kind="ExternalInput").ap())
    for i, shape in enumerate(_OUTS):
        args.append(nc.dram_tensor(f"out_{i}_dram", shape, _mybir.dt.float32, kind="ExternalOutput").ap())
    build(nc, *args)
    r = _run(nc, [arrays], core_ids=[0])
    return tuple(r.results[0][f"out_{i}_dram"] for i in range(len(_OUTS)))
```
